# Optimizing a Trainium2 kernel written in Bass

```python
import math
import jax, jax.numpy as jnp
from jax import lax
import numpy as np

D_MODEL = 1024
BATCH = 1
SEQ = 256
DEPTH = 2

N_MEM = 256
EPS = 1e-6
MOBA_HEADS = 8
MOBA_HEAD_DIM = 64
MOBA_BLOCK = 256
MOBA_TOPK = 3
MOBA_Q_CHUNK = 64
A_WIDTH = MOBA_HEADS * MOBA_HEAD_DIM
POOL_WINDOWS = (2, 4, 8, 16)
POOL_GROUP = 128
POOL_WIDTH = POOL_GROUP * len(POOL_WINDOWS)
EV_IN = 3 * A_WIDTH + POOL_WIDTH
EV_MIX = A_WIDTH + POOL_WIDTH
SGU_GROUPS = 4
SGU_GROUP = 128
SGU_CHUNK = 128
SGU_WIDTH = SGU_GROUPS * SGU_GROUP
DN_HEADS = 4
DN_HEAD_DIM = 128
DN_WIDTH = DN_HEADS * DN_HEAD_DIM
DN_CONV = 4
DN_CHUNK = 64
OD_SPLITS = [2 * SGU_WIDTH, 2 * SGU_WIDTH + 3 * DN_WIDTH,
             2 * SGU_WIDTH + 4 * DN_WIDTH, 2 * SGU_WIDTH + 4 * DN_WIDTH + DN_HEADS]
OD_IN = 2 * SGU_WIDTH + 4 * DN_WIDTH + 2 * DN_HEADS
OD_MIX = SGU_WIDTH + DN_WIDTH
XATTN_HEADS = 4
XATTN_HEAD_DIM = D_MODEL // XATTN_HEADS
D_FF = 256 * ((8 * D_MODEL // 3 + 255) // 256)
FFN_CONV = 3
N_EVEN = (DEPTH + 1) // 2
N_ODD = DEPTH // 2


def rmsnorm(x, g):
    xf = x.astype(jnp.float32)
    y = xf * lax.rsqrt(jnp.mean(xf * xf, axis=-1, keepdims=True) + EPS)
    return (y * g.astype(jnp.float32)).astype(x.dtype)

def causal_dwconv(x, w):
    K = w.shape[0]
    S = x.shape[1]
    xp = jnp.pad(x, ((0, 0), (K - 1, 0), (0, 0)))
    y = xp[:, 0:S] * w[0]
    for j in range(1, K):
        y = y + xp[:, j:j + S] * w[j]
    return y

def split_heads(t, n_heads, head_dim):
    B, S, _ = t.shape
    return t.reshape(B, S, n_heads, head_dim).transpose(0, 2, 1, 3)

def moba_attention(q, k, v):
    B, H, S, Dh = q.shape
    BS, QC = MOBA_BLOCK, MOBA_Q_CHUNK
    nb = -(-S // BS)
    pad = nb * BS - S
    k_blk = jnp.pad(k, ((0, 0), (0, 0), (0, pad), (0, 0))).reshape(B, H, nb, BS, Dh)
    v_blk = jnp.pad(v, ((0, 0), (0, 0), (0, pad), (0, 0))).reshape(B, H, nb, BS, Dh)
    k_mean = jnp.mean(k_blk.astype(jnp.float32), axis=3)
    q_blk_id = jnp.arange(S) // BS
    gate = jnp.einsum('bhsd,bhnd->bhsn', q.astype(jnp.float32), k_mean)
    fully_past = jnp.arange(nb)[None, :] < q_blk_id[:, None]
    gate = jnp.where(fully_past, gate, -jnp.inf)
    n_sel = min(MOBA_TOPK, nb)
    _, sel = lax.top_k(gate, n_sel)
    sel_valid = sel < q_blk_id[:, None]
    scale = Dh ** -0.5
    gather = jax.vmap(jax.vmap(lambda blk, ix: blk[ix]))

    def chunk(c):
        t0 = c * QC
        qc = lax.dynamic_slice_in_dim(q, t0, QC, axis=2)
        sc = lax.dynamic_slice_in_dim(sel, t0, QC, axis=2)
        vc = lax.dynamic_slice_in_dim(sel_valid, t0, QC, axis=2)
        own = t0 // BS
        k_own = lax.dynamic_index_in_dim(k_blk, own, axis=2, keepdims=False)
        v_own = lax.dynamic_index_in_dim(v_blk, own, axis=2, keepdims=False)
        k_sel = gather(k_blk, sc)
        v_sel = gather(v_blk, sc)
        s_sel = jnp.einsum('bhqd,bhqnkd->bhqnk', qc, k_sel).astype(jnp.float32) * scale
        s_sel = jnp.where(vc[..., None], s_sel, -jnp.inf).reshape(B, H, QC, n_sel * BS)
        tq = t0 + jnp.arange(QC)
        tk = own * BS + jnp.arange(BS)
        s_own = jnp.einsum('bhqd,bhkd->bhqk', qc, k_own).astype(jnp.float32) * scale
        s_own = jnp.where(tk[None, :] <= tq[:, None], s_own, -jnp.inf)
        p = jax.nn.softmax(jnp.concatenate([s_sel, s_own], axis=-1), axis=-1).astype(v.dtype)
        p_sel = p[..., :n_sel * BS].reshape(B, H, QC, n_sel, BS)
        p_own = p[..., n_sel * BS:]
        return (jnp.einsum('bhqnk,bhqnkd->bhqd', p_sel, v_sel)
                + jnp.einsum('bhqk,bhkd->bhqd', p_own, v_own))

    out = lax.map(chunk, jnp.arange(S // QC))
    return out.transpose(1, 2, 0, 3, 4).reshape(B, H, S, Dh)

def multiscale_pool(p, pool_w, pool_scale):
    B, S, _ = p.shape
    G = len(POOL_WINDOWS)
    pf = p.astype(jnp.float32).reshape(B, S, G, POOL_GROUP)
    cs = jnp.cumsum(pf, axis=1)
    t1 = jnp.arange(1, S + 1, dtype=jnp.float32)
    outs = []
    for g, w in enumerate(POOL_WINDOWS):
        c = cs[:, :, g]
        c_prev = jnp.pad(c, ((0, 0), (w, 0), (0, 0)))[:, :S]
        cnt = jnp.minimum(t1, float(w))[None, :, None]
        outs.append((c - c_prev) / cnt - pf[:, :, g])
    pooled = jnp.stack(outs, axis=2).astype(p.dtype)
    y = jnp.einsum('bsgc,gcd->bsgd', pooled, pool_w).reshape(B, S, POOL_WIDTH)
    return y * pool_scale

def spatial_gating(z, ln_g, ln_b, w_s, b_s):
    B, S, _ = z.shape
    u, v = jnp.split(z, 2, axis=-1)
    vf = v.astype(jnp.float32)
    mu = jnp.mean(vf, axis=-1, keepdims=True)
    var = jnp.mean(jnp.square(vf - mu), axis=-1, keepdims=True)
    vn = ((vf - mu) * lax.rsqrt(var + EPS) * ln_g + ln_b).astype(z.dtype)
    vn = vn.reshape(B, S // SGU_CHUNK, SGU_CHUNK, SGU_GROUPS, SGU_GROUP)
    causal = jnp.tril(jnp.ones((SGU_CHUNK, SGU_CHUNK), dtype=bool))
    w = jnp.where(causal[None], w_s, 0)
    s = jnp.einsum('gts,bnsgc->bntgc', w, vn) + b_s.T[None, None, :, :, None]
    return u * s.reshape(B, S, SGU_WIDTH)

def l2norm(t):
    return t * lax.rsqrt(jnp.sum(t * t, axis=-1, keepdims=True) + EPS)

def chunked_gated_delta_rule(q, k, v, g, beta):
    B, H, S, DK = q.shape
    DV = v.shape[-1]
    C = DN_CHUNK
    N = S // C
    q = q.reshape(B, H, N, C, DK)
    k = k.reshape(B, H, N, C, DK)
    v = v.reshape(B, H, N, C, DV)
    beta = beta.reshape(B, H, N, C)
    gc = jnp.cumsum(g.reshape(B, H, N, C), axis=-1)
    idx = jnp.arange(C)
    causal = idx[:, None] >= idx[None, :]
    strict = idx[:, None] > idx[None, :]
    decay = jnp.exp(jnp.where(causal, gc[..., :, None] - gc[..., None, :], -jnp.inf))
    kb = k * beta[..., None]
    a = jnp.where(strict, jnp.einsum('bhnid,bhnjd->bhnij', kb, k) * decay, 0.0)
    m = a + jnp.eye(C, dtype=a.dtype)
    rhs = jnp.concatenate([v * beta[..., None], kb * jnp.exp(gc)[..., None]], axis=-1)
    sol = lax.linalg.triangular_solve(m, rhs, left_side=True, lower=True, unit_diagonal=True)
    u, w = sol[..., :DV], sol[..., DV:]
    qk = jnp.einsum('bhnid,bhnjd->bhnij', q, k) * decay
    q_dec = q * jnp.exp(gc)[..., None]
    k_dec = k * jnp.exp(gc[..., -1:] - gc)[..., None]
    g_last = jnp.exp(gc[..., -1])

    def step(state, inp):
        qk_n, qd_n, kd_n, u_n, w_n, gl_n = inp
        v_new = u_n - jnp.einsum('bhck,bhkv->bhcv', w_n, state)
        o = (jnp.einsum('bhck,bhkv->bhcv', qd_n, state)
             + jnp.einsum('bhij,bhjv->bhiv', qk_n, v_new))
        state = state * gl_n[..., None, None] + jnp.einsum('bhck,bhcv->bhkv', kd_n, v_new)
        return state, o

    xs = (jnp.moveaxis(qk, 2, 0), jnp.moveaxis(q_dec, 2, 0), jnp.moveaxis(k_dec, 2, 0),
          jnp.moveaxis(u, 2, 0), jnp.moveaxis(w, 2, 0), jnp.moveaxis(g_last, 2, 0))
    state0 = jnp.zeros((B, H, DK, DV), q.dtype)
    _, o = lax.scan(step, state0, xs)
    return jnp.moveaxis(o, 0, 2).reshape(B, H, S, DV)

def gated_deltanet(qkv, gate, b_raw, a_raw, conv_w, a_log, dt_bias, norm_g):
    B, S, _ = qkv.shape
    dt = qkv.dtype
    qkv = jax.nn.silu(causal_dwconv(qkv, conv_w))
    q, k, v = jnp.split(qkv, 3, axis=-1)
    q = l2norm(split_heads(q, DN_HEADS, DN_HEAD_DIM).astype(jnp.float32)) * DN_HEAD_DIM ** -0.5
    k = l2norm(split_heads(k, DN_HEADS, DN_HEAD_DIM).astype(jnp.float32))
    v = split_heads(v, DN_HEADS, DN_HEAD_DIM).astype(jnp.float32)
    beta = jax.nn.sigmoid(b_raw.astype(jnp.float32)).transpose(0, 2, 1)
    g = (-jnp.exp(a_log.astype(jnp.float32))
         * jax.nn.softplus(a_raw.astype(jnp.float32) + dt_bias.astype(jnp.float32))).transpose(0, 2, 1)
    o = chunked_gated_delta_rule(q, k, v, g, beta)
    o = o * lax.rsqrt(jnp.mean(o * o, axis=-1, keepdims=True) + EPS) * norm_g.astype(jnp.float32)
    o = o.transpose(0, 2, 1, 3) * jax.nn.silu(gate.astype(jnp.float32).reshape(B, S, DN_HEADS, DN_HEAD_DIM))
    return o.reshape(B, S, DN_WIDTH).astype(dt)

def memory_cross_attention(xn, mem_n, wq, wkv, wo):
    B, S, D = xn.shape
    M = mem_n.shape[1]
    q = (xn @ wq).reshape(B, S, XATTN_HEADS, XATTN_HEAD_DIM)
    k, v = jnp.split(mem_n @ wkv, 2, axis=-1)
    k = k.reshape(B, M, XATTN_HEADS, XATTN_HEAD_DIM)
    v = v.reshape(B, M, XATTN_HEADS, XATTN_HEAD_DIM)
    s = jnp.einsum('bshd,bmhd->bhsm', q, k).astype(jnp.float32) * XATTN_HEAD_DIM ** -0.5
    p = jax.nn.softmax(s, axis=-1).astype(v.dtype)
    o = jnp.einsum('bhsm,bmhd->bshd', p, v).reshape(B, S, D)
    return o @ wo

def conv_ffn(xn, w_up, conv_w, w_down):
    h = causal_dwconv(xn @ w_up, conv_w)
    g, u = jnp.split(h, 2, axis=-1)
    return (jax.nn.silu(g) * u) @ w_down

def first_inputs(seed: int = 0) -> dict:
    key = jax.random.key(seed)
    ks = iter(jax.random.split(key, 32))
    D = D_MODEL

    def nrm(shape, scale):
        return jax.random.normal(next(ks), shape, jnp.float32) * scale

    def gain(shape):
        return 1.0 + nrm(shape, 0.02)

    x = nrm((BATCH, SEQ, D), 1.0)
    mem = nrm((BATCH, N_MEM, D), 1.0)
    mem_norm = gain((D,))
    norm_mix = gain((DEPTH, D))
    norm_xattn = gain((DEPTH, D))
    norm_ffn = gain((DEPTH, D))
    ev_w_in = nrm((N_EVEN, D, EV_IN), D ** -0.5)
    pool_w = nrm((N_EVEN, len(POOL_WINDOWS), POOL_GROUP, POOL_GROUP), POOL_GROUP ** -0.5)
    pool_scale = 1.0 + nrm((N_EVEN, POOL_WIDTH), 0.1)
    ev_w_out = nrm((N_EVEN, EV_MIX, D), EV_MIX ** -0.5)
    od_w_in = nrm((N_ODD, D, OD_IN), D ** -0.5)
    sgu_ln_g = gain((N_ODD, SGU_WIDTH))
    sgu_ln_b = nrm((N_ODD, SGU_WIDTH), 0.02)
    sgu_w = nrm((N_ODD, SGU_GROUPS, SGU_CHUNK, SGU_CHUNK), SGU_CHUNK ** -0.5)
    sgu_b = 1.0 + nrm((N_ODD, SGU_GROUPS, SGU_CHUNK), 0.02)
    dn_conv = nrm((N_ODD, DN_CONV, 3 * DN_WIDTH), DN_CONV ** -0.5)
    dn_a_log = jnp.log(jax.random.uniform(next(ks), (N_ODD, DN_HEADS), jnp.float32, 1.0, 16.0))
    dt = jnp.exp(jax.random.uniform(next(ks), (N_ODD, DN_HEADS), jnp.float32,
                                    math.log(1e-3), math.log(1e-1)))
    dn_dt_bias = dt + jnp.log(-jnp.expm1(-dt))
    dn_norm_g = gain((N_ODD, DN_HEAD_DIM))
    od_w_out = nrm((N_ODD, OD_MIX, D), OD_MIX ** -0.5)
    xattn_wq = nrm((DEPTH, D, D), D ** -0.5)
    xattn_wkv = nrm((DEPTH, D, 2 * D), D ** -0.5)
    xattn_wo = nrm((DEPTH, D, D), D ** -0.5)
    ffn_w_up = nrm((DEPTH, D, 2 * D_FF), D ** -0.5)
    ffn_conv = nrm((DEPTH, FFN_CONV, 2 * D_FF), FFN_CONV ** -0.5)
    ffn_w_down = nrm((DEPTH, D_FF, D), D_FF ** -0.5)
    final_norm = gain((D,))
    return {'x': x, 'mem': mem, 'mem_norm': mem_norm, 'norm_mix': norm_mix,
            'norm_xattn': norm_xattn, 'norm_ffn': norm_ffn,
            'ev_w_in': ev_w_in, 'pool_w': pool_w, 'pool_scale': pool_scale, 'ev_w_out': ev_w_out,
            'od_w_in': od_w_in, 'sgu_ln_g': sgu_ln_g, 'sgu_ln_b': sgu_ln_b, 'sgu_w': sgu_w,
            'sgu_b': sgu_b, 'dn_conv': dn_conv, 'dn_a_log': dn_a_log, 'dn_dt_bias': dn_dt_bias,
            'dn_norm_g': dn_norm_g, 'od_w_out': od_w_out,
            'xattn_wq': xattn_wq, 'xattn_wkv': xattn_wkv, 'xattn_wo': xattn_wo,
            'ffn_w_up': ffn_w_up, 'ffn_conv': ffn_conv, 'ffn_w_down': ffn_w_down,
            'final_norm': final_norm}

def first_block(x, mem, mem_norm, norm_mix, norm_xattn, norm_ffn,
              ev_w_in, pool_w, pool_scale, ev_w_out,
              od_w_in, sgu_ln_g, sgu_ln_b, sgu_w, sgu_b,
              dn_conv, dn_a_log, dn_dt_bias, dn_norm_g, od_w_out,
              xattn_wq, xattn_wkv, xattn_wo,
              ffn_w_up, ffn_conv, ffn_w_down, final_norm):
    B, S, _ = x.shape
    mem_n = rmsnorm(mem, mem_norm)
    h = x
    for layer in range(DEPTH):
        xn = rmsnorm(h, norm_mix[layer])
        i = layer // 2
        if layer % 2 == 0:
            proj = xn @ ev_w_in[i]
            q, k, v, p = jnp.split(proj, [A_WIDTH, 2 * A_WIDTH, 3 * A_WIDTH], axis=-1)
            a_out = moba_attention(split_heads(q, MOBA_HEADS, MOBA_HEAD_DIM),
                                   split_heads(k, MOBA_HEADS, MOBA_HEAD_DIM),
                                   split_heads(v, MOBA_HEADS, MOBA_HEAD_DIM))
            a_out = a_out.transpose(0, 2, 1, 3).reshape(B, S, A_WIDTH)
            b_out = multiscale_pool(p, pool_w[i], pool_scale[i])
            mix = jnp.concatenate([a_out, b_out], axis=-1) @ ev_w_out[i]
        else:
            proj = xn @ od_w_in[i]
            z, qkv, gate, b_raw, a_raw = jnp.split(proj, OD_SPLITS, axis=-1)
            c_out = spatial_gating(jax.nn.gelu(z), sgu_ln_g[i], sgu_ln_b[i], sgu_w[i], sgu_b[i])
            d_out = gated_deltanet(qkv, gate, b_raw, a_raw, dn_conv[i], dn_a_log[i],
                                   dn_dt_bias[i], dn_norm_g[i])
            mix = jnp.concatenate([c_out, d_out], axis=-1) @ od_w_out[i]
        h = h + mix
        h = h + memory_cross_attention(rmsnorm(h, norm_xattn[layer]), mem_n,
                                       xattn_wq[layer], xattn_wkv[layer], xattn_wo[layer])
        h = h + conv_ffn(rmsnorm(h, norm_ffn[layer]), ffn_w_up[layer], ffn_conv[layer], ffn_w_down[layer])
    return rmsnorm(h, final_norm)


DEPTH_2 = 4

GRID_W = 64
CTX_LEN = 256
N_MIXERS = 3
D_FF_2 = 4 * D_MODEL

GLA_HEADS = 4
GLA_KEY_DIM = D_MODEL // 2
GLA_VAL_DIM = D_MODEL
GLA_DK = GLA_KEY_DIM // GLA_HEADS
GLA_DV = GLA_VAL_DIM // GLA_HEADS
GLA_RANK = 16
GLA_TAU = 16.0
GLA_CHUNK = 64

CONV_WIDTH = 31
CONV_PAD = CONV_WIDTH // 2

ATTN_HEAD_DIM = 64
ATTN_Q_HEADS = D_MODEL // ATTN_HEAD_DIM
ATTN_KV_HEADS = 4
ATTN_GROUP = ATTN_Q_HEADS // ATTN_KV_HEADS
ATTN_Q_DIM = ATTN_Q_HEADS * ATTN_HEAD_DIM
ATTN_KV_DIM = ATTN_KV_HEADS * ATTN_HEAD_DIM
ATTN_BLOCK = 128
ATTN_SCALE = ATTN_HEAD_DIM ** -0.5
ROPE_THETA = 10000.0

N_GLA = (DEPTH_2 + 2) // 3
N_CONV = (DEPTH_2 + 1) // 3
N_ATTN = DEPTH_2 // 3


def rms_norm(x, g):
    xf = x.astype(jnp.float32)
    y = xf * lax.rsqrt(jnp.mean(xf * xf, axis=-1, keepdims=True) + EPS)
    return (y * g.astype(jnp.float32)).astype(x.dtype)

def layer_norm(x, g, b):
    xf = x.astype(jnp.float32)
    mu = jnp.mean(xf, axis=-1, keepdims=True)
    xc = xf - mu
    y = xc * lax.rsqrt(jnp.mean(xc * xc, axis=-1, keepdims=True) + EPS)
    return (y * g.astype(jnp.float32) + b.astype(jnp.float32)).astype(x.dtype)

def split_heads_2(t, n):
    B, L, _ = t.shape
    return t.reshape(B, L, n, -1).transpose(0, 2, 1, 3)

def axial_rope_tables(row_idx, col_idx):
    n = ATTN_HEAD_DIM // 4
    inv = ROPE_THETA ** (-jnp.arange(n, dtype=jnp.float32) / n)
    ang = jnp.concatenate([row_idx.astype(jnp.float32)[:, None] * inv,
                           col_idx.astype(jnp.float32)[:, None] * inv], axis=-1)
    return jnp.cos(ang), jnp.sin(ang)

def apply_rope(x, cos, sin):
    half = x.shape[-1] // 2
    cos = cos.astype(x.dtype)
    sin = sin.astype(x.dtype)
    x1, x2 = x[..., :half], x[..., half:]
    return jnp.concatenate([x1 * cos - x2 * sin, x2 * cos + x1 * sin], axis=-1)

def gla_chunk_scan(q, k, v, logg, s0):
    B, H, L, _ = q.shape
    n = L // GLA_CHUNK

    def to_chunks(a):
        return jnp.moveaxis(a.reshape(B, H, n, GLA_CHUNK, a.shape[-1]), 2, 0)

    mask = jnp.tril(jnp.ones((GLA_CHUNK, GLA_CHUNK), dtype=bool))

    def step(s, inp):
        qc, kc, vc, gc = inp
        b = jnp.cumsum(gc, axis=-2)
        b_last = b[..., -1:, :]
        qb = qc * jnp.exp(b)
        kb = kc * jnp.exp(-b)
        a = jnp.where(mask, jnp.einsum('bhid,bhjd->bhij', qb, kb), 0.0)
        o = jnp.einsum('bhid,bhde->bhie', qb, s) + jnp.einsum('bhij,bhje->bhie', a, vc)
        kd = kc * jnp.exp(b_last - b)
        s_new = jnp.exp(b_last[..., 0, :])[..., None] * s + jnp.einsum('bhjd,bhje->bhde', kd, vc)
        return s_new, o

    s_fin, o = lax.scan(step, s0, (to_chunks(q), to_chunks(k), to_chunks(v), to_chunks(logg)))
    o = jnp.moveaxis(o, 0, 2).reshape(B, H, L, v.shape[-1])
    return o, s_fin

def gla_mixer(h_ctx, h_lat, w_in, w_g1, w_g2, b_g, g_head, w_out, need_ctx):
    f32 = jnp.float32

    def project(h):
        z = h @ w_in
        q, k, v, r = jnp.split(z, [GLA_KEY_DIM, 2 * GLA_KEY_DIM, 2 * GLA_KEY_DIM + GLA_VAL_DIM], axis=-1)
        q = split_heads_2(q, GLA_HEADS).astype(f32) * (GLA_DK ** -0.5)
        k = split_heads_2(k, GLA_HEADS).astype(f32)
        v = split_heads_2(v, GLA_HEADS).astype(f32)
        gates = []
        for d in range(2):
            zg = (h @ w_g1[d]) @ w_g2[d] + b_g[d]
            gates.append(split_heads_2(jax.nn.log_sigmoid(zg.astype(f32)) / GLA_TAU, GLA_HEADS))
        return q, k, v, r, gates[0], gates[1]

    qc, kc, vc, rc, gcf, gcb = project(h_ctx)
    ql, kl, vl, rl, glf, glb = project(h_lat)

    def flip(a):
        return jnp.flip(a, axis=2)

    B = h_lat.shape[0]
    s0 = jnp.zeros((B, GLA_HEADS, GLA_DK, GLA_DV), f32)
    oc_f, s_f = gla_chunk_scan(qc, kc, vc, gcf, s0)
    oc_b, s_b = gla_chunk_scan(flip(qc), flip(kc), flip(vc), flip(gcb), s0)
    ol_f, _ = gla_chunk_scan(ql, kl, vl, glf, s_f)
    ol_b, _ = gla_chunk_scan(flip(ql), flip(kl), flip(vl), flip(glb), s_b)

    def finish(o, r, dtype):
        o = rms_norm(o, g_head)
        o = o.transpose(0, 2, 1, 3).reshape(o.shape[0], o.shape[2], GLA_VAL_DIM).astype(dtype)
        return (o * jax.nn.silu(r)) @ w_out

    y_lat = finish(ol_f + flip(ol_b), rl, h_lat.dtype)
    y_ctx = finish(oc_f + flip(oc_b), rc, h_ctx.dtype) if need_ctx else None
    return y_ctx, y_lat

def conformer_conv(h, w_pw1, b_pw1, w_dw, b_dw, ln_g, ln_b, w_pw2, b_pw2):
    z = h @ w_pw1 + b_pw1
    a, gt = jnp.split(z, 2, axis=-1)
    u = a * jax.nn.sigmoid(gt)
    u = lax.conv_general_dilated(u, w_dw[:, None, :], window_strides=(1,),
                                 padding=[(CONV_PAD, CONV_PAD)],
                                 dimension_numbers=('NWC', 'WIO', 'NWC'),
                                 feature_group_count=D_MODEL) + b_dw
    u = jax.nn.silu(layer_norm(u, ln_g, ln_b))
    return u @ w_pw2 + b_pw2

def sdpa(q, k, v):
    s = jnp.einsum('bkgqd,bksd->bkgqs', q, k).astype(jnp.float32) * ATTN_SCALE
    p = jax.nn.softmax(s, axis=-1).astype(v.dtype)
    return jnp.einsum('bkgqs,bksd->bkgqd', p, v)

def gqa_mixer(h_ctx, h_lat, w_qkv, g_q, g_k, w_out, cos, sin, need_ctx):

    def project(h, rope):
        B, L, _ = h.shape
        z = h @ w_qkv
        q, k, v = jnp.split(z, [ATTN_Q_DIM, ATTN_Q_DIM + ATTN_KV_DIM], axis=-1)
        q = rms_norm(q.reshape(B, L, ATTN_KV_HEADS, ATTN_GROUP, ATTN_HEAD_DIM), g_q).transpose(0, 2, 3, 1, 4)
        k = rms_norm(k.reshape(B, L, ATTN_KV_HEADS, ATTN_HEAD_DIM), g_k).transpose(0, 2, 1, 3)
        v = v.reshape(B, L, ATTN_KV_HEADS, ATTN_HEAD_DIM).transpose(0, 2, 1, 3)
        if rope:
            q = apply_rope(q, cos, sin)
            k = apply_rope(k, cos, sin)
        return q, k, v

    def merge(o):
        B, _, _, L, _ = o.shape
        return o.transpose(0, 3, 1, 2, 4).reshape(B, L, ATTN_Q_DIM) @ w_out

    qc, kc, vc = project(h_ctx, False)
    ql, kl, vl = project(h_lat, True)
    y_ctx = merge(sdpa(qc, kc, vc)) if need_ctx else None

    k_all = jnp.concatenate([kc, kl], axis=2)
    v_all = jnp.concatenate([vc, vl], axis=2)
    B, KV, G, L, hd = ql.shape
    nb = L // ATTN_BLOCK
    qb = jnp.moveaxis(ql.reshape(B, KV, G, nb, ATTN_BLOCK, hd), 3, 0)
    ob = lax.map(lambda qq: sdpa(qq, k_all, v_all), qb)
    ol = jnp.moveaxis(ob, 0, 3).reshape(B, KV, G, L, hd)
    return y_ctx, merge(ol)

def sq_relu_mlp(h, w_in, w_out):
    return jnp.square(jax.nn.relu(h @ w_in)) @ w_out

def second_inputs(seed: int = 0) -> dict:
    key = jax.random.key(seed)
    ks = iter(jax.random.split(key, 40))
    D = D_MODEL

    def nrm(shape, scale):
        return jax.random.normal(next(ks), shape, jnp.float32) * scale

    return {
        "x": nrm((BATCH, SEQ, D), 1.0),
        "c": nrm((BATCH, D), 1.0),
        "ctx": nrm((BATCH, CTX_LEN, D), 1.0),
        "c_ctx": nrm((D,), 1.0),
        "w_mod": nrm((DEPTH_2, D, 6 * D), 0.5 * D ** -0.5),
        "b_mod": nrm((DEPTH_2, 6 * D), 0.01),
        "g_norm_mix": 1.0 + nrm((DEPTH_2, D), 0.02),
        "g_norm_mlp": 1.0 + nrm((DEPTH_2, D), 0.02),
        "w_mlp_in": nrm((DEPTH_2, D, D_FF_2), D ** -0.5),
        "w_mlp_out": nrm((DEPTH_2, D_FF_2, D), D_FF_2 ** -0.5),
        "gla_w_in": nrm((N_GLA, D, 2 * GLA_KEY_DIM + 2 * GLA_VAL_DIM), D ** -0.5),
        "gla_w_g1": nrm((N_GLA, 2, D, GLA_RANK), D ** -0.5),
        "gla_w_g2": nrm((N_GLA, 2, GLA_RANK, GLA_KEY_DIM), GLA_RANK ** -0.5),
        "gla_b_g": nrm((N_GLA, 2, GLA_KEY_DIM), 0.1),
        "gla_g_head": 1.0 + nrm((N_GLA, GLA_DV), 0.02),
        "gla_w_out": nrm((N_GLA, GLA_VAL_DIM, D), GLA_VAL_DIM ** -0.5),
        "conv_w_pw1": nrm((N_CONV, D, 2 * D), D ** -0.5),
        "conv_b_pw1": nrm((N_CONV, 2 * D), 0.01),
        "conv_w_dw": nrm((N_CONV, CONV_WIDTH, D), CONV_WIDTH ** -0.5),
        "conv_b_dw": nrm((N_CONV, D), 0.01),
        "conv_ln_g": 1.0 + nrm((N_CONV, D), 0.02),
        "conv_ln_b": nrm((N_CONV, D), 0.01),
        "conv_w_pw2": nrm((N_CONV, D, D), D ** -0.5),
        "conv_b_pw2": nrm((N_CONV, D), 0.01),
        "attn_w_qkv": nrm((N_ATTN, D, ATTN_Q_DIM + 2 * ATTN_KV_DIM), D ** -0.5),
        "attn_g_q": 1.0 + nrm((N_ATTN, ATTN_HEAD_DIM), 0.02),
        "attn_g_k": 1.0 + nrm((N_ATTN, ATTN_HEAD_DIM), 0.02),
        "attn_w_out": nrm((N_ATTN, ATTN_Q_DIM, D), ATTN_Q_DIM ** -0.5),
    }

def second_block(x, c, ctx, c_ctx, w_mod, b_mod, g_norm_mix, g_norm_mlp, w_mlp_in, w_mlp_out,
              gla_w_in, gla_w_g1, gla_w_g2, gla_b_g, gla_g_head, gla_w_out,
              conv_w_pw1, conv_b_pw1, conv_w_dw, conv_b_dw, conv_ln_g, conv_ln_b, conv_w_pw2, conv_b_pw2,
              attn_w_qkv, attn_g_q, attn_g_k, attn_w_out):
    L = x.shape[1]
    rows = L // GRID_W
    row_idx = jnp.repeat(jnp.arange(rows, dtype=jnp.int32), GRID_W)
    col_idx = jnp.tile(jnp.arange(GRID_W, dtype=jnp.int32), rows)
    cos, sin = axial_rope_tables(row_idx, col_idx)

    silu_c = jax.nn.silu(c)
    silu_cc = jax.nn.silu(c_ctx)
    x_lat, x_ctx = x, ctx
    for i in range(DEPTH_2):
        last = i == DEPTH_2 - 1
        kind = i % N_MIXERS
        j = i // N_MIXERS
        mod_l = (silu_c @ w_mod[i] + b_mod[i])[:, None, :]
        mod_c = (silu_cc @ w_mod[i] + b_mod[i])[None, None, :]
        sh1_l, sc1_l, gt1_l, sh2_l, sc2_l, gt2_l = jnp.split(mod_l, 6, axis=-1)
        sh1_c, sc1_c, gt1_c, sh2_c, sc2_c, gt2_c = jnp.split(mod_c, 6, axis=-1)

        h_l = rms_norm(x_lat, g_norm_mix[i]) * (1.0 + sc1_l) + sh1_l
        h_c = rms_norm(x_ctx, g_norm_mix[i]) * (1.0 + sc1_c) + sh1_c
        if kind == 0:
            y_c, y_l = gla_mixer(h_c, h_l, gla_w_in[j], gla_w_g1[j], gla_w_g2[j], gla_b_g[j],
                                 gla_g_head[j], gla_w_out[j], not last)
        elif kind == 1:
            conv_args = (conv_w_pw1[j], conv_b_pw1[j], conv_w_dw[j], conv_b_dw[j],
                         conv_ln_g[j], conv_ln_b[j], conv_w_pw2[j], conv_b_pw2[j])
            y_l = conformer_conv(h_l, *conv_args)
            y_c = None if last else conformer_conv(h_c, *conv_args)
        else:
            y_c, y_l = gqa_mixer(h_c, h_l, attn_w_qkv[j], attn_g_q[j], attn_g_k[j], attn_w_out[j],
                                 cos, sin, not last)
        x_lat = x_lat + gt1_l * y_l

        h_l = rms_norm(x_lat, g_norm_mlp[i]) * (1.0 + sc2_l) + sh2_l
        x_lat = x_lat + gt2_l * sq_relu_mlp(h_l, w_mlp_in[i], w_mlp_out[i])
        if not last:
            x_ctx = x_ctx + gt1_c * y_c
            h_c = rms_norm(x_ctx, g_norm_mlp[i]) * (1.0 + sc2_c) + sh2_c
            x_ctx = x_ctx + gt2_c * sq_relu_mlp(h_c, w_mlp_in[i], w_mlp_out[i])
    return x_lat


def setup_inputs(seed=0):
    out = dict(first_inputs(seed))
    for name, value in second_inputs(seed + 1).items():
        if name != "x":
            out[name + "_2"] = value
    return out


def reference(
    x, mem, mem_norm, norm_mix, norm_xattn, norm_ffn, ev_w_in, pool_w, pool_scale, ev_w_out,
    od_w_in, sgu_ln_g, sgu_ln_b, sgu_w, sgu_b, dn_conv, dn_a_log, dn_dt_bias, dn_norm_g,
    od_w_out, xattn_wq, xattn_wkv, xattn_wo, ffn_w_up, ffn_conv, ffn_w_down, final_norm, c_2,
    ctx_2, c_ctx_2, w_mod_2, b_mod_2, g_norm_mix_2, g_norm_mlp_2, w_mlp_in_2, w_mlp_out_2,
    gla_w_in_2, gla_w_g1_2, gla_w_g2_2, gla_b_g_2, gla_g_head_2, gla_w_out_2, conv_w_pw1_2,
    conv_b_pw1_2, conv_w_dw_2, conv_b_dw_2, conv_ln_g_2, conv_ln_b_2, conv_w_pw2_2,
    conv_b_pw2_2, attn_w_qkv_2, attn_g_q_2, attn_g_k_2, attn_w_out_2,
):
    x = first_block(
        x, mem, mem_norm, norm_mix, norm_xattn, norm_ffn, ev_w_in, pool_w, pool_scale, ev_w_out,
        od_w_in, sgu_ln_g, sgu_ln_b, sgu_w, sgu_b, dn_conv, dn_a_log, dn_dt_bias, dn_norm_g,
        od_w_out, xattn_wq, xattn_wkv, xattn_wo, ffn_w_up, ffn_conv, ffn_w_down, final_norm,
    )
    return second_block(
        x, c_2, ctx_2, c_ctx_2, w_mod_2, b_mod_2, g_norm_mix_2, g_norm_mlp_2, w_mlp_in_2,
        w_mlp_out_2, gla_w_in_2, gla_w_g1_2, gla_w_g2_2, gla_b_g_2, gla_g_head_2, gla_w_out_2,
        conv_w_pw1_2, conv_b_pw1_2, conv_w_dw_2, conv_b_dw_2, conv_ln_g_2, conv_ln_b_2,
        conv_w_pw2_2, conv_b_pw2_2, attn_w_qkv_2, attn_g_q_2, attn_g_k_2, attn_w_out_2,
    )


_drawn_inputs = setup_inputs


def setup_inputs(seed=0):
    import zlib

    import numpy as np

    out = dict(_drawn_inputs(seed))
    spreads = {}
    factors = {'mem_norm': 8.0,
     'norm_xattn': 8.0,
     'sgu_ln_g': 8.0,
     'sgu_ln_b': 8.0,
     'sgu_b': 8.0,
     'dn_norm_g': 8.0,
     'g_norm_mix_2': 5.026,
     'g_norm_mlp_2': 3.394,
     'gla_b_g_2': 4.119,
     'gla_g_head_2': 8.0,
     'conv_b_pw1_2': 44.101,
     'conv_b_dw_2': 35.968,
     'conv_ln_g_2': 47.809,
     'conv_ln_b_2': 185.406,
     'conv_b_pw2_2': 64.0,
     'attn_g_q_2': 29.52,
     'attn_g_k_2': 27.605}
    for name, (base, spread) in spreads.items():
        noise = np.random.default_rng([zlib.crc32(name.encode()), seed]).standard_normal(out[name].shape)
        drawn = base * np.exp(spread * noise) if base else spread * noise
        out[name] = __import__('jax').numpy.asarray(drawn.astype(out[name].dtype))
    for name, factor in factors.items():
        out[name] = (out[name] * factor).astype(out[name].dtype)
    return out
```

```python
import numpy as np
import concourse.bass as bass
from concourse import mybir
from concourse.alu_op_type import AluOpType as ALU
from contextlib import ExitStack

F32 = mybir.dt.float32
ACT = mybir.ActivationFunctionType
AX_X = mybir.AxisListType.X

P = 128
D = 1024
KD = D // P
S = 256
T2 = 2 * S
EPS = 1e-6
MOBA_HEADS, MOBA_DIM = 8, 64
A_WIDTH = MOBA_HEADS * MOBA_DIM
POOL_WINDOWS = (2, 4, 8, 16)
SGU_WIDTH = 512
DN_HEADS, DN_CONV, DN_WIDTH = 4, 4, 512
X_HEADS = 4
D_FF = 2816
FC = D_FF // P
FFN_CONV = 3
LAYERS2 = 4
D_FF2 = 4096
FC2 = D_FF2 // P
GLA_HEADS, GLA_DK, GLA_DV, GLA_RANK, GLA_TAU, GLA_C = 4, 128, 256, 16, 16.0, 64
CONV_W = 31
CONV_PAD = CONV_W // 2
PADDED = S + 2 * CONV_PAD
KV_HEADS, Q_HEADS, HD = 4, 16, 64
GRID_W = 64
NEG = -1e30


def spans(sizes):
    at, out = 0, {}
    for name, n in sizes:
        out[name] = (at, n)
        at += n
    return out, at


VEC, NVEC = spans([
    ("mem_norm", KD), ("norm_mix", 2 * KD), ("norm_xattn", 2 * KD), ("norm_ffn", 2 * KD), ("pool_scale", 4),
    ("final_norm", KD), ("dn_conv", DN_CONV * 12), ("dn_norm_g", 1), ("ffn_conv", 2 * FFN_CONV * 2 * FC),
    ("g_norm_mix", LAYERS2 * KD), ("g_norm_mlp", LAYERS2 * KD), ("b_mod", LAYERS2 * 6 * KD),
    ("gla_b_g", 2 * 2 * GLA_HEADS), ("gla_g_head", 2 * 2), ("b_pw1", 2 * KD), ("w_dw", CONV_W * KD), ("b_dw", KD),
    ("ln_g", KD), ("ln_b", KD), ("b_pw2", KD), ("g_q", 1), ("g_k", 1), ("c", 2 * KD)])
ROW, NROW = spans([("sgu_ln_g", SGU_WIDTH), ("sgu_ln_b", SGU_WIDTH), ("sgu_b", 4 * P), ("a_log", DN_HEADS),
                   ("dt_bias", DN_HEADS)])
INV_LEVELS = (1, 2, 4, 8, 16, 32, 64)
CON, NCON = spans([("ident", P), ("ones", P), ("head_ones", P), ("causal", P), ("upto", P), ("rope_swap", P),
                   ("level", P * len(INV_LEVELS)), ("gla_mask", 2 * GLA_HEADS * GLA_C), ("restart", T2),
                   ("cos", S), ("sin", S), ("pool_inv", 4 * S), ("eps", 1), ("one", 1)])


def shape_constants():
    c = np.zeros((P, NCON), np.float32)

    def put(name, value):
        at, n = CON[name]
        c[:, at:at + n] = value

    i = np.arange(P)
    put("ident", np.eye(P))
    put("ones", 1.0)
    put("head_ones", (i[:, None] // HD) == (i[None, :] // HD))
    put("causal", np.where(i[None, :] <= i[:, None], 0.0, NEG))
    put("upto", i[:, None] <= i[None, :])
    put("rope_swap", (i[:, None] ^ 32) == i[None, :])
    levels = []
    for s in INV_LEVELS:
        same = (i[:, None] // (2 * s)) == (i[None, :] // (2 * s))
        levels.append(same & (i[:, None] % (2 * s) < s) & (i[None, :] % (2 * s) >= s))
    put("level", np.concatenate(levels, axis=1))
    j, t = i[:, None] % GLA_C, np.arange(GLA_C)[None, :]
    put("gla_mask", np.concatenate([np.tile(j <= t, (1, GLA_HEADS)), np.tile(j >= t, (1, GLA_HEADS))], axis=1))
    put("restart", (np.arange(T2) % GLA_C != 0)[None, :])
    n = HD // 4
    inv = np.float32(10000.0) ** (-np.arange(n, dtype=np.float32) / np.float32(n))
    tok = np.arange(S)
    ang = np.concatenate([(tok // GRID_W).astype(np.float32)[:, None] * inv,
                          (tok % GRID_W).astype(np.float32)[:, None] * inv], axis=1).astype(np.float32)
    put("cos", np.cos(ang).T[i % 32])
    put("sin", np.sin(ang).T[i % 32] * np.where(i % HD < 32, -1.0, 1.0)[:, None])
    put("pool_inv", np.concatenate([1.0 / np.minimum(tok + 1.0, w) for w in POOL_WINDOWS])[None, :])
    put("eps", EPS)
    put("one", 1.0)
    return c


class Lane:

    def __init__(self, engine, sem):
        self.engine, self.sem, self.count, self.seen = engine, sem, 0, {}

    def done(self, ins):
        ins.then_inc(self.sem, 1)
        self.count += 1
        return (self.sem, self.count)

    def last(self):
        return (self.sem, self.count)

    def wait(self, *marks):
        for sem, value in marks:
            if value > self.seen.get(sem.name, 0):
                self.engine.wait_ge(sem, value)
                self.seen[sem.name] = value

    def chain(self):
        self.wait(self.last())


class Ring:

    def __init__(self, tiles):
        self.free = [(t, ()) for t in tiles]

    def take(self, *lanes):
        tile, marks = self.free.pop(0)
        for lane in lanes:
            lane.wait(*marks)
        return tile

    def give(self, tile, *marks):
        self.free.append((tile, marks))


def build(nc, io):
    ctx = ExitStack()
    with ctx:
        def sb(name, cols):
            return ctx.enter_context(nc.sbuf_tensor(name, [P, cols], F32))

        def lane(engine, name):
            return Lane(engine, ctx.enter_context(nc.semaphore(name)))

        pe, act, dve, pool, sp = (lane(nc.tensor, "pe_done"), lane(nc.scalar, "act_done"), lane(nc.vector, "dve_done"),
                                  lane(nc.gpsimd, "pool_done"), lane(nc.sync, "sp_unused"))
        dma_count = {}

        def dma(out, in_, sem):
            nc.sync.dma_start(out, in_).then_inc(sem, 16)
            dma_count[sem.name] = dma_count.get(sem.name, 0) + 16
            return (sem, dma_count[sem.name])

        x = sb("x", KD * T2)[:, :].rearrange("p (k t) -> p k t", k=KD)
        xn = sb("xn", KD * T2)[:, :].rearrange("p (k t) -> p k t", k=KD)
        con_t = sb("con_t", NCON)
        vec_t = sb("vec_t", NVEC)
        row_t = sb("row_t", NROW)
        mod_t = sb("mod_t", LAYERS2 * 6 * KD * 2)
        modA = sb("modA", KD * 2)
        silu_c = sb("silu_c", KD * 2)
        arena = sb("arena", 21504)
        small_t = sb("small_t", 32 * 8)
        WSLOT, NW = 2048, 6
        wslots = sb("wslots", WSLOT * NW)
        NSCR = 7
        scr_t = sb("scr_t", NSCR * 512)
        banks_t = [ctx.enter_context(nc.psum_tensor(f"bank{i}", [P, 512], F32)) for i in range(8)]
        psum = Ring([b[:, :] for b in banks_t])
        scr = Ring([scr_t[:, i * 512:(i + 1) * 512] for i in range(NSCR)])
        small = Ring([small_t[:, i * 8:(i + 1) * 8] for i in range(32)])
        wring = Ring([(wslots[:, i * WSLOT:(i + 1) * WSLOT], ctx.enter_context(nc.semaphore(f"w_in{i}")))
                      for i in range(NW)])
        in_sem = [ctx.enter_context(nc.semaphore(f"in{i}")) for i in range(8)]
        out_sem = ctx.enter_context(nc.semaphore("out_done"))

        def con(name, i=0, n=None):
            at, size = CON[name]
            return con_t[:, at + i:at + (size if n is None else i + n)]

        def vec(name, i=0, n=1):
            return vec_t[:, VEC[name][0] + i:VEC[name][0] + i + n]

        def row(name, i=0, n=None):
            at, size = ROW[name]
            return row_t[:, at + i:at + (size if n is None else i + n)]

        def region(at, chunks, width):
            return arena[:, at:at + chunks * width].rearrange("p (k t) -> p k t", k=chunks)

        ident = con("ident")
        eps = con("eps")

        con_in = dma(con_t[:, :], io["con"], in_sem[0])
        vec_in = dma(vec_t[:, :], io["vec"], in_sem[1])
        mem_t = region(0, KD, S)
        mem_in = dma(mem_t, io["memT"], in_sem[5])
        x_in = dma(x[:, :, 0:S], io["xT"], in_sem[2])
        row_in = dma(row_t[:, :], io["row"], in_sem[4])
        nc.scalar.preload_act_table_set("natural_log_exp_and_others")
        for e in (pe, act, dve, pool):
            e.wait(con_in, vec_in)
        act.wait(row_in)
        dve.wait(row_in)

        def mm(out, lhsT, rhs, start=True, stop=True):
            return nc.tensor.matmul(out, lhsT, rhs, start=start, stop=stop)

        def v_tt(out, a, b, op):
            return dve.done(nc.vector.tensor_tensor(out, a, b, op))

        def v_ts(out, a, s1, s2=None, op0=ALU.mult, op1=None):
            if op1 is None:
                return dve.done(nc.vector.tensor_scalar(out, a, s1, None, op0))
            return dve.done(nc.vector.tensor_scalar(out, a, s1, s2, op0, op1))

        def v_stt(out, a, s, b, op0, op1):
            return dve.done(nc.vector.scalar_tensor_tensor(out=out, in0=a, scalar=s, in1=b, op0=op0, op1=op1))

        def a_act(out, in_, func, bias=0.0, scale=1.0, accum=None):
            if accum is not None:
                return act.done(nc.scalar.activation(out, in_, func, bias=bias, scale=scale, accum_out=accum))
            return act.done(nc.scalar.activation(out, in_, func, bias=bias, scale=scale))

        mod_work = iter(())

        def load_weights(src, kw, nw):
            slot = wring.take(sp)
            tile, sem = slot
            view = tile[:, 0:kw * nw].rearrange("p (k n) -> p k n", k=kw)
            return slot, view, dma(view, src, sem)

        def linear(W, kchunks, n_lo, n_hi, rhs, ready, T, evac, fill=True):
            Wv = W.rearrange("(k p) n -> p k n", p=P)
            for nb in range(n_lo, n_hi, 512):
                nw = min(512, n_hi - nb)
                nj = nw // P
                banks = [psum.take(pe) for _ in range(nj)]
                for kb in range(0, kchunks, 4):
                    kw = min(4, kchunks - kb)
                    slot, w, landed = load_weights(Wv[:, kb:kb + kw, nb:nb + nw], kw, nw)
                    pe.wait(landed)
                    for j in range(nj):
                        for k in range(kw):
                            pe.wait(ready[kb + k])
                            ins = mm(banks[j][:, 0:T], w[:, k, j * P:(j + 1) * P], rhs(kb + k),
                                     start=(kb + k == 0), stop=(kb + k == kchunks - 1))
                        if kb + kw == kchunks or j == nj - 1:
                            mark = pe.done(ins)
                        if kb + kw == kchunks:
                            psum.give(banks[j], evac((nb - n_lo) // P + j, banks[j][:, 0:T], mark))
                    wring.give(slot, mark)
                if fill:
                    next(mod_work, None)

        def linear_rows(W, n_lo, n_hi, lhs, ready, tiles, evac, fill=True):
            Wv = W.rearrange("(k p) n -> p k n", p=P)
            for nb in range(n_lo, n_hi, 512):
                nw = min(512, n_hi - nb)
                banks = [psum.take(pe) for _ in range(tiles)]
                for kb in range(0, KD, 4):
                    slot, w, landed = load_weights(Wv[:, kb:kb + 4, nb:nb + nw], 4, nw)
                    pe.wait(landed)
                    for j in range(tiles):
                        for k in range(4):
                            pe.wait(ready[kb + k])
                            ins = mm(banks[j][:, 0:nw], lhs(kb + k, j), w[:, k, :],
                                     start=(kb + k == 0), stop=(kb + k == KD - 1))
                        mark = pe.done(ins)
                        if kb + 4 == KD:
                            psum.give(banks[j], evac(j, nb - n_lo, banks[j][:, 0:nw], mark))
                    wring.give(slot, mark)
                if fill:
                    next(mod_work, None)

        def column_sums(srcs, ready, T, ones, square=True):
            bank = psum.take(pe)
            for k, src in enumerate(srcs):
                if square:
                    sq = scr.take(act)
                    act.wait(ready[k])
                    m = a_act(sq[:, 0:T], src, ACT.Square)
                    pe.wait(m)
                    m = pe.done(mm(bank[:, 0:T], ones, sq[:, 0:T], start=(k == 0), stop=(k == len(srcs) - 1)))
                    scr.give(sq, m)
                else:
                    pe.wait(ready[k])
                    m = pe.done(mm(bank[:, 0:T], ones, src, start=(k == 0), stop=(k == len(srcs) - 1)))
            return bank, m

        def inv_rms(bank, m, T, mean_scale):
            r = scr.take(act)
            act.wait(m)
            m = a_act(r[:, 0:T], bank[:, 0:T], ACT.Ln, bias=eps, scale=mean_scale)
            psum.give(bank, m)
            act.chain()
            return r, a_act(r[:, 0:T], r[:, 0:T], ACT.Exp, scale=-0.5)

        def rms(src, gain, out, ready, T):
            bank, m = column_sums([src(k) for k in range(KD)], ready, T, con("ones"))
            r, m = inv_rms(bank, m, T, 1.0 / D)
            dve.wait(m)
            marks = [v_stt(out(k), src(k), gain(k), r[:, 0:T], ALU.mult, ALU.mult) for k in range(KD)]
            scr.give(r, marks[-1])
            return marks

        def sigmoid(out, src, m, T, scale=1.0):
            dve.wait(m)
            dve.chain()
            m = v_ts(out, src, -80.0 / scale, op0=ALU.max)
            act.wait(m)
            m = a_act(out, out, ACT.Exp, scale=-scale)
            dve.wait(m)
            v_ts(out, out, 1.0, op0=ALU.add)
            dve.chain()
            return dve.done(nc.vector.reciprocal(out, out))

        class Attention:
            def __init__(self, units, scale):
                self.units, self.scale, self.open = units, scale, []

            def scores(self, u):
                bank = psum.take(pe)
                nk = u["nk"]
                for i, (q, k) in enumerate(u["pairs"]):
                    pe.wait(*u["ready"])
                    ins = mm(bank[:, 0:nk], q, k, start=(i == 0), stop=(i == len(u["pairs"]) - 1))
                m = pe.done(ins)
                probs = scr.take(dve, act)
                stats = small.take(dve, act)
                src = bank[:, 0:nk]
                dve.wait(m)
                if u["causal"]:
                    if nk > P:
                        v_ts(probs[:, 0:nk - P], bank[:, 0:nk - P], 1.0)
                    m = v_tt(probs[:, nk - P:nk], bank[:, nk - P:nk], con("causal"), ALU.add)
                    psum.give(bank, m)
                    dve.chain()
                    src = probs[:, 0:nk]
                dve.done(nc.vector.tensor_reduce(stats[:, 0:1], src, AX_X, ALU.max))
                dve.chain()
                m = v_ts(stats[:, 1:2], stats[:, 0:1], -self.scale)
                act.wait(m)
                m = a_act(probs[:, 0:nk], src, ACT.Exp, bias=stats[:, 1:2], scale=self.scale, accum=stats[:, 2:3])
                if not u["causal"]:
                    psum.give(bank, m)
                dve.wait(m)
                dve.done(nc.vector.reciprocal(stats[:, 3:4], stats[:, 2:3]))
                dve.chain()
                m = v_ts(probs[:, 0:nk], probs[:, 0:nk], stats[:, 3:4])
                small.give(stats, m)
                self.open.append((u, probs, m))

            def finish(self):
                u, probs, m = self.open.pop(0)
                nk = u["nk"]
                bank = psum.take(pe)
                pe.wait(m)
                for t in range(nk // P):
                    ins = nc.tensor.transpose(bank[:, t * P:(t + 1) * P], probs[:, t * P:(t + 1) * P], ident)
                m = pe.done(ins)
                scr.give(probs, m)
                turned = scr.take(act)
                act.wait(m)
                m = a_act(turned[:, 0:nk], bank[:, 0:nk], ACT.Copy)
                psum.give(bank, m)
                out = psum.take(pe)
                pe.wait(m)
                for o_rows, values, dst, part in u["outs"]:
                    for t in range(nk // P):
                        ins = mm(out[o_rows, part * P:(part + 1) * P], values(t), turned[:, t * P:(t + 1) * P],
                                 start=(t == 0), stop=(t == nk // P - 1))
                m = pe.done(ins)
                scr.give(turned, m)
                dve.wait(m)
                for o_rows, values, dst, part in u["outs"]:
                    m = v_ts(dst, out[o_rows, part * P:(part + 1) * P], 1.0)
                psum.give(out, m)

            def run(self, lag=2):
                for i in range(len(self.units) + lag):
                    if i < len(self.units):
                        self.scores(self.units[i])
                    if i >= lag:
                        self.finish()
                return dve.last()

        def add_to_x(gate=None):
            marks = [None] * KD

            def evac(n, bank, m):
                dve.wait(m)
                T = bank.shape[-1]
                if gate is None:
                    marks[n] = v_tt(x[:, n, 0:T], bank, x[:, n, 0:T], ALU.add)
                else:
                    for s0 in range(0, T, S):
                        marks[n] = v_stt(x[:, n, s0:s0 + S], bank[:, s0:s0 + S], gate(n, s0 // S),
                                         x[:, n, s0:s0 + S], ALU.mult, ALU.add)
                return marks[n]
            return evac, marks

        def copy_to(dst, marks, scale=1.0):
            def evac(n, bank, m):
                act.wait(m)
                marks.append(a_act(dst(n), bank, ACT.Copy, scale=scale))
                return marks[-1]
            return evac

        def causal_conv(out, bank, m, taps, T):
            dve.wait(m)
            m = v_ts(out, bank, taps[0])
            for j in range(1, len(taps)):
                dve.chain()
                m = v_stt(out[:, j:T], bank[:, 0:T - j], taps[j], out[:, j:T], ALU.mult, ALU.add)
            return m

        def hx(k):
            return x[:, k, 0:S]

        def hn(k):
            return xn[:, k, 0:S]

        def hn_tile(k, j):
            return xn[:, k, j * P:(j + 1) * P]

        mod_v = mod_t[:, :].rearrange("p (l n s) -> p l n s", l=LAYERS2, s=2)
        cc = vec("c", 0, 2 * KD)
        m = sigmoid(silu_c[:, :], cc, vec_in, 2 * KD)
        dve.chain()
        silu_ready = v_tt(silu_c[:, :], silu_c[:, :], cc, ALU.mult)
        silu_v = silu_c[:, :].rearrange("p (k s) -> p k s", s=2)

        def modulation():
            for l in range(LAYERS2):
                def evac(n, bank, m, l=l):
                    dve.wait(m)
                    return v_ts(mod_v[:, l, n, :], bank, vec("b_mod", l * 6 * KD + n), op0=ALU.add)
                for nb in range(0, 6 * D, 512):
                    linear(io["w_mod"][l][:, nb:nb + 512], KD, 0, 512, lambda k: silu_v[:, k, :], [silu_ready] * KD, 2,
                           lambda n, b, m, nb=nb: evac(nb // P + n, b, m), fill=False)
                    yield

        mod_work = modulation()

        memn = region(2048, KD, S)
        memn_ready = rms(lambda k: mem_t[:, k, :], lambda k: vec("mem_norm", k), lambda k: memn[:, k, :],
                         [mem_in] * KD, S)
        ready = [x_in] * KD

        for layer in range(2):
            xn_ready = rms(hx, lambda k: vec("norm_mix", layer * KD + k), hn, ready, S)
            mix = region(4096, KD, S)
            mix_ready = [None] * KD
            if layer == 0:
                qk = region(6144, KD, S)
                v = region(8192, 2, A_WIDTH)
                p = region(9216, 4, S)
                W = io["ev_w_in"]
                qk_ready, v_ready, p_ready = [], [], []
                linear(W, KD, 0, 2 * A_WIDTH, hn, xn_ready, S, copy_to(lambda n: qk[:, n, :], qk_ready))

                def evac_v(j, n, bank, m):
                    act.wait(m)
                    v_ready.append(a_act(v[:, j, n:n + 512], bank, ACT.Copy))
                    return v_ready[-1]
                linear_rows(W, 2 * A_WIDTH, 3 * A_WIDTH, hn_tile, xn_ready, 2, evac_v)
                linear(W, KD, 3 * A_WIDTH, 3 * A_WIDTH + 512, hn, xn_ready, S, copy_to(lambda n: p[:, n, :], p_ready))
                units = []
                for h in range(MOBA_HEADS):
                    part = slice(HD * (h % 2), HD * (h % 2) + HD)
                    for qt in range(2):
                        q_ap = qk[part, h // 2, qt * P:(qt + 1) * P]
                        k_ap = qk[part, 4 + h // 2, 0:(qt + 1) * P]
                        units.append(dict(nk=(qt + 1) * P, pairs=[(q_ap, k_ap)], causal=True,
                                          ready=[qk_ready[-1], v_ready[-1]],
                                          outs=[(part, (lambda t, h=h: v[:, t, h * HD:(h + 1) * HD]),
                                                 mix[part, h // 2, qt * P:(qt + 1) * P], 0)]))
                attended = Attention(units, HD ** -0.5).run()
                for n in range(4):
                    mix_ready[n] = attended
                pool_w = region(10240, 4, P)
                pool_w_in = dma(pool_w, io["pool_w"], in_sem[6])
                dve.wait(p_ready[-1])
                for g, w in enumerate(POOL_WINDOWS):
                    a, b = scr.take(dve), scr.take(dve)
                    src = p[:, g, :]
                    step = 1
                    while step < w:
                        v_ts(b[:, 0:step], src[:, 0:step], 1.0)
                        v_tt(b[:, step:S], src[:, step:S], src[:, 0:S - step], ALU.add)
                        dve.chain()
                        src, a, b = b[:, 0:S], b, a
                        step *= 2
                    v_tt(b[:, 0:S], src, con("pool_inv", g * S, S), ALU.mult)
                    dve.chain()
                    m = v_tt(b[:, 0:S], b[:, 0:S], p[:, g, :], ALU.subtract)
                    scr.give(a, m)
                    bank = psum.take(pe)
                    pe.wait(m, pool_w_in)
                    m = pe.done(mm(bank[:, 0:S], pool_w[:, g, :], b[:, 0:S]))
                    scr.give(b, m)
                    dve.wait(m)
                    mix_ready[4 + g] = v_ts(mix[:, 4 + g, :], bank[:, 0:S], vec("pool_scale", g))
                    psum.give(bank, mix_ready[4 + g])
                w_out = io["ev_w_out"]
            else:
                W = io["od_w_in"]
                u = region(6144, 4, S)
                vr = region(7168, 2, SGU_WIDTH)
                dqkv = region(8192, 12, S)
                gate = region(11264, 4, S)

                def gelu(out, bank, m, T):
                    raw, t = scr.take(act), scr.take(act, dve)
                    act.wait(m)
                    done = a_act(raw[:, 0:T], bank, ACT.Copy)
                    act.chain()
                    m = a_act(t[:, 0:T], raw[:, 0:T], ACT.Square)
                    dve.wait(m)
                    v_ts(t[:, 0:T], t[:, 0:T], 0.044715, 1.0, ALU.mult, ALU.add)
                    dve.chain()
                    m = v_tt(t[:, 0:T], t[:, 0:T], raw[:, 0:T], ALU.mult)
                    sigmoid(t[:, 0:T], t[:, 0:T], m, T, scale=2.0 * float(np.sqrt(2.0 / np.pi)))
                    dve.chain()
                    m = v_tt(out, t[:, 0:T], raw[:, 0:T], ALU.mult)
                    scr.give(raw, m)
                    scr.give(t, m)
                    return done, m

                u_ready, vr_ready = [], []

                def evac_u(n, bank, m):
                    done, m = gelu(u[:, n, :], bank, m, S)
                    u_ready.append(m)
                    return done

                def evac_vr(j, n, bank, m):
                    done, m = gelu(vr[:, j, n:n + 512], bank, m, 512)
                    vr_ready.append(m)
                    return done
                linear(W, KD, 0, SGU_WIDTH, hn, xn_ready, S, evac_u)
                linear_rows(W, SGU_WIDTH, 2 * SGU_WIDTH, hn_tile, xn_ready, 2, evac_vr)
                d_ready = []

                def silu_into(out, src, m, T):
                    t = scr.take(act, dve)
                    sigmoid(t[:, 0:T], src, m, T)
                    dve.chain()
                    m = v_tt(out, src, t[:, 0:T], ALU.mult)
                    scr.give(t, m)
                    return m

                def evac_d(n, bank, m):
                    done = causal_conv(dqkv[:, n, :], bank, m, [vec("dn_conv", (DN_CONV - 1 - j) * 12 + n)
                                                               for j in range(DN_CONV)], S)
                    d_ready.append(silu_into(dqkv[:, n, :], dqkv[:, n, :], done, S))
                    return done
                linear(W, KD, 2 * SGU_WIDTH, 2 * SGU_WIDTH + 3 * DN_WIDTH, hn, xn_ready, S, evac_d)
                gate_ready = []

                def evac_g(n, bank, m):
                    gate_ready.append(silu_into(gate[:, n, :], bank, m, S))
                    return gate_ready[-1]
                g0 = 2 * SGU_WIDTH + 3 * DN_WIDTH
                linear(W, KD, g0, g0 + DN_WIDTH, hn, xn_ready, S, evac_g)
                beta, decay = arena[:, 20992:21000], arena[:, 21000:21008]
                ab = arena[:, 21008:21024]

                def evac_ab(j, n, bank, m):
                    act.wait(m)
                    return a_act(ab[:, j * 8:(j + 1) * 8], bank, ACT.Copy)
                linear_rows(W, g0 + DN_WIDTH, g0 + DN_WIDTH + 2 * DN_HEADS, hn_tile, xn_ready, 2, evac_ab)
                neg_a = small.take(act, dve)
                a_act(neg_a[:, 0:4], row("a_log"), ACT.Exp)
                tmp = small.take(act, dve)
                tmp2 = small.take(act, dve)
                for j in range(2):
                    braw, araw = ab[:, j * 8:j * 8 + 4], ab[:, j * 8 + 4:j * 8 + 8]
                    bj, gj = beta[:, j * 4:j * 4 + 4], decay[:, j * 4:j * 4 + 4]
                    sigmoid(bj, braw, act.last(), 4)
                    v_tt(gj, araw, row("dt_bias"), ALU.add)
                    act.wait(dve.last())
                    act.chain()
                    a_act(tmp[:, 0:4], gj, ACT.Abs)
                    act.chain()
                    a_act(tmp[:, 0:4], tmp[:, 0:4], ACT.Exp, scale=-1.0)
                    act.chain()
                    m = a_act(tmp2[:, 0:4], tmp[:, 0:4], ACT.Ln, bias=1.0)
                    dve.wait(m)
                    dve.chain()
                    v_stt(gj, gj, 0.0, tmp2[:, 0:4], ALU.max, ALU.add)
                    dve.chain()
                    m = v_stt(gj, gj, -1.0, neg_a[:, 0:4], ALU.mult, ALU.mult)
                    act.wait(m)
                for s_ in (neg_a, tmp, tmp2):
                    small.give(s_, m)
                beta_ready = m
                sgu_w = region(12288, 4, P)
                sgu_in = dma(sgu_w, io["sgu_wT"], in_sem[6])
                for j in range(2):
                    st = small.take(dve, act)
                    c0 = scr.take(act, dve)
                    dve.wait(vr_ready[j])
                    dve.done(nc.vector.tensor_reduce(st[:, 0:1], vr[:, j, :], AX_X, ALU.add))
                    dve.chain()
                    v_ts(st[:, 1:2], st[:, 0:1], -1.0 / SGU_WIDTH)
                    dve.chain()
                    m = v_ts(vr[:, j, :], vr[:, j, :], st[:, 1:2], op0=ALU.add)
                    act.wait(m)
                    a_act(c0, vr[:, j, :], ACT.Square, accum=st[:, 2:3])
                    act.chain()
                    a_act(st[:, 3:4], st[:, 2:3], ACT.Ln, bias=eps, scale=1.0 / SGU_WIDTH)
                    act.chain()
                    m = a_act(st[:, 4:5], st[:, 3:4], ACT.Exp, scale=-0.5)
                    scr.give(c0, m)
                    dve.wait(m)
                    v_stt(vr[:, j, :], vr[:, j, :], st[:, 4:5], row("sgu_ln_g"), ALU.mult, ALU.mult)
                    dve.chain()
                    m = v_tt(vr[:, j, :], vr[:, j, :], row("sgu_ln_b"), ALU.add)
                    small.give(st, m)
                    vr_ready[j] = m
                dve.wait(sgu_in)
                for g in range(4):
                    m = v_tt(sgu_w[:, g, :], sgu_w[:, g, :], con("upto"), ALU.mult)
                pe.wait(m)
                for g in range(4):
                    bank = psum.take(pe)
                    for j in range(2):
                        ins = mm(bank[:, j * P:(j + 1) * P], vr[:, j, g * P:(g + 1) * P], sgu_w[:, g, :])
                    m = pe.done(ins)
                    t = scr.take(dve)
                    dve.wait(m)
                    for j in range(2):
                        m = v_tt(t[:, j * P:(j + 1) * P], bank[:, j * P:(j + 1) * P], row("sgu_b", g * P, P), ALU.add)
                    psum.give(bank, m)
                    dve.chain()
                    mix_ready[g] = v_tt(mix[:, g, :], t[:, 0:S], u[:, g, :], ALU.mult)
                    scr.give(t, mix_ready[g])
                for c in range(8):
                    bank, m = column_sums([dqkv[:, c, :]], [d_ready[c]], S, con("ones"))
                    r, m = inv_rms(bank, m, S, 1.0)
                    dve.wait(m)
                    d_ready[c] = v_stt(dqkv[:, c, :], dqkv[:, c, :], (P ** -0.5) if c < 4 else 1.0, r[:, 0:S],
                                       ALU.mult, ALU.mult)
                    scr.give(r, d_ready[c])
                H4 = DN_HEADS * P
                GB = arena[:, 12800:12800 + H4]
                bB = arena[:, 13312:13312 + H4]
                eG = arena[:, 13824:13824 + H4]
                AT = arena[:, 14336:14336 + H4]
                QK = arena[:, 14848:14848 + H4]
                Tm = arena[:, 15360:15360 + H4]
                TT = arena[:, 15872:15872 + H4]
                Xm = arena[:, 16384:16384 + H4]
                LT = arena[:, 16896:16896 + H4]
                vb = arena[:, 17408:17408 + H4]
                kg = arena[:, 17920:17920 + H4]
                kd = arena[:, 18432:18432 + H4]
                wT = arena[:, 18944:18944 + H4]
                qd = arena[:, 19456:19456 + H4]
                vn = arena[:, 19968:19968 + H4]
                Um = arena[:, 20480:20480 + H4]
                state = arena[:, 0:H4]
                o_raw = region(512, 4, S)
                one_bc = region(1536, 1, H4)[:, 0, :]
                gcol = small.take(dve, act)
                memn_last = pe.last()
                dve.wait(memn_last)
                act.wait(memn_last)

                def h_(t, h):
                    return t[:, h * P:(h + 1) * P]

                for n in range(2):
                    tok = slice(n * P, (n + 1) * P)
                    dve.wait(pe.last(), act.last())
                    act.wait(pe.last(), dve.last())
                    for h in range(DN_HEADS):
                        v_ts(h_(one_bc, h), con("ones"), decay[:, n * 4 + h:n * 4 + h + 1])
                    m = dve.last()
                    pe.wait(m)
                    bank, bank2 = psum.take(pe), psum.take(pe)
                    for h in range(DN_HEADS):
                        mm(h_(bank, h), h_(one_bc, h), con("upto"))
                    pe.wait(beta_ready)
                    m = pe.done(mm(bank2[:, 0:4], con("upto"), decay[:, n * 4:n * 4 + 4]))
                    act.wait(m)
                    a_act(GB, bank, ACT.Copy)
                    m = a_act(eG, bank, ACT.Exp)
                    psum.give(bank, m)
                    m = a_act(gcol[:, 0:4], bank2[:, 0:4], ACT.Copy)
                    psum.give(bank2, m)
                    dve.wait(m)
                    for h in range(DN_HEADS):
                        v_ts(h_(one_bc, h), con("ones"), beta[:, n * 4 + h:n * 4 + h + 1])
                    pe.wait(dve.last())
                    bank = psum.take(pe)
                    for h in range(DN_HEADS):
                        ins = mm(h_(bank, h), h_(one_bc, h), ident)
                    m = pe.done(ins)
                    act.wait(m)
                    m = a_act(bB, bank, ACT.Copy)
                    psum.give(bank, m)
                    for h in range(DN_HEADS):
                        v_ts(h_(LT, h), h_(GB, h), gcol[:, h:h + 1], 0.0, ALU.subtract, ALU.min)
                    last_col = GB.rearrange("p (h t) -> p h t", h=DN_HEADS)[:, :, P - 1:P].rearrange("p h o -> p (h o)")
                    kdc, egc = small.take(dve, act), small.take(dve, act)
                    m = v_tt(kdc[:, 0:4], last_col, gcol[:, 0:4], ALU.subtract)
                    act.wait(m)
                    a_act(LT, LT, ACT.Exp)
                    act.chain()
                    a_act(kdc[:, 0:4], kdc[:, 0:4], ACT.Exp)
                    m = a_act(egc[:, 0:4], gcol[:, 0:4], ACT.Exp)
                    dve.wait(m)
                    for h in range(DN_HEADS):
                        v_tt(h_(LT, h), h_(LT, h), con("upto"), ALU.mult)
                    dve.chain()
                    bank, bank2 = psum.take(pe), psum.take(pe)
                    pe.wait(d_ready[11], d_ready[7])
                    for h in range(DN_HEADS):
                        mm(h_(bank, h), dqkv[:, 4 + h, tok], dqkv[:, 4 + h, tok])
                    for h in range(DN_HEADS):
                        ins = mm(h_(bank2, h), dqkv[:, 4 + h, tok], dqkv[:, h, tok])
                    m = pe.done(ins)
                    dve.wait(m)
                    v_tt(AT, bank, LT, ALU.mult)
                    m = v_tt(QK, bank2, LT, ALU.mult)
                    psum.give(bank, m)
                    psum.give(bank2, m)
                    dve.wait(act.last())
                    dve.chain()
                    v_tt(AT, AT, bB, ALU.mult)
                    for h in range(DN_HEADS):
                        v_tt(h_(qd, h), dqkv[:, h, tok], h_(eG, h), ALU.mult)
                    bank, bank2 = psum.take(pe), psum.take(pe)
                    for h in range(DN_HEADS):
                        nc.tensor.transpose(h_(bank, h), dqkv[:, 8 + h, tok], ident)
                        ins = nc.tensor.transpose(h_(bank2, h), dqkv[:, 4 + h, tok], ident)
                    m = pe.done(ins)
                    dve.wait(m)
                    for h in range(DN_HEADS):
                        bcol = beta[:, n * 4 + h:n * 4 + h + 1]
                        v_ts(h_(vb, h), h_(bank, h), bcol)
                        v_ts(h_(kg, h), h_(bank2, h), bcol, egc[:, h:h + 1], ALU.mult, ALU.mult)
                        m = v_ts(h_(kd, h), h_(bank2, h), kdc[:, h:h + 1])
                    psum.give(bank, m)
                    psum.give(bank2, m)
                    small.give(kdc, m)
                    small.give(egc, m)
                    for li, s_ in enumerate(INV_LEVELS):
                        lev = con("level", li * P, P)
                        dve.chain()
                        if s_ == 1:
                            for h in range(DN_HEADS):
                                v_tt(h_(LT, h), h_(AT, h), lev, ALU.mult)
                            dve.chain()
                            for h in range(DN_HEADS):
                                m = v_tt(h_(TT, h), ident, h_(LT, h), ALU.subtract)
                            bank = psum.take(pe)
                            pe.wait(m)
                            for h in range(DN_HEADS):
                                ins = nc.tensor.transpose(h_(bank, h), h_(TT, h), ident)
                            m = pe.done(ins)
                            act.wait(m)
                            T_ready = a_act(Tm, bank, ACT.Copy)
                            psum.give(bank, T_ready)
                            continue
                        for h in range(DN_HEADS):
                            m = v_tt(h_(LT, h), h_(AT, h), lev, ALU.mult)
                        bank = psum.take(pe)
                        pe.wait(m, T_ready)
                        for h in range(DN_HEADS):
                            ins = mm(h_(bank, h), h_(LT, h), h_(Tm, h))
                        m = pe.done(ins)
                        act.wait(m)
                        m = a_act(Xm, bank, ACT.Copy)
                        psum.give(bank, m)
                        pe.wait(m)
                        bank, bank2 = psum.take(pe), psum.take(pe)
                        for h in range(DN_HEADS):
                            mm(h_(bank, h), h_(TT, h), h_(Xm, h))
                        for h in range(DN_HEADS):
                            ins = mm(h_(bank2, h), h_(Xm, h), h_(TT, h))
                        m = pe.done(ins)
                        dve.wait(m)
                        v_stt(TT, bank2, -1.0, TT, ALU.mult, ALU.add)
                        T_ready = v_stt(Tm, bank, -1.0, Tm, ALU.mult, ALU.add)
                        psum.give(bank, T_ready)
                        psum.give(bank2, T_ready)
                    pe.wait(T_ready)
                    bank, bank2 = psum.take(pe), psum.take(pe)
                    for h in range(DN_HEADS):
                        mm(h_(bank, h), h_(TT, h), h_(vb, h))
                    for h in range(DN_HEADS):
                        ins = mm(h_(bank2, h), h_(kg, h), h_(TT, h))
                    m = pe.done(ins)
                    act.wait(m)
                    new_v = vn
                    if n == 0:
                        m = a_act(new_v, bank, ACT.Copy)
                        psum.give(bank, m)
                        psum.give(bank2, m)
                        pe.wait(m)
                    else:
                        a_act(Um, bank, ACT.Copy)
                        m = a_act(wT, bank2, ACT.Copy)
                        psum.give(bank, m)
                        psum.give(bank2, m)
                        bank = psum.take(pe)
                        pe.wait(m, state_ready)
                        for h in range(DN_HEADS):
                            ins = mm(h_(bank, h), h_(wT, h), h_(state, h))
                        m = pe.done(ins)
                        dve.wait(m, act.last())
                        m = v_stt(new_v, bank, -1.0, Um, ALU.mult, ALU.add)
                        psum.give(bank, m)
                        pe.wait(m)
                    bank = psum.take(pe)
                    for h in range(DN_HEADS):
                        if n:
                            mm(h_(bank, h), h_(state, h), h_(qd, h), start=True, stop=False)
                        ins = mm(h_(bank, h), h_(new_v, h), h_(QK, h), start=(n == 0), stop=True)
                    m = pe.done(ins)
                    act.wait(m)
                    o_ready = a_act(o_raw[:, :, tok], bank.rearrange("p (h t) -> p h t", h=DN_HEADS), ACT.Copy)
                    psum.give(bank, o_ready)
                    if n == 0:
                        bank = psum.take(pe)
                        for h in range(DN_HEADS):
                            ins = mm(h_(bank, h), h_(kd, h), h_(new_v, h))
                        m = pe.done(ins)
                        act.wait(m)
                        state_ready = a_act(state, bank, ACT.Copy)
                        psum.give(bank, state_ready)
                small.give(gcol, dve.last(), act.last())
                for h in range(DN_HEADS):
                    bank, m = column_sums([o_raw[:, h, :]], [o_ready], S, con("ones"))
                    r, m = inv_rms(bank, m, S, 1.0 / P)
                    dve.wait(m, gate_ready[-1])
                    v_stt(r[:, 0:S], o_raw[:, h, :], vec("dn_norm_g"), r[:, 0:S], ALU.mult, ALU.mult)
                    dve.chain()
                    mix_ready[4 + h] = v_tt(mix[:, 4 + h, :], r[:, 0:S], gate[:, h, :], ALU.mult)
                    scr.give(r, mix_ready[4 + h])
                w_out = io["od_w_out"]
            evac, ready = add_to_x()
            linear(w_out, KD, 0, D, lambda k: mix[:, k, :], mix_ready, S, evac)

            kT = region(6144, KD, S)
            vm = region(8192, 2, D)
            qT = region(10240, KD, S)
            oT = region(4096, KD, S)
            k_ready, vm_ready, q_ready = [], [], []
            wkv = io["xattn_wkv"][layer]
            act.wait(pe.last(), dve.last())
            linear(wkv, KD, 0, D, lambda k: memn[:, k, :], memn_ready, S, copy_to(lambda n: kT[:, n, :], k_ready))

            def evac_vm(j, n, bank, m):
                act.wait(m)
                vm_ready.append(a_act(vm[:, j, n:n + 512], bank, ACT.Copy))
                return vm_ready[-1]
            linear_rows(wkv, D, 2 * D, lambda k, j: memn[:, k, j * P:(j + 1) * P], memn_ready, 2, evac_vm)
            xn_ready = rms(hx, lambda k: vec("norm_xattn", layer * KD + k), hn, ready, S)
            linear(io["xattn_wq"][layer], KD, 0, D, hn, xn_ready, S, copy_to(lambda n: qT[:, n, :], q_ready))
            units = []
            for h in range(X_HEADS):
                for qt in range(2):
                    tok = slice(qt * P, (qt + 1) * P)
                    units.append(dict(nk=S, causal=False, ready=[q_ready[-1], k_ready[-1], vm_ready[-1]],
                                      pairs=[(qT[:, 2 * h + i, tok], kT[:, 2 * h + i, :]) for i in range(2)],
                                      outs=[(slice(0, P), (lambda t, c=2 * h + i: vm[:, t, c * P:(c + 1) * P]),
                                             oT[:, 2 * h + i, tok], i) for i in range(2)]))
            attended = Attention(units, S ** -0.5).run()
            evac, ready = add_to_x()
            linear(io["xattn_wo"][layer], KD, 0, D, lambda k: oT[:, k, :], [attended] * KD, S, evac)

            xn_ready = rms(hx, lambda k: vec("norm_ffn", layer * KD + k), hn, ready, S)
            hid = region(4096, FC, S)
            W = io["ffn_w_up"][layer]
            hid_ready = [None] * FC
            for n0 in range(0, D_FF, 512):
                nw = min(512, D_FF - n0)

                def conv_taps(c):
                    return [vec("ffn_conv", (layer * FFN_CONV + FFN_CONV - 1 - j) * 2 * FC + c)
                            for j in range(FFN_CONV)]

                def evac_gate(n, bank, m, n0=n0):
                    c = n0 // P + n
                    t = scr.take(act, dve)
                    done = causal_conv(hid[:, c, :], bank, m, conv_taps(c), S)
                    sigmoid(t[:, 0:S], hid[:, c, :], done, S)
                    dve.chain()
                    m = v_tt(hid[:, c, :], hid[:, c, :], t[:, 0:S], ALU.mult)
                    scr.give(t, m)
                    return done

                def evac_up(n, bank, m, n0=n0):
                    c = n0 // P + n
                    t = scr.take(act, dve)
                    done = causal_conv(t[:, 0:S], bank, m, conv_taps(FC + c), S)
                    dve.chain()
                    hid_ready[c] = v_tt(hid[:, c, :], hid[:, c, :], t[:, 0:S], ALU.mult)
                    scr.give(t, hid_ready[c])
                    return done
                linear(W, KD, n0, n0 + nw, hn, xn_ready, S, evac_gate)
                linear(W, KD, D_FF + n0, D_FF + n0 + nw, hn, xn_ready, S, evac_up)
            evac, ready = add_to_x()
            linear(io["ffn_w_down"][layer], FC, 0, D, lambda k: hid[:, k, :], hid_ready, S, evac)

        for _ in mod_work:
            pass
        mod_ready = dve.last()
        ctx_in = dma(x[:, :, S:T2], io["ctxT"], in_sem[3])
        ready = rms(hx, lambda k: vec("final_norm", k), hx, ready, S)

        def modulated(layer, gains, shift, scale, ready, T, extra):
            dve.wait(mod_ready)
            dve.chain()
            mA = modA[:, :].rearrange("p (k s) -> p k s", s=2)
            for s_ in range(T // S):
                m = v_stt(mA[:, :, s_], mod_v[:, layer, scale * KD:(scale + 1) * KD, s_], 1.0,
                          vec(gains, layer * KD, KD), ALU.add, ALU.mult)
            bank, m = column_sums([x[:, k, 0:T] for k in range(KD)], ready, T, con("ones"))
            r, m = inv_rms(bank, m, T, 1.0 / D)
            dve.wait(m)
            dve.chain()
            act.wait(mod_ready)
            marks = []
            for k in range(KD):
                for s_ in range(T // S):
                    c = slice(s_ * S, (s_ + 1) * S)
                    m = v_stt(xn[:, k, c], x[:, k, c], mA[:, k, s_:s_ + 1], r[:, c], ALU.mult, ALU.mult)
                last = m
                act.wait(m)
                for s_ in range(T // S):
                    c = slice(s_ * S, (s_ + 1) * S)
                    m = a_act(xn[:, k, c], xn[:, k, c], ACT.Identity, bias=mod_v[:, layer, shift * KD + k, s_:s_ + 1])
                marks.append(m)
            scr.give(r, last)
            return marks

        def gate_of(layer, which):
            return lambda n, s_: mod_v[:, layer, which * KD + n, s_:s_ + 1]

        dve.wait(ctx_in)
        act.wait(ctx_in)
        for layer in range(LAYERS2):
            last_layer = layer == LAYERS2 - 1
            TO = S if last_layer else T2
            xn_ready = modulated(layer, "g_norm_mix", 0, 1, ready, T2, None)
            if layer % 3 == 0:
                g = layer // 3
                W = io["gla_w_in"][g]
                qT, kT = region(0, 4, T2), region(2048, 4, T2)
                vr, rT = region(4096, 4, D), region(8192, KD, T2)
                qb, kb = region(12288, 4, T2), region(14336, 4, T2)
                bT, kd = region(16384, 4, T2), region(18432, 4, T2)
                state = region(20480, 4, GLA_DV)
                oT = xn
                r_ready = []
                act.wait(pe.last(), dve.last())
                linear(W, KD, 0, 512, lambda k: xn[:, k, 0:TO], xn_ready, TO,
                       copy_to(lambda n: qT[:, n, 0:TO], [], scale=GLA_DK ** -0.5))
                linear(W, KD, 512, 1024, lambda k: xn[:, k, :], xn_ready, T2, copy_to(lambda n: kT[:, n, :], []))

                def evac_v2(j, n, bank, m):
                    act.wait(m)
                    return a_act(vr[:, j, n:n + 512], bank, ACT.Copy)
                linear_rows(W, 1024, 2048, hn_tile, xn_ready, 4, evac_v2)

                def evac_r(n, bank, m):
                    t = scr.take(act, dve)
                    sigmoid(t[:, 0:TO], bank, m, TO)
                    dve.chain()
                    m = v_tt(rT[:, n, 0:TO], bank, t[:, 0:TO], ALU.mult)
                    scr.give(t, m)
                    r_ready.append(m)
                    return m
                linear(W, KD, 2048, 3072, lambda k: xn[:, k, 0:TO], xn_ready, TO, evac_r)
                qkv_ready = act.last()
                slot = wring.take(sp)
                g1 = slot[0][:, 0:2 * KD * GLA_RANK].rearrange("p (d k r) -> p d k r", d=2, k=KD)
                dma(g1[:, 0, :, :], io["gla_w_g1"][g][0], slot[1])
                g1_in = dma(g1[:, 1, :, :], io["gla_w_g1"][g][1], slot[1])
                slot2 = wring.take(sp)
                g2 = slot2[0][0:GLA_RANK, 0:2 * 512].rearrange("r (d n) -> r d n", d=2)
                g2_in = dma(g2, io["gla_w_g2"][g], slot2[1])
                low = []
                pe.wait(g1_in)
                for d in range(2):
                    bank = psum.take(pe)
                    for k in range(KD):
                        ins = mm(bank[0:GLA_RANK, :], g1[:, d, k, :], xn[:, k, :], start=(k == 0), stop=(k == KD - 1))
                    m = pe.done(ins)
                    lt = scr.take(act)
                    act.wait(m)
                    m = a_act(lt[0:GLA_RANK, :], bank[0:GLA_RANK, :], ACT.Copy)
                    psum.give(bank, m)
                    low.append((lt, m))
                wring.give(slot, pe.last())
                xn_read = pe.last()
                pe.wait(g2_in)
                for d in range(2):
                    lt, lm = low[d]
                    pe.wait(lm)
                    ebl = small_ebl = scr.take(act, dve)
                    for h in range(GLA_HEADS):
                        bank = psum.take(pe)
                        m = pe.done(mm(bank, g2[:, d, h * P:(h + 1) * P], lt[0:GLA_RANK, :]))
                        if h == GLA_HEADS - 1:
                            scr.give(lt, m)
                            if d == 1:
                                wring.give(slot2, m)
                        z, a = scr.take(act, dve), scr.take(act, dve)
                        bias = vec("gla_b_g", (g * 2 + d) * 4 + h)
                        act.wait(m)
                        a_act(z, bank, ACT.Identity, bias=bias)
                        m = a_act(a, bank, ACT.Abs, bias=bias)
                        psum.give(bank, m)
                        act.chain()
                        a_act(a, a, ACT.Exp, scale=-1.0)
                        act.chain()
                        m = a_act(a, a, ACT.Ln, bias=1.0)
                        dve.wait(m)
                        v_stt(z, z, 0.0, a, ALU.min, ALU.subtract)
                        dve.chain()
                        v_ts(z, z, 1.0 / GLA_TAU)
                        dve.chain()
                        b = bT[:, h, :]
                        bc = b.rearrange("p (c t) -> p c t", t=GLA_C)
                        m = dve.done(nc.vector.tensor_tensor_scan(b, con("restart"), z, 0.0, ALU.mult, ALU.add))
                        dve.chain()
                        eblh = ebl[:, h * 8:(h + 1) * 8]
                        tot = bc[:, :, GLA_C - 1:GLA_C]
                        totc = ebl[:, 64 + h * 8:64 + (h + 1) * 8]
                        v_ts(totc, tot.rearrange("p c o -> p (c o)"), 1.0)
                        dve.chain()
                        if d == 1:
                            v_tt(b, z, b, ALU.subtract)
                            dve.chain()
                            for c in range(8):
                                v_ts(bc[:, c, :], bc[:, c, :], totc[:, c:c + 1], op0=ALU.add)
                            dve.chain()
                        m = dve.last()
                        act.wait(m)
                        a_act(eblh, totc, ACT.Exp)
                        a_act(z, b, ACT.Exp)
                        m = a_act(a, b, ACT.Exp, scale=-1.0)
                        dve.wait(m, qkv_ready)
                        v_tt(qb[:, h, 0:TO], qT[:, h, 0:TO], z[:, 0:TO], ALU.mult)
                        v_tt(kb[:, h, :], kT[:, h, :], a, ALU.mult)
                        dve.chain()
                        for c in range(8):
                            m = v_ts(z[:, c * GLA_C:(c + 1) * GLA_C], bc[:, c, :], -1.0, totc[:, c:c + 1],
                                     ALU.mult, ALU.add)
                        act.wait(m)
                        m = a_act(z, z, ACT.Exp)
                        dve.wait(m)
                        m = v_tt(a, kT[:, h, :], z, ALU.mult)
                        scr.give(z, m)
                        bank = psum.take(pe)
                        pe.wait(m)
                        for t in range(4):
                            ins = nc.tensor.transpose(bank[:, t * P:(t + 1) * P], a[:, t * P:(t + 1) * P], ident)
                        m = pe.done(ins)
                        scr.give(a, m)
                        act.wait(m)
                        m = a_act(kd[:, h, :], bank, ACT.Copy)
                        psum.give(bank, m)
                    qb_ready = dve.last()
                    kd_ready = act.last()
                    ctx_chunks, lat_chunks = [4, 5, 6, 7], [0, 1, 2, 3]
                    order = ctx_chunks + lat_chunks if d == 0 else ctx_chunks[::-1] + lat_chunks[::-1]
                    pe.wait(qb_ready, kd_ready, qkv_ready)
                    mask = con("gla_mask", d * 256, 256)
                    state_ready = None
                    for step, c in enumerate(order):
                        part = slice(GLA_C * (c % 2), GLA_C * (c % 2) + GLA_C)
                        tile = c // 2
                        tk = slice(c * GLA_C, (c + 1) * GLA_C)
                        want = not (last_layer and c >= 4)
                        if want:
                            bank = psum.take(pe)
                            for h in range(GLA_HEADS):
                                ins = mm(bank[part, h * GLA_C:(h + 1) * GLA_C], kb[:, h, tk], qb[:, h, tk])
                            m = pe.done(ins)
                            aT = scr.take(dve)
                            dve.wait(m)
                            a_ready = v_tt(aT[part, 0:256], bank[part, 0:256], mask[part, :], ALU.mult)
                            psum.give(bank, a_ready)
                        if step < 7:
                            ub = [psum.take(pe), psum.take(pe)]
                            for h in range(GLA_HEADS):
                                ins = mm(ub[h // 2][:, (h % 2) * 256:(h % 2) * 256 + 256],
                                         kd[part, h, tile * P:(tile + 1) * P],
                                         vr[part, tile, h * GLA_DV:(h + 1) * GLA_DV])
                            u_done = pe.done(ins)
                        if want:
                            bank = psum.take(pe)
                            if state_ready:
                                pe.wait(state_ready)
                            pe.wait(a_ready)
                            for h in range(GLA_HEADS):
                                for e in range(2):
                                    out = bank[:, (2 * h + e) * GLA_C:(2 * h + e + 1) * GLA_C]
                                    if step:
                                        mm(out, state[:, h, e * P:(e + 1) * P], qb[:, h, tk], start=True, stop=False)
                                    ins = mm(out, vr[part, tile, h * GLA_DV + e * P:h * GLA_DV + (e + 1) * P],
                                             aT[part, h * GLA_C:(h + 1) * GLA_C], start=(step == 0), stop=True)
                            m = pe.done(ins)
                            scr.give(aT, m)
                            src = bank.rearrange("p (c t) -> p c t", t=GLA_C)
                            if d == 0:
                                act.wait(m, xn_read)
                                m = a_act(oT[:, :, tk], src, ACT.Copy)
                                of_ready = m
                            else:
                                dve.wait(m, of_ready)
                                m = v_tt(oT[:, :, tk], src, oT[:, :, tk], ALU.add)
                            psum.give(bank, m)
                        if step < 7:
                            dve.wait(u_done, pe.last())
                            for h in range(GLA_HEADS):
                                src = ub[h // 2][:, (h % 2) * 256:(h % 2) * 256 + 256]
                                if step == 0:
                                    m = v_ts(state[:, h, :], src, 1.0)
                                else:
                                    m = v_stt(state[:, h, :], state[:, h, :], ebl[:, h * 8 + c:h * 8 + c + 1], src,
                                              ALU.mult, ALU.add)
                            state_ready = m
                            for b_ in ub:
                                psum.give(b_, m)
                            dve.chain()
                    scr.give(ebl, dve.last())
                    act.wait(pe.last())
                    dve.wait(pe.last(), act.last())
                o_ready = dve.last()
                m_ready = []
                for h in range(GLA_HEADS):
                    bank, m = column_sums([oT[:, 2 * h, 0:TO], oT[:, 2 * h + 1, 0:TO]], [o_ready] * 2, TO, con("ones"))
                    r, m = inv_rms(bank, m, TO, 1.0 / GLA_DV)
                    dve.wait(m)
                    for e in range(2):
                        o = oT[:, 2 * h + e, 0:TO]
                        v_stt(o, o, vec("gla_g_head", g * 2 + e), r[:, 0:TO], ALU.mult, ALU.mult)
                        dve.chain()
                        m_ready.append(v_tt(o, o, rT[:, 2 * h + e, 0:TO], ALU.mult))
                    scr.give(r, dve.last())
                evac, ready = add_to_x(gate_of(layer, 2))
                linear(io["gla_w_out"][g], KD, 0, D, lambda k: oT[:, k, 0:TO], m_ready, TO, evac)
            elif layer % 3 == 1:
                u = arena[:, 0:KD * 2 * PADDED].rearrange("p (k s t) -> p k s t", k=KD, s=2)
                y = region(KD * 2 * PADDED, KD, T2)
                dve.wait(pe.last(), act.last())
                for k in range(KD):
                    dve.done(nc.vector.memset(u[:, k, :, 0:CONV_PAD], 0.0))
                    dve.done(nc.vector.memset(u[:, k, :, CONV_PAD + S:PADDED], 0.0))
                dve.chain()
                act.wait(dve.last())
                W = io["conv_w_pw1"]

                def evac_a(n, bank, m, n0):
                    act.wait(m)
                    return a_act(u[:, n0 + n, :, CONV_PAD:CONV_PAD + S], bank.rearrange("p (s t) -> p s t", s=2),
                                 ACT.Identity, bias=vec("b_pw1", n0 + n))

                u_ready = [None] * KD

                def evac_gt(n, bank, m, n0):
                    t = scr.take(act, dve)
                    act.wait(m)
                    m = a_act(t, bank, ACT.Identity, bias=vec("b_pw1", KD + n0 + n))
                    done = m
                    act.chain()
                    sigmoid(t, t, m, T2)
                    dve.chain()
                    ua = u[:, n0 + n, :, CONV_PAD:CONV_PAD + S]
                    u_ready[n0 + n] = v_tt(ua, ua, t.rearrange("p (s t) -> p s t", s=2), ALU.mult)
                    scr.give(t, u_ready[n0 + n])
                    return done
                y_ready = [None] * KD

                def depthwise(n):
                    out = y[:, n, :].rearrange("p (s t) -> p s t", s=2)
                    dve.wait(u_ready[n])
                    v_ts(out, u[:, n, :, 0:S], vec("w_dw", n), vec("b_dw", n), ALU.mult, ALU.add)
                    for j in range(1, CONV_W):
                        dve.chain()
                        m = v_stt(out, u[:, n, :, j:j + S], vec("w_dw", j * KD + n), out, ALU.mult, ALU.add)
                    y_ready[n] = m
                for n0 in range(0, KD, 4):
                    linear(W, KD, n0 * P, n0 * P + 512, lambda k: xn[:, k, :], xn_ready, T2,
                           lambda n, b, m, n0=n0: evac_a(n, b, m, n0))
                    linear(W, KD, D + n0 * P, D + n0 * P + 512, lambda k: xn[:, k, :], xn_ready, T2,
                           lambda n, b, m, n0=n0: evac_gt(n, b, m, n0))
                for n in range(KD):
                    depthwise(n)
                bank, m = column_sums([y[:, k, :] for k in range(KD)], y_ready, T2, con("ones"), square=False)
                mean = scr.take(act)
                act.wait(m)
                m = a_act(mean, bank, ACT.Copy, scale=1.0 / D)
                psum.give(bank, m)
                dve.wait(m)
                y_ready = [v_tt(y[:, k, :], y[:, k, :], mean, ALU.subtract) for k in range(KD)]
                scr.give(mean, y_ready[-1])
                bank, m = column_sums([y[:, k, :] for k in range(KD)], y_ready, T2, con("ones"))
                r, m = inv_rms(bank, m, T2, 1.0 / D)
                dve.wait(m)
                for k in range(KD):
                    yk = y[:, k, :]
                    v_stt(yk, yk, vec("ln_g", k), r, ALU.mult, ALU.mult)
                    dve.chain()
                    m = v_ts(yk, yk, vec("ln_b", k), op0=ALU.add)
                    t = scr.take(act, dve)
                    sigmoid(t, yk, m, T2)
                    dve.chain()
                    y_ready[k] = v_tt(yk, yk, t, ALU.mult)
                    scr.give(t, y_ready[k])
                scr.give(r, dve.last())
                ready = [None] * KD

                def evac_pw2(n, bank, m):
                    t = scr.take(act)
                    act.wait(m)
                    done = a_act(t, bank, ACT.Identity, bias=vec("b_pw2", n))
                    dve.wait(done)
                    for s_ in range(2):
                        c = slice(s_ * S, (s_ + 1) * S)
                        m = v_stt(x[:, n, c], t[:, c], gate_of(layer, 2)(n, s_), x[:, n, c], ALU.mult, ALU.add)
                    scr.give(t, m)
                    ready[n] = m
                    return done
                linear(io["conv_w_pw2"], KD, 0, D, lambda k: y[:, k, :], y_ready, T2, evac_pw2)
            else:
                qT, kT = region(0, KD, T2), region(4096, 4, T2)
                vr, oT = region(6144, 4, KV_HEADS * HD), region(7168, KD, T2)
                W = io["attn_w_qkv"]
                act.wait(pe.last(), dve.last())
                q_raw = []
                linear(W, KD, 0, D, lambda k: xn[:, k, :], xn_ready, T2, copy_to(lambda n: qT[:, n, :], q_raw))
                Wv = W.rearrange("(k p) n -> p k n", p=P)
                banks = [psum.take(pe) for _ in range(KV_HEADS)]
                for kb_ in range(0, KD, 4):
                    slot = wring.take(sp)
                    w = slot[0][:, :].rearrange("p (k h c d) -> p k h c d", k=4, h=KV_HEADS, c=2)
                    for h in range(KV_HEADS):
                        for c in range(2):
                            k_in = dma(w[:, :, h, c, :], Wv[:, kb_:kb_ + 4, D + h * HD:D + (h + 1) * HD], slot[1])
                    pe.wait(k_in)
                    for h in range(KV_HEADS):
                        for k in range(4):
                            ins = mm(banks[h], w[:, k, h, :, :].rearrange("p c d -> p (c d)"), xn[:, kb_ + k, :],
                                     start=(kb_ + k == 0), stop=(kb_ + k == KD - 1))
                        m = pe.done(ins)
                        if kb_ + 4 == KD:
                            act.wait(m)
                            m2 = a_act(kT[:, h, :], banks[h], ACT.Copy)
                            q_raw.append(m2)
                            psum.give(banks[h], m2)
                    wring.give(slot, m)

                def evac_v3(j, n, bank, m):
                    act.wait(m)
                    return a_act(vr[:, j, :], bank, ACT.Copy)
                linear_rows(W, D + KV_HEADS * HD, D + 2 * KV_HEADS * HD, hn_tile, xn_ready, 4, evac_v3)
                v_ready = act.last()
                for n in range(KD + KV_HEADS):
                    t_ = qT[:, n, :] if n < KD else kT[:, n - KD, :]
                    bank, m = column_sums([t_], [q_raw[n]], T2, con("head_ones"))
                    r, m = inv_rms(bank, m, T2, 1.0 / HD)
                    dve.wait(m)
                    m = v_stt(t_, t_, vec("g_q") if n < KD else vec("g_k"), r, ALU.mult, ALU.mult)
                    bank = psum.take(pe)
                    pe.wait(m)
                    m2 = pe.done(mm(bank[:, 0:S], con("rope_swap"), t_[:, 0:S]))
                    dve.wait(m2)
                    m = v_tt(r[:, 0:S], bank[:, 0:S], con("sin"), ALU.mult)
                    psum.give(bank, m)
                    v_tt(t_[:, 0:S], t_[:, 0:S], con("cos"), ALU.mult)
                    dve.chain()
                    m = v_tt(t_[:, 0:S], t_[:, 0:S], r[:, 0:S], ALU.add)
                    scr.give(r, m)
                qk_ready = dve.last()
                units = []
                for h in range(Q_HEADS):
                    part = slice(HD * (h % 2), HD * (h % 2) + HD)
                    kv = h // (Q_HEADS // KV_HEADS)
                    for qt in range(4):
                        tok = slice(qt * P, (qt + 1) * P)
                        lat = qt < 2
                        first = 0 if lat else 2
                        units.append(dict(nk=T2 if lat else S, causal=False, ready=[qk_ready, v_ready],
                                          pairs=[(qT[part, h // 2, tok], kT[part, kv, first * P:T2])],
                                          outs=[(part, (lambda t, kv=kv, first=first:
                                                        vr[:, first + t, kv * HD:(kv + 1) * HD]),
                                                 oT[part, h // 2, tok], 0)]))
                attended = Attention(units, HD ** -0.5).run()
                evac, ready = add_to_x(gate_of(layer, 2))
                linear(io["attn_w_out"], KD, 0, D, lambda k: oT[:, k, :], [attended] * KD, T2, evac)

            xn_ready = modulated(layer, "g_norm_mlp", 3, 4, ready, TO, None)
            hid = region(0, FC2, T2)
            hid_ready = []
            act.wait(pe.last())

            def evac_relu(n, bank, m):
                act.wait(m)
                m = a_act(hid[:, n, 0:TO], bank, ACT.Relu)
                dve.wait(m)
                hid_ready.append(v_tt(hid[:, n, 0:TO], hid[:, n, 0:TO], hid[:, n, 0:TO], ALU.mult))
                return m
            linear(io["w_mlp_in"][layer], KD, 0, D_FF2, lambda k: xn[:, k, 0:TO], xn_ready, TO, evac_relu)
            evac, ready = add_to_x(gate_of(layer, 5))
            linear(io["w_mlp_out"][layer], FC2, 0, D, lambda k: hid[:, k, 0:TO], hid_ready, TO, evac)

        sp.wait(ready[-1])
        out_mark = dma(io["out"], x[:, :, 0:S], out_sem)
        sp.wait(out_mark)


WEIGHTS = [("ev_w_in", "ev_w_in", 0), ("ev_w_out", "ev_w_out", 0), ("od_w_in", "od_w_in", 0),
           ("od_w_out", "od_w_out", 0), ("xattn_wq", "xattn_wq", None), ("xattn_wkv", "xattn_wkv", None),
           ("xattn_wo", "xattn_wo", None), ("ffn_w_up", "ffn_w_up", None), ("ffn_w_down", "ffn_w_down", None),
           ("w_mod", "w_mod_2", None), ("w_mlp_in", "w_mlp_in_2", None), ("w_mlp_out", "w_mlp_out_2", None),
           ("gla_w_in", "gla_w_in_2", None), ("gla_w_out", "gla_w_out_2", None), ("conv_w_pw1", "conv_w_pw1_2", 0),
           ("conv_w_pw2", "conv_w_pw2_2", 0), ("attn_w_qkv", "attn_w_qkv_2", 0), ("attn_w_out", "attn_w_out_2", 0)]


def kernel(**inputs):
    import concourse.bacc as _bacc
    from concourse.bass_utils import run_bass_kernel_spmd as _run

    a = {k: np.asarray(v) for k, v in inputs.items()}

    def cols(v):
        return np.ascontiguousarray(v.reshape(-1, P).T)

    def tokens(t):
        return np.ascontiguousarray(t[0].T.reshape(KD, P, -1).transpose(1, 0, 2))

    vec = np.zeros((P, NVEC), np.float32)

    def put(name, value):
        at, n = VEC[name]
        vec[:, at:at + n] = value
    for name in ("mem_norm", "norm_mix", "norm_xattn", "norm_ffn", "pool_scale", "final_norm", "dn_conv", "dn_norm_g",
                 "ffn_conv"):
        put(name, cols(a[name]))
    for name, src in (("g_norm_mix", "g_norm_mix_2"), ("g_norm_mlp", "g_norm_mlp_2"), ("b_mod", "b_mod_2"),
                      ("gla_b_g", "gla_b_g_2"), ("gla_g_head", "gla_g_head_2"), ("b_pw1", "conv_b_pw1_2"),
                      ("w_dw", "conv_w_dw_2"), ("b_dw", "conv_b_dw_2"), ("ln_g", "conv_ln_g_2"),
                      ("ln_b", "conv_ln_b_2"), ("b_pw2", "conv_b_pw2_2")):
        put(name, cols(a[src]))
    put("g_q", np.concatenate([a["attn_g_q_2"][0]] * 2)[:, None])
    put("g_k", np.concatenate([a["attn_g_k_2"][0]] * 2)[:, None])
    put("c", np.stack([cols(a["c_2"]), cols(a["c_ctx_2"])], axis=2).reshape(P, 2 * KD))
    row = np.broadcast_to(np.concatenate([a["sgu_ln_g"].ravel(), a["sgu_ln_b"].ravel(), a["sgu_b"].ravel(),
                                          a["dn_a_log"].ravel(), a["dn_dt_bias"].ravel()]), (P, NROW))

    arrays = {
        "con": shape_constants(), "vec": vec, "row": np.ascontiguousarray(row),
        "xT": tokens(a["x"]), "memT": tokens(a["mem"]), "ctxT": tokens(a["ctx_2"]),
        "pool_w": np.ascontiguousarray(a["pool_w"][0].transpose(1, 0, 2)),
        "sgu_wT": np.ascontiguousarray(a["sgu_w"][0].transpose(2, 0, 1)),
        "gla_w_g1": np.ascontiguousarray(a["gla_w_g1_2"].reshape(2, 2, KD, P, GLA_RANK).transpose(0, 1, 3, 2, 4)),
        "gla_w_g2": np.ascontiguousarray(a["gla_w_g2_2"].transpose(0, 2, 1, 3)),
    }
    for name, src, index in WEIGHTS:
        arrays[name] = np.ascontiguousarray(a[src] if index is None else a[src][index])
    nc = _bacc.Bacc("TRN2", target_bir_lowering=False, num_devices=1)
    io = {name: nc.dram_tensor(f"in_{name}", v.shape, F32, kind="ExternalInput").ap() for name, v in arrays.items()}
    io["out"] = nc.dram_tensor("out_xT", (P, KD, S), F32, kind="ExternalOutput").ap()
    build(nc, io)
    r = _run(nc, [{f"in_{name}": v for name, v in arrays.items()}], core_ids=[0])
    out = r.results[0]["out_xT"]
    return np.ascontiguousarray(out.transpose(1, 0, 2).reshape(D, S).T)[None]
```

```python
import numpy as np
import concourse.bass as bass
from concourse import mybir
from concourse.alu_op_type import AluOpType as ALU
from contextlib import ExitStack

F32 = mybir.dt.float32
F32R = mybir.dt.float32r
ACT = mybir.ActivationFunctionType
AX_X = mybir.AxisListType.X

P = 128
D = 1024
KD = D // P
S = 256
T2 = 2 * S
EPS = 1e-6
MOBA_HEADS, MOBA_DIM = 8, 64
A_WIDTH = MOBA_HEADS * MOBA_DIM
POOL_WINDOWS = (2, 4, 8, 16)
SGU_WIDTH = 512
DN_HEADS, DN_CONV, DN_WIDTH = 4, 4, 512
X_HEADS = 4
D_FF = 2816
FC = D_FF // P
FFN_CONV = 3
LAYERS2 = 4
D_FF2 = 4096
FC2 = D_FF2 // P
GLA_HEADS, GLA_DK, GLA_DV, GLA_RANK, GLA_TAU, GLA_C = 4, 128, 256, 16, 16.0, 64
CONV_W = 31
CONV_PAD = CONV_W // 2
PADDED = S + 2 * CONV_PAD
KV_HEADS, Q_HEADS, HD = 4, 16, 64
GRID_W = 64
NEG = -1e30


def spans(sizes):
    at, out = 0, {}
    for name, n in sizes:
        out[name] = (at, n)
        at += n
    return out, at


VEC, NVEC = spans([
    ("mem_norm", KD), ("norm_mix", 2 * KD), ("norm_xattn", 2 * KD), ("norm_ffn", 2 * KD), ("pool_scale", 4),
    ("final_norm", KD), ("dn_conv", DN_CONV * 12), ("dn_norm_g", 1), ("ffn_conv", 2 * FFN_CONV * 2 * FC),
    ("g_norm_mix", LAYERS2 * KD), ("g_norm_mlp", LAYERS2 * KD), ("b_mod", LAYERS2 * 6 * KD),
    ("gla_b_g", 2 * 2 * GLA_HEADS), ("gla_g_head", 2 * 2), ("b_pw1", 2 * KD), ("w_dw", CONV_W * KD), ("b_dw", KD),
    ("ln_g", KD), ("ln_b", KD), ("b_pw2", KD), ("g_q", 1), ("g_k", 1), ("c", 2 * KD), ("a_log", DN_HEADS), ("dt_bias", DN_HEADS)])
ROW, NROW = spans([("sgu_ln_g", SGU_WIDTH), ("sgu_ln_b", SGU_WIDTH), ("sgu_b", 4 * P)])
INV_LEVELS = (1, 2, 4, 8, 16, 32, 64)
CON, NCON = spans([("ident", P), ("ones", P), ("head_ones", P), ("causal", P), ("upto", P), ("rope_swap", P),
                   ("eps", 1), ("one", 1),
                   ("level", P * len(INV_LEVELS)), ("gla_mask", 2 * GLA_C), ("restart", T2), ("cos", S), ("sin", S),
                   ("pool_inv", 4 * S)])
NCON_KEPT = CON["level"][0]


def shape_constants():
    c = np.zeros((P, NCON), np.float32)

    def put(name, value):
        at, n = CON[name]
        c[:, at:at + n] = value

    i = np.arange(P)
    put("ident", np.eye(P))
    put("ones", 1.0)
    put("head_ones", (i[:, None] // HD) == (i[None, :] // HD))
    put("causal", np.where(i[None, :] <= i[:, None], 0.0, NEG))
    put("upto", i[:, None] <= i[None, :])
    put("rope_swap", (i[:, None] ^ 32) == i[None, :])
    levels = []
    for s in INV_LEVELS:
        same = (i[:, None] // (2 * s)) == (i[None, :] // (2 * s))
        levels.append(same & (i[:, None] % (2 * s) < s) & (i[None, :] % (2 * s) >= s))
    put("level", np.concatenate(levels, axis=1))
    j, t = i[:, None] % GLA_C, np.arange(GLA_C)[None, :]
    put("gla_mask", np.concatenate([j <= t, j >= t], axis=1))
    put("restart", (np.arange(T2) % GLA_C != 0)[None, :])
    n = HD // 4
    inv = np.float32(10000.0) ** (-np.arange(n, dtype=np.float32) / np.float32(n))
    tok = np.arange(S)
    ang = np.concatenate([(tok // GRID_W).astype(np.float32)[:, None] * inv,
                          (tok % GRID_W).astype(np.float32)[:, None] * inv], axis=1).astype(np.float32)
    put("cos", np.cos(ang).T[i % 32])
    put("sin", np.sin(ang).T[i % 32] * np.where(i % HD < 32, -1.0, 1.0)[:, None])
    put("pool_inv", np.concatenate([1.0 / np.minimum(tok + 1.0, w) for w in POOL_WINDOWS])[None, :])
    put("eps", EPS)
    put("one", 1.0)
    return c


SLAB_K, SLAB_N = 2, 512
SLAB = SLAB_K * SLAB_N
BG_K, BG_N = 4, 256


def products():
    for layer in range(2):
        if layer == 0:
            yield from ((("ev_w_in", None, 0, KD, a, b)) for a, b in ((0, 1024), (1024, 1536), (1536, 2048)))
        else:
            g0 = 2 * SGU_WIDTH + 3 * DN_WIDTH
            yield from ((("od_w_in", None, 0, KD, a, b))
                        for a, b in ((0, 512), (512, 1024), (g0 + 512, g0 + 520), (1024, g0), (g0, g0 + 512)))
        yield (("ev_w_out", "od_w_out")[layer], None, 0, KD, 0, D)
        yield ("xattn_wkv", layer, 0, KD, 0, D)
        yield ("xattn_wkv", layer, 0, KD, D, 2 * D)
        yield ("xattn_wq", layer, 0, KD, 0, D)
        yield ("xattn_wo", layer, 0, KD, 0, D)
        for n0 in range(0, D_FF, 512):
            n1 = min(n0 + 512, D_FF)
            yield ("ffn_w_up", layer, 0, KD, n0, n1)
            yield ("ffn_w_up", layer, 0, KD, D_FF + n0, D_FF + n1)
        yield ("ffn_w_down", layer, 0, FC, 0, D)
    for layer in range(LAYERS2):
        if layer % 3 == 0:
            g = layer // 3
            yield ("gla_w_in", g, 0, KD, 0, 512)
            yield ("gla_w_in", g, 0, KD, 512, 1024)
            yield ("gla_w_g1", g, 0, KD, 0, P)
            yield ("gla_w_in", g, 0, KD, 1024, 2048)
            yield ("gla_w_in", g, 0, KD, 2048, 3072)
            yield ("gla_w_out", g, 0, KD, 0, D)
        elif layer % 3 == 1:
            for n0 in range(0, D, 512):
                yield ("conv_w_pw1", None, 0, KD, n0, n0 + 512)
                yield ("conv_w_pw1", None, 0, KD, D + n0, D + n0 + 512)
            yield ("conv_w_pw2", None, 0, KD, 0, D)
        else:
            yield ("attn_w_qkv", None, 0, KD, 0, D)
            yield ("attn_w_qkv", None, 0, KD, D, D + 512)
            yield ("attn_w_qkv", None, 0, KD, D + 512, D + 768)
            yield ("attn_w_out", None, 0, KD, 0, D)
        for half in range(2):
            yield ("w_mlp_in", layer, 0, KD, half * D_FF2 // 2, (half + 1) * D_FF2 // 2)
            yield ("w_mlp_out", layer, half * FC2 // 2, (half + 1) * FC2 // 2, 0, D)


def slabs(product):
    name, index, k0, k1, n0, n1 = product
    for nb in range(n0, n1, SLAB_N):
        for kb in range(k0, k1, SLAB_K):
            yield (name, index, kb, min(kb + SLAB_K, k1), nb, min(nb + SLAB_N, n1))


class Lane:

    def __init__(self, engine, sem):
        self.engine, self.sem, self.count, self.seen = engine, sem, 0, {}

    def done(self, ins):
        ins.then_inc(self.sem, 1)
        self.count += 1
        return (self.sem, self.count)

    def last(self):
        return (self.sem, self.count)

    def wait(self, *marks):
        for mark in marks:
            sem, value = mark
            if value > self.seen.get(sem.name, 0):
                self.engine.wait_ge(sem, value)
                self.seen[sem.name] = value

    def chain(self):
        self.wait(self.last())


class Ring:

    def __init__(self, tiles):
        self.free = [(t, ()) for t in tiles]

    def take(self, *lanes):
        tile, marks = self.free.pop(0)
        for lane in lanes:
            lane.wait(*marks)
        return tile

    def give(self, tile, *marks):
        self.free.append((tile, marks))


class WeightStream:

    def __init__(self, items, raw, halves, load, split):
        self.items, self.raw, self.halves = items, raw, halves
        self.load, self.split = load, split
        self.loaded, self.in_flight, self.ready, self.used = 0, [], [], 0

    def pump(self):
        while True:
            if self.raw.free and self.loaded < len(self.items):
                slot = self.raw.take()
                self.in_flight.append((self.items[self.loaded], slot, self.load(self.items[self.loaded], *slot)))
                self.loaded += 1
            elif self.halves.free and self.in_flight:
                item, (slot, marks), landed = self.in_flight.pop(0)
                pair, pair_marks = self.halves.take()
                done = self.split(item, slot, landed, pair, pair_marks)
                self.raw.give(slot, done)
                self.ready.append((item, pair, done))
            else:
                return

    def next(self, item):
        self.pump()
        got, pair, mark = self.ready.pop(0)
        assert got == item, (got, item)
        return pair, mark

    def used_up(self, pair, mark):
        self.halves.give(pair, mark)
        self.pump()


class LateRing(Ring):

    def take(self):
        return self.free.pop(0)


def build(nc, io):
    ctx = ExitStack()
    with ctx:
        def lane(engine, name):
            return Lane(engine, ctx.enter_context(nc.semaphore(name)))

        def tile(where, name, cols, dt=F32):
            return where.enter_context(nc.sbuf_tensor(name, [P, cols], dt))[:, :]

        def tiles(where, name, k, width, dt=F32):
            return tile(where, name, k * width, dt).rearrange("p (k t) -> p k t", k=k)

        def halves(where, name, k, width):
            return tiles(where, name + "_hi", k, width, F32R), tiles(where, name + "_lo", k, width, F32R)

        pe, act, dve, pool, sp = (lane(nc.tensor, "pe_done"), lane(nc.scalar, "act_done"), lane(nc.vector, "dve_done"),
                                  lane(nc.gpsimd, "pool_done"), lane(nc.sync, "sp_unused"))
        dma_count = {}

        def dma(out, in_, sem, engine=None):
            (engine or nc.sync).dma_start(out, in_).then_inc(sem, 16)
            dma_count[sem.name] = dma_count.get(sem.name, 0) + 16
            return (sem, dma_count[sem.name])

        x = tiles(ctx, "x", KD, T2)
        xn = halves(ctx, "xn", KD, T2)
        con_t = tile(ctx, "con_t", NCON_KEPT)
        vec_t = tile(ctx, "vec_t", NVEC)
        mod_t = tile(ctx, "mod_t", LAYERS2 * 6 * KD * 2)
        modA = tile(ctx, "modA", KD * 2)
        silu_c = tile(ctx, "silu_c", KD * 2)
        small_t = tile(ctx, "small_t", 32 * 8)
        NRAW, NPAIR, NBG, NSCR = 5, 3, 2, 7
        raw_t = tile(ctx, "raw_t", SLAB * NRAW)
        whi_t = tile(ctx, "whi_t", SLAB * NPAIR, F32R)
        wlo_t = tile(ctx, "wlo_t", SLAB * NPAIR, F32R)
        bg_t = tile(ctx, "bg_t", KD * P * NBG)
        scr_t = tile(ctx, "scr_t", NSCR * T2)
        banks_t = [ctx.enter_context(nc.psum_tensor(f"bank{i}", [P, 512], F32)) for i in range(8)]
        psum = Ring([b[:, :] for b in banks_t])
        scr = Ring([scr_t[:, i * T2:(i + 1) * T2] for i in range(NSCR)])
        small = Ring([small_t[:, i * 8:(i + 1) * 8] for i in range(32)])

        def sems(name, n):
            return [ctx.enter_context(nc.semaphore(f"{name}{i}")) for i in range(n)]

        raw_in, bg_in, in_sem = sems("raw_in", NRAW), sems("bg_in", NBG), sems("in", 16)
        out_sem = ctx.enter_context(nc.semaphore("out_done"))

        def con(name, i=0, n=None):
            at, size = CON[name]
            return con_t[:, at + i:at + (size if n is None else i + n)]

        def vec(name, i=0, n=1):
            return vec_t[:, VEC[name][0] + i:VEC[name][0] + i + n]

        ident, eps, ones = con("ident"), con("eps"), con("ones")

        con_in = dma(con_t, io["con"][:, 0:NCON_KEPT], in_sem[0])
        vec_in = dma(vec_t, io["vec"], in_sem[1])
        x_in = dma(x[:, :, 0:S], io["xT"], in_sem[2])
        nc.scalar.preload_act_table_set("natural_log_exp_and_others")
        for e in (pe, act, dve, pool):
            e.wait(con_in, vec_in)

        def mm(out, lhsT, rhs, start=True, stop=True):
            return nc.tensor.matmul(out, lhsT, rhs, start=start, stop=stop)

        def v_tt(out, a, b, op):
            return dve.done(nc.vector.tensor_tensor(out, a, b, op))

        def v_ts(out, a, s1, s2=None, op0=ALU.mult, op1=None):
            if op1 is None:
                return dve.done(nc.vector.tensor_scalar(out, a, s1, None, op0))
            return dve.done(nc.vector.tensor_scalar(out, a, s1, s2, op0, op1))

        def v_stt(out, a, s, b, op0, op1):
            return dve.done(nc.vector.scalar_tensor_tensor(out=out, in0=a, scalar=s, in1=b, op0=op0, op1=op1))

        def a_act(out, in_, func, bias=0.0, scale=1.0, accum=None):
            if accum is not None:
                return act.done(nc.scalar.activation(out, in_, func, bias=bias, scale=scale, accum_out=accum))
            return act.done(nc.scalar.activation(out, in_, func, bias=bias, scale=scale))

        def fence():
            act.wait(pe.last(), dve.last(), pool.last())
            dve.wait(pe.last(), act.last(), pool.last())
            pool.wait(pe.last(), act.last(), dve.last())

        def stage_load(dst, src, sem):
            return dma(dst, src, in_sem[sem], nc.gpsimd)

        def cut_all(parts, *marks):
            act.wait(*marks)
            for hi, lo, src in parts:
                m = a_act(hi, src, ACT.Copy)
            dve.wait(m, *marks)
            for hi, lo, src in parts:
                m = v_tt(lo, src, hi.bitcast(F32), ALU.subtract)
            return m

        def cut(hi, lo, src, *marks):
            return cut_all([(hi, lo, src)], *marks)

        def slab_view(flat, item):
            _, _, k0, k1, n0, n1 = item
            return flat[:, 0:(k1 - k0) * (n1 - n0)].rearrange("p (k n) -> p k n", k=k1 - k0)

        def slab_load(item, slot, marks):
            name, index, k0, k1, n0, n1 = item
            W = io[name] if index is None else io[name][index]
            sp.wait(*marks)
            return dma(slab_view(slot[0], item), W.rearrange("(k p) n -> p k n", p=P)[:, k0:k1, n0:n1], slot[1])

        def slab_split(item, slot, landed, pair, pair_marks):
            act.wait(*pair_marks)
            dve.wait(*pair_marks)
            size = (item[3] - item[2]) * (item[5] - item[4])
            return cut(pair[0][:, 0:size], pair[1][:, 0:size], slot[0][:, 0:size], landed)

        plan = [item for product in products() for item in slabs(product)]
        stream = WeightStream(
            plan, LateRing([(raw_t[:, i * SLAB:(i + 1) * SLAB], raw_in[i]) for i in range(NRAW)]),
            LateRing([(whi_t[:, i * SLAB:(i + 1) * SLAB], wlo_t[:, i * SLAB:(i + 1) * SLAB]) for i in range(NPAIR)]),
            slab_load, slab_split)
        next_product = products()

        def three(out, w, x_, start, stop):
            mm(out, w[0], x_[0], start=start, stop=False)
            mm(out, w[0], x_[1], start=False, stop=False)
            return mm(out, w[1], x_[0], start=False, stop=stop)

        def linear_steps(name, src, ready, T, evac, rows=None):
            product = next(next_product)
            assert product[0] == name, (product, name)
            _, _, k_lo, k_hi, n_lo, n_hi = product
            for item in slabs(product):
                _, _, k0, k1, n0, n1 = item
                if k0 == k_lo:
                    banks = [psum.take(pe) for _ in range(rows or (n1 - n0) // P)]
                pair, landed = stream.next(item)
                w = [slab_view(half, item) for half in pair]
                pe.wait(landed)
                for j, bank in enumerate(banks):
                    for k in range(k0, k1):
                        i = k - k_lo
                        pe.wait(ready[i])
                        start, stop = k == k_lo, k == k_hi - 1
                        if rows:
                            tok = slice(j * P, (j + 1) * P)
                            x_hi, x_lo = src[0][:, i, tok], src[1][:, i, tok]
                            out = bank[:, 0:n1 - n0]
                            mm(out, x_hi, w[0][:, k - k0, :], start=start, stop=False)
                            mm(out, x_hi, w[1][:, k - k0, :], start=False, stop=False)
                            ins = mm(out, x_lo, w[0][:, k - k0, :], start=False, stop=stop)
                        else:
                            col = slice(j * P, (j + 1) * P)
                            ins = three(bank[:, 0:T], [half[:, k - k0, col] for half in w],
                                        [half[:, i, 0:T] for half in src], start, stop)
                    mark = pe.done(ins)
                    if k1 == k_hi:
                        if j == len(banks) - 1:
                            stream.used_up(pair, mark)
                        if rows:
                            psum.give(bank, evac(j, n0 - n_lo, bank[:, 0:n1 - n0], mark))
                        else:
                            psum.give(bank, evac((n0 - n_lo) // P + j, bank[:, 0:T], mark))
                if k1 != k_hi:
                    stream.used_up(pair, mark)
                yield

        def linear(name, src, ready, T, evac, rows=None, side=None):
            for _ in linear_steps(name, src, ready, T, evac, rows):
                if side is not None:
                    next(side, None)

        mod_v = mod_t.rearrange("p (l n s) -> p l n s", l=LAYERS2, s=2)
        bg_free = LateRing([(bg_t[:, i * KD * P:(i + 1) * KD * P], bg_in[i]) for i in range(NBG)])
        bg_todo = [(l, n) for l in range(LAYERS2) for n in range(6 * KD)]
        bg_flight = []
        bg_done = [0]

        def bg_pump():
            while bg_free.free and bg_done[0] + len(bg_flight) < len(bg_todo):
                l, n = bg_todo[bg_done[0] + len(bg_flight)]
                (slot, sem), marks = bg_free.take()
                sp.wait(*marks)
                bg_flight.append((slot, sem, dma(slot, io["w_mod"][l, n], sem)))

        def fill(steps=1):
            for _ in range(steps):
                if bg_done[0] == len(bg_todo):
                    return
                bg_pump()
                slot, sem, landed = bg_flight.pop(0)
                l, n = bg_todo[bg_done[0]]
                bg_done[0] += 1
                bank = psum.take(pe)
                pe.wait(landed, silu_ready)
                for k in range(KD):
                    ins = mm(bank[:, 0:2], slot[:, k * P:(k + 1) * P], silu_v[:, k, :], start=(k == 0),
                             stop=(k == KD - 1))
                m = pe.done(ins)
                bg_free.give((slot, sem), m)
                bg_pump()
                dve.wait(m)
                psum.give(bank, v_ts(mod_v[:, l, n, :], bank[:, 0:2], vec("b_mod", l * 6 * KD + n), op0=ALU.add))

        def finish_modulation(layer):
            fill((layer + 1) * 6 * KD - bg_done[0])

        class SumSquares:

            def __init__(self, T):
                self.T, self.acc, self.mark = T, None, None

            def add(self, src, *marks):
                sq = scr.take(act, dve)
                act.wait(*marks)
                m = a_act(sq[:, 0:self.T], src, ACT.Square)
                if self.acc is None:
                    self.acc, self.mark = sq, m
                else:
                    dve.wait(m, self.mark)
                    self.mark = v_tt(self.acc[:, 0:self.T], self.acc[:, 0:self.T], sq[:, 0:self.T], ALU.add)
                    scr.give(sq, self.mark)

            def inv_rms(self, mean_scale, group=ones):
                T = self.T
                bank = psum.take(pe)
                pe.wait(self.mark)
                m = pe.done(mm(bank[:, 0:T], group, self.acc[:, 0:T]))
                scr.give(self.acc, m)
                r = scr.take(act)
                act.wait(m)
                m = a_act(r[:, 0:T], bank[:, 0:T], ACT.Ln, bias=eps, scale=mean_scale)
                psum.give(bank, m)
                act.chain()
                return r, a_act(r[:, 0:T], r[:, 0:T], ACT.Exp, scale=-0.5)

        def squares_of(src, ready, T):
            sums = SumSquares(T)
            for k in range(KD):
                sums.add(src(k), ready[k])
            return sums

        def rms(sums, src, gain, out, T):
            r, m = sums.inv_rms(1.0 / D)
            fill(2)
            marks = []
            for k in range(KD):
                t = scr.take(dve)
                dve.wait(m)
                m2 = v_stt(t[:, 0:T], src(k), gain(k), r[:, 0:T], ALU.mult, ALU.mult)
                if k == KD - 1:
                    scr.give(r, m2)
                marks.append(cut(out[0][:, k, 0:T], out[1][:, k, 0:T], t[:, 0:T], m2))
                scr.give(t, marks[-1])
            return marks

        def sigmoid(out, src, m, scale=1.0, guard=False):
            if guard:
                dve.wait(m)
                m = v_ts(out, src, -80.0 / scale, op0=ALU.max)
                src = out
            act.wait(m)
            a_act(out, src, ACT.Exp, scale=-scale)
            act.chain()
            m = a_act(out, out, ACT.Identity, bias=con("one"))
            dve.wait(m)
            return dve.done(nc.vector.reciprocal(out, out))

        def silu_into(out, src, m, T, guard=False):
            t = scr.take(act, dve)
            sigmoid(t[:, 0:T], src, m, guard=guard)
            dve.wait(m)
            dve.chain()
            m = v_tt(out, src, t[:, 0:T], ALU.mult)
            scr.give(t, m)
            return m

        class Attention:

            def __init__(self, units, scale):
                self.units, self.scale, self.open, self.turned = units, scale, [], []

            def scores(self, u):
                bank = psum.take(pe)
                nk = u["nk"]
                pe.wait(*u["ready"])
                for i, (q, k) in enumerate(u["pairs"]):
                    ins = mm(bank[:, 0:nk], q, k, start=(i == 0), stop=(i == len(u["pairs"]) - 1))
                m = pe.done(ins)
                probs = scr.take(dve, act)
                stats = small.take(dve, act)
                src = bank[:, 0:nk]
                dve.wait(m)
                if u["causal"]:
                    if nk > P:
                        v_ts(probs[:, 0:nk - P], bank[:, 0:nk - P], 1.0)
                    m = v_tt(probs[:, nk - P:nk], bank[:, nk - P:nk], con("causal"), ALU.add)
                    psum.give(bank, m)
                    dve.chain()
                    src = probs[:, 0:nk]
                dve.done(nc.vector.tensor_reduce(stats[:, 0:1], src, AX_X, ALU.max))
                dve.chain()
                m = v_ts(stats[:, 1:2], stats[:, 0:1], -self.scale)
                act.wait(m)
                m = a_act(probs[:, 0:nk], src, ACT.Exp, bias=stats[:, 1:2], scale=self.scale, accum=stats[:, 2:3])
                if not u["causal"]:
                    psum.give(bank, m)
                dve.wait(m)
                dve.done(nc.vector.reciprocal(stats[:, 3:4], stats[:, 2:3]))
                dve.chain()
                m = v_ts(probs[:, 0:nk], probs[:, 0:nk], stats[:, 3:4])
                small.give(stats, m)
                self.open.append((u, probs, m))

            def turn(self):
                u, probs, m = self.open.pop(0)
                nk = u["nk"]
                bank = psum.take(pe)
                pe.wait(m)
                for t in range(nk // P):
                    ins = nc.tensor.transpose(bank[:, t * P:(t + 1) * P], probs[:, t * P:(t + 1) * P], ident)
                m = pe.done(ins)
                scr.give(probs, m)
                turned = scr.take(act)
                act.wait(m)
                m = a_act(turned[:, 0:nk], bank[:, 0:nk], ACT.Copy)
                psum.give(bank, m)
                self.turned.append((u, turned, m))

            def finish(self):
                u, turned, m = self.turned.pop(0)
                nk = u["nk"]
                out = psum.take(pe)
                pe.wait(m)
                for o_rows, values, dst, part in u["outs"]:
                    for t in range(nk // P):
                        ins = mm(out[o_rows, part * P:(part + 1) * P], values(t), turned[:, t * P:(t + 1) * P],
                                 start=(t == 0), stop=(t == nk // P - 1))
                m = pe.done(ins)
                scr.give(turned, m)
                m2 = cut_all([(dst[0], dst[1], out[o_rows, part * P:(part + 1) * P])
                              for o_rows, _, dst, part in u["outs"]], m)
                psum.give(out, m2)

            def run(self, lag=3, extra=0):
                for i in range(len(self.units) + lag + 1):
                    if i < len(self.units):
                        self.scores(self.units[i])
                    if lag <= i < len(self.units) + lag:
                        self.turn()
                    if i > lag:
                        self.finish()
                    if i < len(self.units) or i > len(self.units):
                        fill(extra)
                return dve.last()

        def add_to_x(sums, gate=None, bias=None):
            def evac(n, bank, m):
                T = bank.shape[-1]
                src, freed = bank, None
                if bias is not None:
                    t = scr.take(act)
                    act.wait(m)
                    m = freed = a_act(t[:, 0:T], bank, ACT.Identity, bias=bias(n))
                    src = t
                dve.wait(m)
                if gate is None:
                    m = v_tt(x[:, n, 0:T], src[:, 0:T], x[:, n, 0:T], ALU.add)
                else:
                    for s0 in range(0, T, S):
                        m = v_stt(x[:, n, s0:s0 + S], src[:, s0:s0 + S], gate(n, s0 // S), x[:, n, s0:s0 + S],
                                  ALU.mult, ALU.add)
                if bias is not None:
                    scr.give(t, m)
                if sums is not None:
                    sums.add(x[:, n, 0:sums.T], m)
                return freed or m
            return evac

        def copy_to(dst, marks=None, scale=1.0):
            def evac(n, bank, m):
                act.wait(m)
                m = a_act(dst(n), bank, ACT.Copy, scale=scale)
                if marks is not None:
                    marks.append(m)
                return m
            return evac

        def rows_to(dst):
            def evac(j, n, bank, m):
                act.wait(m)
                return a_act(dst[:, j, n:n + bank.shape[-1]], bank, ACT.Copy)
            return evac

        def causal_conv(out, bank, m, taps, T):
            dve.wait(m)
            m = v_ts(out, bank, taps[0])
            for j in range(1, len(taps)):
                dve.chain()
                m = v_stt(out[:, j:T], bank[:, 0:T - j], taps[j], out[:, j:T], ALU.mult, ALU.add)
            return m

        def hx(k):
            return x[:, k, 0:S]

        stream.pump()
        silu_v = silu_c.rearrange("p (k s) -> p k s", s=2)
        silu_ready = silu_into(silu_c, vec("c", 0, 2 * KD), vec_in, 2 * KD)

        first = ExitStack()
        memn = halves(first, "memn", KD, S)
        with ExitStack() as st:
            mem_t = tiles(st, "mem_t", KD, S)
            mem_in = dma(mem_t, io["memT"], in_sem[5])
            sums = squares_of(hx, [x_in] * KD, S)
            mem_sums = squares_of(lambda k: mem_t[:, k, :], [mem_in] * KD, S)
            xn_ready = rms(sums, hx, lambda k: vec("norm_mix", k), xn, S)
            memn_ready = rms(mem_sums, lambda k: mem_t[:, k, :], lambda k: vec("mem_norm", k), memn, S)

        for layer in range(2):
            st = ExitStack()
            mix = halves(st, f"mix{layer}", KD, S)
            mix_ready = [None] * KD
            if layer == 0:
                qk = tiles(st, "qk", KD, S)
                v = tiles(st, "v", 2, A_WIDTH)
                p = tiles(st, "p", 4, S)
                pool_w = tiles(st, "pool_w", 4, P)
                pool_inv = tile(st, "pool_inv", 4 * S)
                fence()
                pool_w_in = stage_load(pool_w, io["pool_w"], 6)
                at, n = CON["pool_inv"]
                pool_inv_in = stage_load(pool_inv, io["con"][:, at:at + n], 7)
                linear("ev_w_in", xn, xn_ready, S, copy_to(lambda n: qk[:, n, :]))
                linear("ev_w_in", xn, xn_ready, S, rows_to(v), rows=2)
                qkv_ready = act.last()
                linear("ev_w_in", xn, xn_ready, S, copy_to(lambda n: p[:, n, :]))
                p_ready = act.last()
                units = []
                for h in range(MOBA_HEADS):
                    part = slice(HD * (h % 2), HD * (h % 2) + HD)
                    for qt in range(2):
                        tok = slice(qt * P, (qt + 1) * P)
                        units.append(dict(nk=(qt + 1) * P, causal=True, ready=[qkv_ready],
                                          pairs=[(qk[part, h // 2, tok], qk[part, 4 + h // 2, 0:(qt + 1) * P])],
                                          outs=[(part, (lambda t, h=h: v[:, t, h * HD:(h + 1) * HD]),
                                                 [half[part, h // 2, tok] for half in mix], 0)]))
                attended = Attention(units, HD ** -0.5).run(extra=1)
                for n in range(4):
                    mix_ready[n] = attended
                dve.wait(p_ready, pool_inv_in)
                pooled = []
                for g, w in enumerate(POOL_WINDOWS):
                    a, b = scr.take(dve), scr.take(dve)
                    src = p[:, g, :]
                    step = 1
                    while step < w:
                        v_ts(b[:, 0:step], src[:, 0:step], 1.0)
                        v_tt(b[:, step:S], src[:, step:S], src[:, 0:S - step], ALU.add)
                        dve.chain()
                        src, a, b = b[:, 0:S], b, a
                        step *= 2
                    v_tt(b[:, 0:S], src, pool_inv[:, g * S:(g + 1) * S], ALU.mult)
                    dve.chain()
                    m = v_tt(b[:, 0:S], b[:, 0:S], p[:, g, :], ALU.subtract)
                    scr.give(a, m)
                    pooled.append((b, m))
                fill(3)
                for g, (b, m) in enumerate(pooled):
                    bank = psum.take(pe)
                    pe.wait(m, pool_w_in)
                    m = pe.done(mm(bank[:, 0:S], pool_w[:, g, :], b[:, 0:S]))
                    dve.wait(m)
                    m = v_ts(b[:, 0:S], bank[:, 0:S], vec("pool_scale", g))
                    psum.give(bank, m)
                    mix_ready[4 + g] = cut(mix[0][:, 4 + g, :], mix[1][:, 4 + g, :], b[:, 0:S], m)
                    scr.give(b, mix_ready[4 + g])
            else:
                sgu = ExitStack()
                ab = tile(st, "ab", 16)
                beta, decay = tile(st, "beta", 8), tile(st, "decay", 8)
                u = tiles(sgu, "u", 4, S)
                vr = tiles(sgu, "vr", 2, SGU_WIDTH)
                sgu_w = tiles(sgu, "sgu_w", 4, P)
                sgu_row = tile(sgu, "sgu_row", NROW)
                fence()
                sgu_in = stage_load(sgu_w, io["sgu_wT"], 8)
                row_in = stage_load(sgu_row, io["row"], 9)

                def row(name, i=0, n=None):
                    at, size = ROW[name]
                    return sgu_row[:, at + i:at + (size if n is None else i + n)]

                def gelu(out, bank, m, T):
                    raw, t = scr.take(act), scr.take(act, dve)
                    act.wait(m)
                    done = a_act(raw[:, 0:T], bank, ACT.Copy)
                    act.chain()
                    m = a_act(t[:, 0:T], raw[:, 0:T], ACT.Square)
                    dve.wait(m)
                    v_ts(t[:, 0:T], t[:, 0:T], 0.044715, 1.0, ALU.mult, ALU.add)
                    dve.chain()
                    m = v_tt(t[:, 0:T], t[:, 0:T], raw[:, 0:T], ALU.mult)
                    sigmoid(t[:, 0:T], t[:, 0:T], m, scale=2.0 * float(np.sqrt(2.0 / np.pi)))
                    dve.chain()
                    m = v_tt(out, t[:, 0:T], raw[:, 0:T], ALU.mult)
                    scr.give(raw, m)
                    scr.give(t, m)
                    return done, m

                u_ready, vr_ready = [], []

                def evac_u(n, bank, m):
                    done, m = gelu(u[:, n, :], bank, m, S)
                    u_ready.append(m)
                    return done

                def evac_vr(j, n, bank, m):
                    done, m = gelu(vr[:, j, n:n + 512], bank, m, 512)
                    vr_ready.append(m)
                    return done
                linear("od_w_in", xn, xn_ready, S, evac_u)
                linear("od_w_in", xn, xn_ready, S, evac_vr, rows=2)

                def evac_ab(j, n, bank, m):
                    act.wait(m)
                    return a_act(ab[:, j * 8:(j + 1) * 8], bank, ACT.Copy)
                linear("od_w_in", xn, xn_ready, S, evac_ab, rows=2)

                def small_steps():
                    neg_a, tmp, tmp2 = (small.take(act, dve) for _ in range(3))
                    a_act(neg_a[:, 0:4], vec("a_log", 0, DN_HEADS), ACT.Exp)
                    for j in range(2):
                        braw, araw = ab[:, j * 8:j * 8 + 4], ab[:, j * 8 + 4:j * 8 + 8]
                        bj, gj = beta[:, j * 4:j * 4 + 4], decay[:, j * 4:j * 4 + 4]
                        sigmoid(bj, braw, act.last())
                        dve.wait(act.last())
                        v_tt(gj, araw, vec("dt_bias", 0, DN_HEADS), ALU.add)
                        act.wait(dve.last())
                        act.chain()
                        a_act(tmp[:, 0:4], gj, ACT.Abs)
                        act.chain()
                        a_act(tmp[:, 0:4], tmp[:, 0:4], ACT.Exp, scale=-1.0)
                        act.chain()
                        m = a_act(tmp2[:, 0:4], tmp[:, 0:4], ACT.Ln, bias=con("one"))
                        dve.wait(m)
                        dve.chain()
                        v_stt(gj, gj, 0.0, tmp2[:, 0:4], ALU.max, ALU.add)
                        dve.chain()
                        m = v_stt(gj, gj, -1.0, neg_a[:, 0:4], ALU.mult, ALU.mult)
                        act.wait(m)
                        yield
                    for s_ in (neg_a, tmp, tmp2):
                        small.give(s_, m)
                    for j in range(2):
                        s_ = small.take(dve, act)
                        c0 = scr.take(act, dve)
                        dve.wait(vr_ready[j], row_in)
                        dve.done(nc.vector.tensor_reduce(s_[:, 0:1], vr[:, j, :], AX_X, ALU.add))
                        dve.chain()
                        v_ts(s_[:, 1:2], s_[:, 0:1], -1.0 / SGU_WIDTH)
                        dve.chain()
                        m = v_ts(vr[:, j, :], vr[:, j, :], s_[:, 1:2], op0=ALU.add)
                        act.wait(m)
                        a_act(c0, vr[:, j, :], ACT.Square, accum=s_[:, 2:3])
                        act.chain()
                        a_act(s_[:, 3:4], s_[:, 2:3], ACT.Ln, bias=eps, scale=1.0 / SGU_WIDTH)
                        act.chain()
                        m = a_act(s_[:, 4:5], s_[:, 3:4], ACT.Exp, scale=-0.5)
                        scr.give(c0, m)
                        yield
                        dve.wait(m)
                        v_stt(vr[:, j, :], vr[:, j, :], s_[:, 4:5], row("sgu_ln_g"), ALU.mult, ALU.mult)
                        dve.chain()
                        m = v_tt(vr[:, j, :], vr[:, j, :], row("sgu_ln_b"), ALU.add)
                        small.give(s_, m)
                        vr_ready[j] = m
                    dve.wait(sgu_in)
                    m = v_tt(sgu_w, sgu_w, con("upto").unsqueeze(1).to_broadcast([P, 4, P]), ALU.mult)
                    yield
                    pe.wait(m)
                    for g in range(4):
                        bank = psum.take(pe)
                        for j in range(2):
                            ins = mm(bank[:, j * P:(j + 1) * P], vr[:, j, g * P:(g + 1) * P], sgu_w[:, g, :])
                        m = pe.done(ins)
                        t = scr.take(dve)
                        dve.wait(m)
                        for j in range(2):
                            m = v_tt(t[:, j * P:(j + 1) * P], bank[:, j * P:(j + 1) * P], row("sgu_b", g * P, P),
                                     ALU.add)
                        psum.give(bank, m)
                        dve.chain()
                        m = v_tt(t[:, 0:S], t[:, 0:S], u[:, g, :], ALU.mult)
                        mix_ready[g] = cut(mix[0][:, g, :], mix[1][:, g, :], t[:, 0:S], m)
                        scr.give(t, mix_ready[g])
                        yield
                for _ in small_steps():
                    fill(1)
                beta_ready = act.last()
                sgu.close()

                dqkv = tiles(st, "dqkv", 12, S)
                gate = tiles(st, "gate", 4, S)
                fence()
                d_ready = [None] * 12

                def evac_d_later():
                    waiting = []

                    def evac(n, bank, m):
                        done = causal_conv(dqkv[:, n, :], bank, m, [vec("dn_conv", (DN_CONV - 1 - j) * 12 + n)
                                                                   for j in range(DN_CONV)], S)
                        d_ready[n] = silu_into(dqkv[:, n, :], dqkv[:, n, :], done, S)
                        if n < 8:
                            waiting.append(n)
                        return done

                    def side():
                        while True:
                            if waiting:
                                n = waiting.pop(0)
                                sums = SumSquares(S)
                                sums.add(dqkv[:, n, :], d_ready[n])
                                yield
                                r, m = sums.inv_rms(1.0)
                                dve.wait(m)
                                d_ready[n] = v_stt(dqkv[:, n, :], dqkv[:, n, :], (P ** -0.5) if n < 4 else 1.0,
                                                   r[:, 0:S], ALU.mult, ALU.mult)
                                scr.give(r, d_ready[n])
                            elif all(d_ready):
                                return
                            yield
                    return evac, side()
                evac, side = evac_d_later()
                linear("od_w_in", xn, xn_ready, S, evac, side=side)
                linear("od_w_in", xn, xn_ready, S,
                       lambda n, bank, m: silu_into(gate[:, n, :], bank, m, S), side=side)
                for _ in side:
                    pass
                gate_ready = dve.last()

                H4 = DN_HEADS * P
                delta = ExitStack()
                (eG, bB, AT, QK, Tm, TT, Xm, LT, vb, kg, kd, qd, state, spread) = (
                    tile(delta, name, H4) for name in ("eG", "bB", "AT", "QK", "Tm", "TT", "Xm", "LT", "vb", "kg", "kd",
                                                       "qd", "state", "spread"))
                o_raw = tiles(delta, "o_raw", 4, S)
                level = tile(delta, "level", P * len(INV_LEVELS))
                gcol = small.take(dve, act)
                fence()
                at, n = CON["level"]
                level_in = stage_load(level, io["con"][:, at:at + n], 10)

                def h_(t, h):
                    return t[:, h * P:(h + 1) * P]

                def by_head(t):
                    return t.rearrange("p (h t) -> p h t", h=DN_HEADS)

                def all_heads(t):
                    return t.unsqueeze(1).to_broadcast([P, DN_HEADS, P])

                def spread_columns(src):
                    for h in range(DN_HEADS):
                        m = v_ts(h_(spread, h), ones, src[:, h:h + 1])
                    return m

                for n in range(2):
                    tok = slice(n * P, (n + 1) * P)
                    if n:
                        fence()
                    dve.wait(beta_ready)
                    m = spread_columns(decay[:, n * 4:n * 4 + 4])
                    pe.wait(m)
                    bank, bank2 = psum.take(pe), psum.take(pe)
                    for h in range(DN_HEADS):
                        mm(h_(bank, h), h_(spread, h), con("upto"))
                    m = pe.done(mm(bank2[:, 0:4], con("upto"), decay[:, n * 4:n * 4 + 4]))
                    fill(1)
                    act.wait(m)
                    m = a_act(gcol[:, 0:4], bank2[:, 0:4], ACT.Copy)
                    psum.give(bank2, m)
                    m2 = a_act(eG, bank, ACT.Exp)
                    dve.wait(m, m2)
                    for h in range(DN_HEADS):
                        v_ts(h_(LT, h), h_(bank, h), gcol[:, h:h + 1], 0.0, ALU.subtract, ALU.min)
                    last_col = by_head(bank)[:, :, P - 1:P].rearrange("p h o -> p (h o)")
                    kdc, egc = small.take(dve, act), small.take(dve, act)
                    m = v_tt(kdc[:, 0:4], last_col, gcol[:, 0:4], ALU.subtract)
                    psum.give(bank, m)
                    act.wait(m)
                    a_act(LT, LT, ACT.Exp)
                    act.chain()
                    a_act(kdc[:, 0:4], kdc[:, 0:4], ACT.Exp)
                    m3 = a_act(egc[:, 0:4], gcol[:, 0:4], ACT.Exp)
                    dve.wait(m)
                    m = spread_columns(beta[:, n * 4:n * 4 + 4])
                    pe.wait(m)
                    bank = psum.take(pe)
                    for h in range(DN_HEADS):
                        ins = mm(h_(bank, h), h_(spread, h), ident)
                    m = pe.done(ins)
                    act.wait(m)
                    m = a_act(bB, bank, ACT.Copy)
                    psum.give(bank, m)
                    dve.wait(m3, m)
                    v_tt(by_head(LT), by_head(LT), all_heads(con("upto")), ALU.mult)
                    bank, bank2 = psum.take(pe), psum.take(pe)
                    pe.wait(*d_ready)
                    for h in range(DN_HEADS):
                        mm(h_(bank, h), dqkv[:, 4 + h, tok], dqkv[:, 4 + h, tok])
                    for h in range(DN_HEADS):
                        ins = mm(h_(bank2, h), dqkv[:, 4 + h, tok], dqkv[:, h, tok])
                    m = pe.done(ins)
                    dve.wait(m)
                    dve.chain()
                    v_tt(AT, bank, LT, ALU.mult)
                    m = v_tt(QK, bank2, LT, ALU.mult)
                    psum.give(bank, m)
                    psum.give(bank2, m)
                    dve.chain()
                    v_tt(AT, AT, bB, ALU.mult)
                    v_tt(by_head(qd), dqkv[:, 0:4, tok], by_head(eG), ALU.mult)
                    bank, bank2 = psum.take(pe), psum.take(pe)
                    for h in range(DN_HEADS):
                        nc.tensor.transpose(h_(bank, h), dqkv[:, 8 + h, tok], ident)
                        ins = nc.tensor.transpose(h_(bank2, h), dqkv[:, 4 + h, tok], ident)
                    m = pe.done(ins)
                    dve.wait(m)
                    for h in range(DN_HEADS):
                        bcol = beta[:, n * 4 + h:n * 4 + h + 1]
                        v_ts(h_(vb, h), h_(bank, h), bcol)
                        v_ts(h_(kg, h), h_(bank2, h), bcol, egc[:, h:h + 1], ALU.mult, ALU.mult)
                        m = v_ts(h_(kd, h), h_(bank2, h), kdc[:, h:h + 1])
                    psum.give(bank, m)
                    psum.give(bank2, m)
                    small.give(kdc, m)
                    small.give(egc, m)
                    dve.wait(level_in)
                    for li, s_ in enumerate(INV_LEVELS):
                        lev = all_heads(level[:, li * P:(li + 1) * P])
                        dve.chain()
                        m = v_tt(by_head(LT), by_head(AT), lev, ALU.mult)
                        if s_ == 1:
                            dve.chain()
                            m = v_tt(by_head(TT), all_heads(ident), by_head(LT), ALU.subtract)
                            bank = psum.take(pe)
                            pe.wait(m)
                            for h in range(DN_HEADS):
                                ins = nc.tensor.transpose(h_(bank, h), h_(TT, h), ident)
                            m = pe.done(ins)
                            act.wait(m)
                            T_ready = a_act(Tm, bank, ACT.Copy)
                            psum.give(bank, T_ready)
                            continue
                        bank = psum.take(pe)
                        pe.wait(m, T_ready)
                        for h in range(DN_HEADS):
                            ins = mm(h_(bank, h), h_(LT, h), h_(Tm, h))
                        m = pe.done(ins)
                        act.wait(m)
                        m = a_act(Xm, bank, ACT.Copy)
                        psum.give(bank, m)
                        fill(1)
                        pe.wait(m)
                        bank, bank2 = psum.take(pe), psum.take(pe)
                        for h in range(DN_HEADS):
                            mm(h_(bank, h), h_(TT, h), h_(Xm, h))
                        for h in range(DN_HEADS):
                            ins = mm(h_(bank2, h), h_(Xm, h), h_(TT, h))
                        m = pe.done(ins)
                        fill(1)
                        dve.wait(m)
                        v_stt(TT, bank2, -1.0, TT, ALU.mult, ALU.add)
                        T_ready = v_stt(Tm, bank, -1.0, Tm, ALU.mult, ALU.add)
                        psum.give(bank, T_ready)
                        psum.give(bank2, T_ready)
                    pe.wait(T_ready)
                    bank, bank2 = psum.take(pe), psum.take(pe)
                    for h in range(DN_HEADS):
                        mm(h_(bank, h), h_(TT, h), h_(vb, h))
                    for h in range(DN_HEADS):
                        ins = mm(h_(bank2, h), h_(kg, h), h_(TT, h))
                    m = pe.done(ins)
                    new_v = scr.take(act, dve)
                    act.wait(m)
                    if n == 0:
                        m = a_act(new_v, bank, ACT.Copy)
                        psum.give(bank, m)
                        psum.give(bank2, m)
                        pe.wait(m)
                    else:
                        Um, wT = scr.take(act), scr.take(act)
                        a_act(Um, bank, ACT.Copy)
                        m = a_act(wT, bank2, ACT.Copy)
                        psum.give(bank, m)
                        psum.give(bank2, m)
                        bank = psum.take(pe)
                        pe.wait(m, state_ready)
                        for h in range(DN_HEADS):
                            ins = mm(h_(bank, h), h_(wT, h), h_(state, h))
                        m = pe.done(ins)
                        scr.give(wT, m)
                        dve.wait(m, act.last())
                        m = v_stt(new_v, bank, -1.0, Um, ALU.mult, ALU.add)
                        scr.give(Um, m)
                        psum.give(bank, m)
                        pe.wait(m)
                    bank = psum.take(pe)
                    for h in range(DN_HEADS):
                        if n:
                            mm(h_(bank, h), h_(state, h), h_(qd, h), start=True, stop=False)
                        ins = mm(h_(bank, h), h_(new_v, h), h_(QK, h), start=(n == 0), stop=True)
                    m = pe.done(ins)
                    act.wait(m)
                    o_ready = a_act(o_raw[:, :, tok], by_head(bank), ACT.Copy)
                    psum.give(bank, o_ready)
                    if n == 0:
                        bank = psum.take(pe)
                        for h in range(DN_HEADS):
                            ins = mm(h_(bank, h), h_(kd, h), h_(new_v, h))
                        m = pe.done(ins)
                        act.wait(m)
                        state_ready = a_act(state, bank, ACT.Copy)
                        psum.give(bank, state_ready)
                    scr.give(new_v, m)
                small.give(gcol, dve.last(), act.last())
                normed = []
                for h in range(DN_HEADS):
                    sums = SumSquares(S)
                    sums.add(o_raw[:, h, :], o_ready)
                    normed.append(sums)
                normed = [sums.inv_rms(1.0 / P) for sums in normed]
                fill(2)
                for h, (r, m) in enumerate(normed):
                    dve.wait(m, gate_ready)
                    v_stt(r[:, 0:S], o_raw[:, h, :], vec("dn_norm_g"), r[:, 0:S], ALU.mult, ALU.mult)
                    dve.chain()
                    m = v_tt(r[:, 0:S], r[:, 0:S], gate[:, h, :], ALU.mult)
                    mix_ready[4 + h] = cut(mix[0][:, 4 + h, :], mix[1][:, 4 + h, :], r[:, 0:S], m)
                    scr.give(r, mix_ready[4 + h])
                delta.close()
            sums = SumSquares(S)
            linear(("ev_w_out", "od_w_out")[layer], mix, mix_ready, S, add_to_x(sums))
            st.close()

            st = ExitStack()
            oT = halves(st, f"oT{layer}", KD, S)
            kT, qT = tiles(st, f"kT{layer}", KD, S), tiles(st, f"qT{layer}", KD, S)
            vm = tiles(st, f"vm{layer}", 2, D)
            fence()
            linear("xattn_wkv", memn, memn_ready, S, copy_to(lambda n: kT[:, n, :]))
            xn_ready = rms(sums, hx, lambda k: vec("norm_xattn", layer * KD + k), xn, S)
            linear("xattn_wkv", memn, memn_ready, S, rows_to(vm), rows=2)
            linear("xattn_wq", xn, xn_ready, S, copy_to(lambda n: qT[:, n, :]))
            qkv_ready = act.last()
            units = []
            for h in range(X_HEADS):
                for qt in range(2):
                    tok = slice(qt * P, (qt + 1) * P)
                    units.append(dict(nk=S, causal=False, ready=[qkv_ready],
                                      pairs=[(qT[:, 2 * h + i, tok], kT[:, 2 * h + i, :]) for i in range(2)],
                                      outs=[(slice(0, P), (lambda t, c=2 * h + i: vm[:, t, c * P:(c + 1) * P]),
                                             [half[:, 2 * h + i, tok] for half in oT], i) for i in range(2)]))
            attended = Attention(units, S ** -0.5).run(extra=1)
            sums = SumSquares(S)
            linear("xattn_wo", oT, [attended] * KD, S, add_to_x(sums))
            st.close()

            xn_ready = rms(sums, hx, lambda k: vec("norm_ffn", layer * KD + k), xn, S)
            st = ExitStack()
            hid = halves(st, f"hid{layer}", FC, S)
            gated = tiles(st, f"gated{layer}", 4, S)
            fence()
            hid_ready = [None] * FC

            def conv_taps(c):
                return [vec("ffn_conv", (layer * FFN_CONV + FFN_CONV - 1 - j) * 2 * FC + c) for j in range(FFN_CONV)]

            for n0 in range(0, FC, 4):
                def evac_gate(n, bank, m, n0=n0):
                    done = causal_conv(gated[:, n, :], bank, m, conv_taps(n0 + n), S)
                    silu_into(gated[:, n, :], gated[:, n, :], done, S)
                    return done

                def evac_up(n, bank, m, n0=n0):
                    c = n0 + n
                    t = scr.take(act, dve)
                    done = causal_conv(t[:, 0:S], bank, m, conv_taps(FC + c), S)
                    dve.chain()
                    m = v_tt(t[:, 0:S], gated[:, n, :], t[:, 0:S], ALU.mult)
                    hid_ready[c] = cut(hid[0][:, c, :], hid[1][:, c, :], t[:, 0:S], m)
                    scr.give(t, hid_ready[c])
                    return done
                linear("ffn_w_up", xn, xn_ready, S, evac_gate)
                linear("ffn_w_up", xn, xn_ready, S, evac_up)
            sums = SumSquares(S)
            linear("ffn_w_down", hid, hid_ready, S, add_to_x(sums))
            st.close()
            if layer == 0:
                xn_ready = rms(sums, hx, lambda k: vec("norm_mix", KD + k), xn, S)
        first.close()

        sp.wait(dve.last())
        ctx_in = dma(x[:, :, S:T2], io["ctxT"], in_sem[3])
        r, m = sums.inv_rms(1.0 / D)
        fill(2)
        dve.wait(m)
        sums = SumSquares(T2)
        for k in range(KD):
            m = v_stt(hx(k), hx(k), vec("final_norm", k), r[:, 0:S], ALU.mult, ALU.mult)
            if k == KD - 1:
                scr.give(r, m)
            sums.add(x[:, k, :], m, ctx_in)

        def modulated(sums, layer, gains, shift, scale, T):
            r, m = sums.inv_rms(1.0 / D)
            finish_modulation(layer)
            fill(2)
            mA = modA.rearrange("p (k s) -> p k s", s=2)
            dve.chain()
            for s_ in range(T // S):
                v_stt(mA[:, :, s_], mod_v[:, layer, scale * KD:(scale + 1) * KD, s_], 1.0,
                      vec(gains, layer * KD, KD), ALU.add, ALU.mult)
            dve.wait(m)
            dve.chain()
            marks = []
            for k in range(KD):
                t = scr.take(dve)
                streams = [slice(s_ * S, (s_ + 1) * S) for s_ in range(T // S)]
                for s_, c in enumerate(streams):
                    m = v_stt(t[:, c], x[:, k, c], mA[:, k, s_:s_ + 1], r[:, c], ALU.mult, ALU.mult)
                if k == KD - 1:
                    scr.give(r, m)
                act.wait(m)
                for s_, c in enumerate(streams):
                    add = mod_v[:, layer, shift * KD + k, s_:s_ + 1]
                    m = a_act(xn[0][:, k, c], t[:, c], ACT.Identity, bias=add)
                dve.wait(m)
                for s_, c in enumerate(streams):
                    add = mod_v[:, layer, shift * KD + k, s_:s_ + 1]
                    m = v_stt(xn[1][:, k, c], t[:, c], add, xn[0][:, k, c].bitcast(F32), ALU.add, ALU.subtract)
                marks.append(m)
                scr.give(t, m)
            return marks

        def gate_of(layer, which):
            return lambda n, s_: mod_v[:, layer, which * KD + n, s_:s_ + 1]

        for layer in range(LAYERS2):
            last_layer = layer == LAYERS2 - 1
            TO = S if last_layer else T2
            xn_ready = modulated(sums, layer, "g_norm_mix", 0, 1, T2)
            sums = SumSquares(TO)
            st = ExitStack()
            if layer % 3 == 0:
                g = layer // 3
                name = f"gla{g}_"
                oT = tiles(st, name + "o", KD, T2)
                inner = ExitStack()
                qT, kT = tiles(inner, name + "q", 4, T2), tiles(inner, name + "k", 4, T2)
                vr = tiles(inner, name + "v", 4, D)
                sets = [[tiles(inner, f"{name}set{i}{d}", 3, T2) for d in range(2)] for i in range(2)]
                states = [tile(inner, f"{name}state{d}", GLA_DV) for d in range(2)]
                low = tile(inner, name + "low", T2)
                g2 = tile(inner, name + "g2", 512)
                restart = tile(inner, name + "restart", T2)
                masks = tile(inner, name + "masks", 2 * GLA_C)
                masked = [tile(inner, f"{name}masked{i}", GLA_C) for i in range(4)]
                e_last = tile(inner, name + "e_last", 4 * 8)
                totals = tile(inner, name + "totals", 4 * 8)
                fence()
                g2_in = stage_load(g2[0:32 + GLA_RANK, :], io["gla_w_g2"][g], 11)
                at, n = CON["restart"]
                restart_in = stage_load(restart, io["con"][:, at:at + n], 12)
                at, n = CON["gla_mask"]
                masks_in = stage_load(masks, io["con"][:, at:at + n], 13)
                linear("gla_w_in", xn, xn_ready, TO, copy_to(lambda n: qT[:, n, 0:TO], scale=GLA_DK ** -0.5))
                linear("gla_w_in", xn, xn_ready, T2, copy_to(lambda n: kT[:, n, :]))
                linear("gla_w_g1", xn, xn_ready, T2, copy_to(lambda n: low))
                low_ready = act.last()

                def prepare(h):
                    pe.wait(low_ready, g2_in)
                    dve.wait(restart_in)
                    for d in range(2):
                        qb, kb, kd = (sets[h % 2][d][:, i, :] for i in range(3))
                        slot = (h % 2) * 2 + d
                        bank = psum.take(pe)
                        rank = slice(32 * d, 32 * d + GLA_RANK)
                        m = pe.done(mm(bank, g2[rank, h * P:(h + 1) * P], low[rank, :]))
                        z, a, b = scr.take(act, dve), scr.take(act, dve), scr.take(act, dve)
                        bias = vec("gla_b_g", (g * 2 + d) * 4 + h)
                        act.wait(m)
                        a_act(z, bank, ACT.Identity, bias=bias)
                        m = a_act(a, bank, ACT.Abs, bias=bias)
                        psum.give(bank, m)
                        act.chain()
                        a_act(a, a, ACT.Exp, scale=-1.0)
                        act.chain()
                        m = a_act(a, a, ACT.Ln, bias=con("one"))
                        yield
                        dve.wait(m)
                        v_stt(z, z, 0.0, a, ALU.min, ALU.subtract)
                        dve.chain()
                        v_ts(z, z, 1.0 / GLA_TAU)
                        dve.chain()
                        dve.done(nc.vector.tensor_tensor_scan(b, restart, z, 0.0, ALU.mult, ALU.add))
                        dve.chain()
                        bc = b.rearrange("p (c t) -> p c t", t=GLA_C)
                        total = totals[:, slot * 8:slot * 8 + 8]
                        total_b = total.unsqueeze(2).to_broadcast([P, 8, GLA_C])
                        m = v_ts(total, bc[:, :, GLA_C - 1:GLA_C].rearrange("p c o -> p (c o)"), 1.0)
                        yield
                        dve.chain()
                        if d == 1:
                            v_tt(b, z, b, ALU.subtract)
                            dve.chain()
                            m = v_tt(bc, bc, total_b, ALU.add)
                            dve.chain()
                        v_tt(z.rearrange("p (c t) -> p c t", t=GLA_C), total_b, bc, ALU.subtract)
                        m = dve.last()
                        act.wait(m)
                        a_act(e_last[:, slot * 8:slot * 8 + 8], total, ACT.Exp)
                        m1 = a_act(a, b, ACT.Exp)
                        act.chain()
                        m2 = a_act(b, b, ACT.Exp, scale=-1.0)
                        m3 = a_act(z, z, ACT.Exp)
                        yield
                        dve.wait(m1)
                        v_tt(qb[:, 0:TO], qT[:, h, 0:TO], a[:, 0:TO], ALU.mult)
                        dve.wait(m2)
                        v_tt(kb, kT[:, h, :], b, ALU.mult)
                        dve.wait(m3)
                        dve.chain()
                        m = v_tt(a, kT[:, h, :], z, ALU.mult)
                        scr.give(z, m)
                        scr.give(b, m)
                        yield
                        bank = psum.take(pe)
                        pe.wait(m)
                        for t in range(4):
                            ins = nc.tensor.transpose(bank[:, t * P:(t + 1) * P], a[:, t * P:(t + 1) * P], ident)
                        m = pe.done(ins)
                        scr.give(a, m)
                        act.wait(m)
                        m = a_act(kd, bank, ACT.Copy)
                        psum.give(bank, m)
                        yield

                prep = prepare(0)
                linear("gla_w_in", xn, xn_ready, T2, rows_to(vr), rows=4, side=prep)
                v_ready = act.last()
                for _ in prep:
                    fill(1)

                def evac_r(n, bank, m):
                    t = scr.take(act, dve)
                    sigmoid(t[:, 0:TO], bank, m)
                    dve.wait(m)
                    dve.chain()
                    m = v_tt(t[:, 0:TO], bank, t[:, 0:TO], ALU.mult)
                    dve.wait(normed[n // 2])
                    dve.chain()
                    m2 = v_tt(oT[:, n, 0:TO], oT[:, n, 0:TO], t[:, 0:TO], ALU.mult)
                    scr.give(t, m2)
                    r_ready.append(m2)
                    return m

                r_ready, normed = [], [None] * 4
                r_steps = linear_steps("gla_w_in", xn, xn_ready, TO, evac_r)
                written = {}
                orders = ([4, 5, 6, 7, 0, 1, 2, 3], [7, 6, 5, 4, 3, 2, 1, 0])
                dve.wait(masks_in)
                masked_ring = Ring(masked)

                def scan(h):
                    pe.wait(dve.last(), act.last(), v_ready)
                    state_ready = [None, None]

                    def early(step):
                        out = []
                        bank = psum.take(pe)
                        m = None
                        for d in range(2):
                            c = orders[d][step]
                            part = slice(GLA_C * (c % 2), GLA_C * (c % 2) + GLA_C)
                            qb, kb, kd = (sets[h % 2][d][:, i, :] for i in range(3))
                            tk = slice(c * GLA_C, (c + 1) * GLA_C)
                            if not (last_layer and c >= 4):
                                m = pe.done(mm(bank[part, d * GLA_C:(d + 1) * GLA_C], kb[:, tk], qb[:, tk]))
                                am = masked_ring.take(dve)
                                dve.wait(m)
                                m = v_tt(am[part, :], bank[part, d * GLA_C:(d + 1) * GLA_C],
                                         masks[part, d * GLA_C:(d + 1) * GLA_C], ALU.mult)
                                out.append((am, m))
                            else:
                                out.append(None)
                        psum.give(bank, *([m] if m else []))
                        ub = [psum.take(pe), psum.take(pe)]
                        u_done = None
                        if step < 7:
                            for d in range(2):
                                c = orders[d][step]
                                part = slice(GLA_C * (c % 2), GLA_C * (c % 2) + GLA_C)
                                kd = sets[h % 2][d][:, 2, :]
                                ins = mm(ub[d][:, 0:256], kd[part, (c // 2) * P:(c // 2 + 1) * P],
                                         vr[part, c // 2, h * GLA_DV:(h + 1) * GLA_DV])
                            u_done = pe.done(ins)
                        return out, ub, u_done

                    def late(step, out, ub, u_done):
                        m = None
                        for d in range(2):
                            c = orders[d][step]
                            if out[d] is None:
                                continue
                            part = slice(GLA_C * (c % 2), GLA_C * (c % 2) + GLA_C)
                            tk = slice(c * GLA_C, (c + 1) * GLA_C)
                            am, m = out[d]
                            pe.wait(m)
                            if step:
                                pe.wait(state_ready[d])
                            for e in range(2):
                                o = ub[d][:, 256 + e * GLA_C:256 + (e + 1) * GLA_C]
                                if step:
                                    mm(o, states[d][:, e * P:(e + 1) * P], sets[h % 2][d][:, 0, tk], start=True,
                                       stop=False)
                                ins = mm(o, vr[part, c // 2, h * GLA_DV + e * P:h * GLA_DV + (e + 1) * P], am[part, :],
                                         start=(step == 0), stop=True)
                            m = pe.done(ins)
                            masked_ring.give(am, m)
                        m_o = m
                        if step < 7:
                            dve.wait(u_done, pe.last())
                            for d in range(2):
                                src, c = ub[d][:, 0:256], orders[d][step]
                                slot = (h % 2) * 2 + d
                                if step == 0:
                                    state_ready[d] = v_ts(states[d], src, 1.0)
                                else:
                                    dve.wait(state_ready[d])
                                    state_ready[d] = v_stt(states[d], states[d],
                                                           e_last[:, slot * 8 + c:slot * 8 + c + 1], src,
                                                           ALU.mult, ALU.add)
                        for d in range(2):
                            c = orders[d][step]
                            if out[d] is None:
                                continue
                            tk = slice(c * GLA_C, (c + 1) * GLA_C)
                            src = ub[d][:, 256:256 + 2 * GLA_C].rearrange("p (e t) -> p e t", e=2)
                            dst = oT[:, 2 * h:2 * h + 2, tk]
                            key = (h, c)
                            dve.wait(m_o)
                            if key in written:
                                dve.wait(written[key])
                                m = v_tt(dst, src, dst, ALU.add)
                            else:
                                m = v_ts(dst, src, 1.0)
                            written[key] = m
                        for bank in ub:
                            psum.give(bank, pe.last(), dve.last())

                    held = early(0)
                    for step in range(8):
                        after = early(step + 1) if step < 7 else None
                        late(step, *held)
                        held = after
                        yield

                def norm_head(h):
                    squares = SumSquares(TO)
                    for e in range(2):
                        squares.add(oT[:, 2 * h + e, 0:TO], dve.last())
                    yield
                    r, m = squares.inv_rms(1.0 / GLA_DV)
                    dve.wait(m)
                    for e in range(2):
                        o = oT[:, 2 * h + e, 0:TO]
                        normed[h] = v_stt(o, o, vec("gla_g_head", g * 2 + e), r[:, 0:TO], ALU.mult, ALU.mult)
                    scr.give(r, normed[h])
                    yield

                for h in range(GLA_HEADS):
                    prep = prepare(h + 1) if h < GLA_HEADS - 1 else iter(())
                    norm = norm_head(h - 1) if h else iter(())
                    for step, _ in enumerate(scan(h)):
                        next(norm, None)
                        next(prep, None)
                        if h >= 2 and step >= 4 and (h > 2 or step > 5):
                            next(r_steps, None) if step == 7 or h > 2 else None
                        else:
                            fill(1)
                    for _ in prep:
                        fill(1)
                for _ in norm_head(GLA_HEADS - 1):
                    fill(1)
                inner.close()
                mixed = halves(st, name + "mixed", KD, T2)
                for _ in r_steps:
                    pass
                fence()
                m_ready = [cut(mixed[0][:, k, 0:TO], mixed[1][:, k, 0:TO], oT[:, k, 0:TO], r_ready[k])
                           for k in range(KD)]
                linear("gla_w_out", mixed, m_ready, TO, add_to_x(sums, gate_of(layer, 2)))
            elif layer % 3 == 1:
                u = tile(st, "u_pad", KD * 2 * PADDED).rearrange("p (k s t) -> p k s t", k=KD, s=2)
                y = tiles(st, "y", KD, T2)
                yh = halves(st, "yh", KD, T2)
                fence()
                for k in range(KD):
                    dve.done(nc.vector.memset(u[:, k, :, 0:CONV_PAD], 0.0))
                    dve.done(nc.vector.memset(u[:, k, :, CONV_PAD + S:PADDED], 0.0))
                u_ready = [None] * KD
                y_ready = [None] * KD

                def depthwise(chunks):
                    for n in chunks:
                        out = y[:, n, :].rearrange("p (s t) -> p s t", s=2)
                        dve.wait(u_ready[n])
                        v_ts(out, u[:, n, :, 0:S], vec("w_dw", n), vec("b_dw", n), ALU.mult, ALU.add)
                        for j in range(1, CONV_W):
                            dve.chain()
                            m = v_stt(out, u[:, n, :, j:j + S], vec("w_dw", j * KD + n), out, ALU.mult, ALU.add)
                            if j % 6 == 0:
                                yield
                        y_ready[n] = m

                taps = iter(())
                for n0 in range(0, KD, 4):
                    def evac_a(n, bank, m, n0=n0):
                        act.wait(m)
                        return a_act(u[:, n0 + n, :, CONV_PAD:CONV_PAD + S], bank.rearrange("p (s t) -> p s t", s=2),
                                     ACT.Identity, bias=vec("b_pw1", n0 + n))

                    def evac_gt(n, bank, m, n0=n0):
                        t = scr.take(act, dve)
                        act.wait(m)
                        m = done = a_act(t, bank, ACT.Identity, bias=vec("b_pw1", KD + n0 + n))
                        act.chain()
                        sigmoid(t, t, m)
                        dve.chain()
                        ua = u[:, n0 + n, :, CONV_PAD:CONV_PAD + S]
                        u_ready[n0 + n] = v_tt(ua, ua, t.rearrange("p (s t) -> p s t", s=2), ALU.mult)
                        scr.give(t, u_ready[n0 + n])
                        return done
                    linear("conv_w_pw1", xn, xn_ready, T2, evac_a, side=taps)
                    linear("conv_w_pw1", xn, xn_ready, T2, evac_gt, side=taps)
                    if n0 == 0:
                        taps = depthwise(range(4))
                for rest in (taps, depthwise(range(4, KD))):
                    for _ in rest:
                        fill(2)
                bank = psum.take(pe)
                total = scr.take(dve)
                dve.wait(y_ready[-1])
                m = v_tt(total, y[:, 0, :], y[:, 1, :], ALU.add)
                for k in range(2, KD):
                    dve.chain()
                    m = v_tt(total, total, y[:, k, :], ALU.add)
                pe.wait(m)
                m = pe.done(mm(bank, ones, total))
                scr.give(total, m)
                mean = scr.take(act)
                act.wait(m)
                m = a_act(mean, bank, ACT.Copy, scale=1.0 / D)
                psum.give(bank, m)
                dve.wait(m)
                squares = SumSquares(T2)
                for k in range(KD):
                    m = v_tt(y[:, k, :], y[:, k, :], mean, ALU.subtract)
                    if k == KD - 1:
                        scr.give(mean, m)
                    squares.add(y[:, k, :], m)
                    fill(1)
                r, m = squares.inv_rms(1.0 / D)
                dve.wait(m)
                for k in range(KD):
                    yk = y[:, k, :]
                    v_stt(yk, yk, vec("ln_g", k), r, ALU.mult, ALU.mult)
                    dve.chain()
                    m = v_ts(yk, yk, vec("ln_b", k), op0=ALU.add)
                    m = silu_into(yk, yk, m, T2, guard=True)
                    y_ready[k] = cut(yh[0][:, k, :], yh[1][:, k, :], yk, m)
                    fill(1)
                scr.give(r, dve.last())
                linear("conv_w_pw2", yh, y_ready, T2, add_to_x(sums, gate_of(layer, 2), lambda n: vec("b_pw2", n)))
            else:
                qT, kT = tiles(st, "gq", KD, T2), tiles(st, "gk", KV_HEADS, T2)
                vr = tiles(st, "gv", 4, KV_HEADS * HD)
                oT = halves(st, "go", KD, T2)
                rot = tile(st, "rot", 2 * S)
                fence()
                at, _ = CON["cos"]
                rot_in = stage_load(rot, io["con"][:, at:at + 2 * S], 14)
                cos, sin = rot[:, 0:S], rot[:, S:2 * S]
                raw_ready = []
                rotated = []

                def norm_and_rotate():
                    n = 0
                    while n < KD + KV_HEADS:
                        if n >= len(raw_ready):
                            yield
                            continue
                        t_ = qT[:, n, :] if n < KD else kT[:, n - KD, :]
                        squares = SumSquares(T2)
                        squares.add(t_, raw_ready[n])
                        yield
                        r, m = squares.inv_rms(1.0 / HD, con("head_ones"))
                        dve.wait(m, rot_in)
                        m = v_stt(t_, t_, vec("g_q") if n < KD else vec("g_k"), r, ALU.mult, ALU.mult)
                        yield
                        bank = psum.take(pe)
                        pe.wait(m)
                        m2 = pe.done(mm(bank[:, 0:S], con("rope_swap"), t_[:, 0:S]))
                        dve.wait(m2)
                        m = v_tt(r[:, 0:S], bank[:, 0:S], sin, ALU.mult)
                        psum.give(bank, m)
                        v_tt(t_[:, 0:S], t_[:, 0:S], cos, ALU.mult)
                        dve.chain()
                        m = v_tt(t_[:, 0:S], t_[:, 0:S], r[:, 0:S], ALU.add)
                        scr.give(r, m)
                        rotated.append(m)
                        n += 1
                rotate = norm_and_rotate()
                linear("attn_w_qkv", xn, xn_ready, T2, copy_to(lambda n: qT[:, n, :], raw_ready), side=rotate)
                linear("attn_w_qkv", xn, xn_ready, T2, copy_to(lambda n: kT[:, n, :], raw_ready), side=rotate)
                linear("attn_w_qkv", xn, xn_ready, T2, rows_to(vr), rows=4, side=rotate)
                v_ready = act.last()
                for _ in rotate:
                    fill(1)
                units = []
                for h in range(Q_HEADS):
                    part = slice(HD * (h % 2), HD * (h % 2) + HD)
                    kv = h // (Q_HEADS // KV_HEADS)
                    for qt in range(4):
                        tok = slice(qt * P, (qt + 1) * P)
                        lat = qt < 2
                        first_tile = 0 if lat else 2
                        units.append(dict(nk=T2 if lat else S, causal=False, ready=[rotated[-1], v_ready],
                                          pairs=[(qT[part, h // 2, tok], kT[part, kv, first_tile * P:T2])],
                                          outs=[(part, (lambda t, kv=kv, f=first_tile:
                                                        vr[:, f + t, kv * HD:(kv + 1) * HD]),
                                                 [half[part, h // 2, tok] for half in oT], 0)]))
                attended = Attention(units, HD ** -0.5).run()
                linear("attn_w_out", oT, [attended] * KD, T2, add_to_x(sums, gate_of(layer, 2)))
            st.close()

            xn_ready = modulated(sums, layer, "g_norm_mlp", 3, 4, TO)
            sums = None if last_layer else SumSquares(T2)
            HC = FC2 // 2
            for half in range(2):
                st = ExitStack()
                hid = halves(st, f"mlp{layer}{half}", HC, T2)
                fence()
                hid_ready = []

                def evac_relu(n, bank, m):
                    t = scr.take(act)
                    act.wait(m)
                    done = a_act(t[:, 0:TO], bank, ACT.Relu)
                    dve.wait(done)
                    m = v_tt(t[:, 0:TO], t[:, 0:TO], t[:, 0:TO], ALU.mult)
                    hid_ready.append(cut(hid[0][:, n, 0:TO], hid[1][:, n, 0:TO], t[:, 0:TO], m))
                    scr.give(t, hid_ready[-1])
                    return done
                linear("w_mlp_in", xn, xn_ready, TO, evac_relu)
                linear("w_mlp_out", hid, hid_ready, TO,
                       add_to_x(sums if half else None, gate_of(layer, 5)))
                st.close()

        sp.wait(dve.last())
        out_mark = dma(io["out"], x[:, :, 0:S], out_sem)
        sp.wait(out_mark)
        assert stream.loaded == len(plan) and bg_done[0] == len(bg_todo)


WEIGHTS = [("ev_w_in", "ev_w_in", 0), ("ev_w_out", "ev_w_out", 0), ("od_w_in", "od_w_in", 0),
           ("od_w_out", "od_w_out", 0), ("xattn_wq", "xattn_wq", None), ("xattn_wkv", "xattn_wkv", None),
           ("xattn_wo", "xattn_wo", None), ("ffn_w_up", "ffn_w_up", None), ("ffn_w_down", "ffn_w_down", None),
           ("w_mlp_in", "w_mlp_in_2", None), ("w_mlp_out", "w_mlp_out_2", None),
           ("gla_w_in", "gla_w_in_2", None), ("gla_w_out", "gla_w_out_2", None), ("conv_w_pw1", "conv_w_pw1_2", 0),
           ("conv_w_pw2", "conv_w_pw2_2", 0), ("attn_w_out", "attn_w_out_2", 0)]


def kernel(**inputs):
    import concourse.bacc as _bacc
    from concourse.bass_utils import run_bass_kernel_spmd as _run

    a = {k: np.asarray(v) for k, v in inputs.items()}

    def cols(v):
        return np.ascontiguousarray(v.reshape(-1, P).T)

    def tokens(t):
        return np.ascontiguousarray(t[0].T.reshape(KD, P, -1).transpose(1, 0, 2))

    vec = np.zeros((P, NVEC), np.float32)

    def put(name, value):
        at, n = VEC[name]
        vec[:, at:at + n] = value
    for name in ("mem_norm", "norm_mix", "norm_xattn", "norm_ffn", "pool_scale", "final_norm", "dn_conv", "dn_norm_g",
                 "ffn_conv"):
        put(name, cols(a[name]))
    for name, src in (("g_norm_mix", "g_norm_mix_2"), ("g_norm_mlp", "g_norm_mlp_2"), ("b_mod", "b_mod_2"),
                      ("gla_b_g", "gla_b_g_2"), ("gla_g_head", "gla_g_head_2"), ("b_pw1", "conv_b_pw1_2"),
                      ("w_dw", "conv_w_dw_2"), ("b_dw", "conv_b_dw_2"), ("ln_g", "conv_ln_g_2"),
                      ("ln_b", "conv_ln_b_2"), ("b_pw2", "conv_b_pw2_2")):
        put(name, cols(a[src]))
    put("g_q", np.concatenate([a["attn_g_q_2"][0]] * 2)[:, None])
    put("g_k", np.concatenate([a["attn_g_k_2"][0]] * 2)[:, None])
    put("c", np.stack([cols(a["c_2"]), cols(a["c_ctx_2"])], axis=2).reshape(P, 2 * KD))
    put("a_log", a["dn_a_log"].ravel())
    put("dt_bias", a["dn_dt_bias"].ravel())
    row = np.broadcast_to(np.concatenate([a["sgu_ln_g"].ravel(), a["sgu_ln_b"].ravel(), a["sgu_b"].ravel()]), (P, NROW))

    g1 = np.zeros((2, D, P), np.float32)
    g2 = np.zeros((2, 32 + GLA_RANK, 512), np.float32)
    for d in range(2):
        g1[:, :, 32 * d:32 * d + GLA_RANK] = a["gla_w_g1_2"][:, d]
        g2[:, 32 * d:32 * d + GLA_RANK] = a["gla_w_g2_2"][:, d]
    qkv = a["attn_w_qkv_2"][0]
    heads = [qkv[:, D + HD * (i // 2):D + HD * (i // 2) + HD] for i in range(2 * KV_HEADS)]
    qkv = np.concatenate([qkv[:, :D]] + heads + [qkv[:, D + KV_HEADS * HD:]], axis=1)
    arrays = {
        "attn_w_qkv": qkv,
        "con": shape_constants(), "vec": vec, "row": np.ascontiguousarray(row),
        "xT": tokens(a["x"]), "memT": tokens(a["mem"]), "ctxT": tokens(a["ctx_2"]),
        "pool_w": np.ascontiguousarray(a["pool_w"][0].transpose(1, 0, 2)),
        "sgu_wT": np.ascontiguousarray(a["sgu_w"][0].transpose(2, 0, 1)),
        "gla_w_g1": g1,
        "gla_w_g2": g2,
    }
    arrays["w_mod"] = np.ascontiguousarray(a["w_mod_2"].reshape(LAYERS2, KD, P, 6 * KD, P).transpose(0, 3, 2, 1, 4)
                                           ).reshape(LAYERS2, 6 * KD, P, KD * P)
    for name, src, index in WEIGHTS:
        arrays[name] = np.ascontiguousarray(a[src] if index is None else a[src][index])
    nc = _bacc.Bacc("TRN2", target_bir_lowering=False, num_devices=1)
    io = {name: nc.dram_tensor(f"in_{name}", v.shape, F32, kind="ExternalInput").ap() for name, v in arrays.items()}
    io["out"] = nc.dram_tensor("out_xT", (P, KD, S), F32, kind="ExternalOutput").ap()
    build(nc, io)
    r = _run(nc, [{f"in_{name}": v for name, v in arrays.items()}], core_ids=[0])
    out = r.results[0]["out_xT"]
    return np.ascontiguousarray(out.transpose(1, 0, 2).reshape(D, S).T)[None]
```

```python
import numpy as np
import concourse.bass as bass
from concourse import mybir
from concourse.alu_op_type import AluOpType as ALU
from contextlib import ExitStack

F32 = mybir.dt.float32
F32R = mybir.dt.float32r
ACT = mybir.ActivationFunctionType
AX_X = mybir.AxisListType.X

P = 128
D = 1024
KD = D // P
S = 256
T2 = 2 * S
EPS = 1e-6
MOBA_HEADS, MOBA_DIM = 8, 64
A_WIDTH = MOBA_HEADS * MOBA_DIM
POOL_WINDOWS = (2, 4, 8, 16)
SGU_WIDTH = 512
DN_HEADS, DN_CONV, DN_WIDTH = 4, 4, 512
X_HEADS = 4
D_FF = 2816
FC = D_FF // P
FFN_CONV = 3
LAYERS2 = 4
D_FF2 = 4096
FC2 = D_FF2 // P
GLA_HEADS, GLA_DK, GLA_DV, GLA_RANK, GLA_TAU, GLA_C = 4, 128, 256, 16, 16.0, 64
CONV_W = 31
CONV_PAD = CONV_W // 2
PADDED = S + 2 * CONV_PAD
KV_HEADS, Q_HEADS, HD = 4, 16, 64
GRID_W = 64
HEAD_ORDER = [h for a in (0, 2) for i in range(4) for h in (4 * a + i, 4 * (a + 1) + i)]
NEG = -1e30


def spans(sizes):
    at, out = 0, {}
    for name, n in sizes:
        out[name] = (at, n)
        at += n
    return out, at


VEC, NVEC = spans([
    ("mem_norm", KD), ("norm_mix", 2 * KD), ("norm_xattn", 2 * KD), ("norm_ffn", 2 * KD), ("pool_scale", 4),
    ("final_norm", KD), ("dn_conv", DN_CONV * 12), ("dn_norm_g", 1), ("ffn_conv", 2 * FFN_CONV * 2 * FC),
    ("g_norm_mix", LAYERS2 * KD), ("g_norm_mlp", LAYERS2 * KD), ("b_mod", LAYERS2 * 6 * KD),
    ("gla_b_g", 2 * 2 * GLA_HEADS), ("gla_g_head", 2 * 2), ("b_pw1", 2 * KD), ("w_dw", CONV_W * KD), ("b_dw", KD),
    ("ln_g", KD), ("ln_b", KD), ("b_pw2", KD), ("g_q", 1), ("g_k", 1), ("c", 2 * KD), ("a_log", DN_HEADS), ("dt_bias", DN_HEADS)])
ROW, NROW = spans([("sgu_ln_g", SGU_WIDTH), ("sgu_ln_b", SGU_WIDTH), ("sgu_b", 4 * P)])
INV_LEVELS = (1, 2, 4, 8, 16, 32, 64)
CON, NCON = spans([("ident", P), ("ones", P), ("head_ones", P), ("causal", P), ("upto", P), ("rope_swap", P),
                   ("eps", 1), ("one", 1),
                   ("level", P * len(INV_LEVELS)), ("gla_mask", 2 * GLA_C), ("restart", T2), ("cos", S), ("sin", S),
                   ("pool_inv", 4 * S)])
NCON_KEPT = CON["level"][0]


def shape_constants():
    c = np.zeros((P, NCON), np.float32)

    def put(name, value):
        at, n = CON[name]
        c[:, at:at + n] = value

    i = np.arange(P)
    put("ident", np.eye(P))
    put("ones", 1.0)
    put("head_ones", (i[:, None] // HD) == (i[None, :] // HD))
    put("causal", np.where(i[None, :] <= i[:, None], 0.0, NEG))
    put("upto", i[:, None] <= i[None, :])
    put("rope_swap", (i[:, None] ^ 32) == i[None, :])
    levels = []
    for s in INV_LEVELS:
        same = (i[:, None] // (2 * s)) == (i[None, :] // (2 * s))
        levels.append(same & (i[:, None] % (2 * s) < s) & (i[None, :] % (2 * s) >= s))
    put("level", np.concatenate(levels, axis=1))
    j, t = i[:, None] % GLA_C, np.arange(GLA_C)[None, :]
    put("gla_mask", np.concatenate([j <= t, j >= t], axis=1))
    put("restart", (np.arange(T2) % GLA_C != 0)[None, :])
    n = HD // 4
    inv = np.float32(10000.0) ** (-np.arange(n, dtype=np.float32) / np.float32(n))
    tok = np.arange(S)
    ang = np.concatenate([(tok // GRID_W).astype(np.float32)[:, None] * inv,
                          (tok % GRID_W).astype(np.float32)[:, None] * inv], axis=1).astype(np.float32)
    put("cos", np.cos(ang).T[i % 32])
    put("sin", np.sin(ang).T[i % 32] * np.where(i % HD < 32, -1.0, 1.0)[:, None])
    put("pool_inv", np.concatenate([1.0 / np.minimum(tok + 1.0, w) for w in POOL_WINDOWS])[None, :])
    put("eps", EPS)
    put("one", 1.0)
    return c


SLAB_K, SLAB_N = 2, 512
SLAB = SLAB_K * SLAB_N
BG_K, BG_N = 2, 512
WIDE_LAYER, WIDE_AT = 2, {0: (0, 1, 2), 1: (3, 4, 5)}
WIDE = 8 * P


def products():
    for layer in range(2):
        if layer == 0:
            yield from ((("ev_w_in", None, 0, KD, a, b)) for a, b in ((0, 1024), (1024, 1536), (1536, 2048)))
        else:
            g0 = 2 * SGU_WIDTH + 3 * DN_WIDTH
            yield from ((("od_w_in", None, 0, KD, a, b))
                        for a, b in ((0, 512), (512, 1024), (g0 + 512, g0 + 520), (1024, g0), (g0, g0 + 512)))
        yield (("ev_w_out", "od_w_out")[layer], None, 0, KD, 0, D)
        yield ("xattn_wkv", layer, 0, KD, 0, D)
        yield ("xattn_wkv", layer, 0, KD, D, 2 * D)
        yield ("xattn_wq", layer, 0, KD, 0, D)
        yield ("xattn_wo", layer, 0, KD, 0, D)
        for n0 in range(0, D_FF, 512):
            n1 = min(n0 + 512, D_FF)
            yield ("ffn_w_up", layer, 0, KD, n0, n1)
            yield ("ffn_w_up", layer, 0, KD, D_FF + n0, D_FF + n1)
        yield ("ffn_w_down", layer, 0, FC, 0, D)
    for layer in range(LAYERS2):
        if layer % 3 == 0:
            g = layer // 3
            yield ("gla_w_in", g, 0, KD, 0, 512)
            yield ("gla_w_in", g, 0, KD, 512, 1024)
            yield ("gla_w_g1", g, 0, KD, 0, P)
            yield ("gla_w_in", g, 0, KD, 1024, 2048)
            yield ("gla_w_in", g, 0, KD, 2048, 3072)
            yield ("gla_w_out", g, 0, KD, 0, D)
        elif layer % 3 == 1:
            for n0 in range(0, D, 512):
                yield ("conv_w_pw1", None, 0, KD, n0, n0 + 512)
                yield ("conv_w_pw1", None, 0, KD, D + n0, D + n0 + 512)
            yield ("conv_w_pw2", None, 0, KD, 0, D)
        else:
            yield ("attn_w_qkv", None, 0, KD, 0, D)
            yield ("attn_w_qkv", None, 0, KD, D, D + KV_HEADS * HD)
            yield ("attn_w_qkv", None, 0, KD, D + KV_HEADS * HD, D + 2 * KV_HEADS * HD)
            yield ("attn_w_out", None, 0, KD, 0, D)
        for half in range(2):
            yield ("w_mlp_in", layer, 0, KD, half * D_FF2 // 2, (half + 1) * D_FF2 // 2)
            yield ("w_mlp_out", layer, half * FC2 // 2, (half + 1) * FC2 // 2, 0, D)


def slabs(product):
    name, index, k0, k1, n0, n1 = product
    for nb in range(n0, n1, SLAB_N):
        for kb in range(k0, k1, SLAB_K):
            yield (name, index, kb, min(kb + SLAB_K, k1), nb, min(nb + SLAB_N, n1))


class Lane:

    def __init__(self, engine, sem):
        self.engine, self.sem, self.count, self.seen = engine, sem, 0, {}

    def done(self, ins):
        ins.then_inc(self.sem, 1)
        self.count += 1
        return (self.sem, self.count)

    def last(self):
        return (self.sem, self.count)

    def wait(self, *marks):
        for mark in marks:
            sem, value = mark
            if value > self.seen.get(sem.name, 0):
                self.engine.wait_ge(sem, value)
                self.seen[sem.name] = value

    def chain(self):
        self.wait(self.last())


class Ring:

    def __init__(self, tiles):
        self.free = [(t, ()) for t in tiles]

    def take(self, *lanes):
        tile, marks = self.free.pop(0)
        for lane in lanes:
            lane.wait(*marks)
        return tile

    def give(self, tile, *marks):
        self.free.append((tile, marks))


class WeightStream:

    def __init__(self, items, raw, halves, load, split):
        self.items, self.raw, self.halves = items, raw, halves
        self.load, self.split = load, split
        self.loaded, self.in_flight, self.splitting, self.ready = 0, [], [], []

    def pump(self):
        while True:
            if self.raw.free and self.loaded < len(self.items):
                slot = self.raw.take()
                self.in_flight.append((self.items[self.loaded], slot, self.load(self.items[self.loaded], *slot)))
                self.loaded += 1
            elif self.halves.free and self.in_flight:
                item, (slot, marks), landed = self.in_flight.pop(0)
                pair, pair_marks = self.halves.take()
                self.splitting.append((item, slot, pair, self.split(item, slot, landed, pair, pair_marks)))
                if len(self.splitting) > 1:
                    self.finish_split()
            else:
                return

    def finish_split(self):
        item, slot, pair, halves = self.splitting.pop(0)
        next(halves)
        done = next(halves)
        self.raw.give(slot, done)
        self.ready.append((item, pair, done))

    def next(self, item):
        self.pump()
        if not self.ready:
            self.finish_split()
        got, pair, mark = self.ready.pop(0)
        assert got == item, (got, item)
        return pair, mark

    def used_up(self, pair, mark):
        self.halves.give(pair, mark)
        self.pump()


class Later:

    def __init__(self):
        self.open = []

    def add(self, steps):
        if next(steps, self) is not self:
            self.open.append(steps)

    def step(self):
        self.open = [steps for steps in self.open if next(steps, self) is not self]

    def until(self, condition):
        for _ in range(1000):
            if condition():
                return
            self.step()
        raise RuntimeError("the open steps wait for each other")

    def drain(self):
        self.until(lambda: not self.open)


class LateRing(Ring):

    def take(self):
        return self.free.pop(0)


def build(nc, io):
    ctx = ExitStack()
    with ctx:
        def lane(engine, name):
            return Lane(engine, ctx.enter_context(nc.semaphore(name)))

        def tile(where, name, cols, dt=F32):
            return where.enter_context(nc.sbuf_tensor(name, [P, cols], dt))[:, :]

        def tiles(where, name, k, width, dt=F32):
            return tile(where, name, k * width, dt).rearrange("p (k t) -> p k t", k=k)

        def halves(where, name, k, width):
            return tiles(where, name + "_hi", k, width, F32R), tiles(where, name + "_lo", k, width, F32R)

        pe, act, dve, pool, sp = (lane(nc.tensor, "pe_done"), lane(nc.scalar, "act_done"), lane(nc.vector, "dve_done"),
                                  lane(nc.gpsimd, "pool_done"), lane(nc.sync, "sp_unused"))
        dma_count = {}

        def dma(out, in_, sem, engine=None):
            (engine or nc.sync).dma_start(out, in_).then_inc(sem, 16)
            dma_count[sem.name] = dma_count.get(sem.name, 0) + 16
            return (sem, dma_count[sem.name])

        x = tiles(ctx, "x", KD, T2)
        xn = halves(ctx, "xn", KD, T2)
        con_t = tile(ctx, "con_t", NCON_KEPT)
        vec_t = tile(ctx, "vec_t", NVEC)
        mod_t = tile(ctx, "mod_t", LAYERS2 * 6 * KD * 2)
        modA = tile(ctx, "modA", KD * 2)
        silu_c = tile(ctx, "silu_c", KD * 2)
        small_t = tile(ctx, "small_t", 32 * 8)
        NRAW, NPAIR, NBG, NSCR = 4, 3, 3, 7
        raw_t = tile(ctx, "raw_t", SLAB * NRAW)
        whi_t = tile(ctx, "whi_t", SLAB * NPAIR, F32R)
        wlo_t = tile(ctx, "wlo_t", SLAB * NPAIR, F32R)
        bg_t = tile(ctx, "bg_t", BG_K * BG_N * NBG)
        scr_t = tile(ctx, "scr_t", NSCR * T2)
        banks_t = [ctx.enter_context(nc.psum_tensor(f"bank{i}", [P, 512], F32)) for i in range(8)]
        psum = Ring([b[:, :] for b in banks_t])
        scr = Ring([scr_t[:, i * T2:(i + 1) * T2] for i in range(NSCR)])
        small = Ring([small_t[:, i * 8:(i + 1) * 8] for i in range(32)])

        def sems(name, n):
            return [ctx.enter_context(nc.semaphore(f"{name}{i}")) for i in range(n)]

        raw_in, bg_in, wide_in, in_sem = (sems("raw_in", NRAW), sems("bg_in", NBG), sems("wide_in", 2),
                                          sems("in", 16))
        x_sem = sems("x_in", 4)
        out_sem = ctx.enter_context(nc.semaphore("out_done"))

        def con(name, i=0, n=None):
            at, size = CON[name]
            return con_t[:, at + i:at + (size if n is None else i + n)]

        def vec(name, i=0, n=1):
            return vec_t[:, VEC[name][0] + i:VEC[name][0] + i + n]

        ident, eps, ones = con("ident"), con("eps"), con("ones")

        x_in = [dma(x[:, 2 * i:2 * i + 2, 0:S], io["xT"][:, 2 * i:2 * i + 2, :], x_sem[i]) for i in range(4)]
        con_in = dma(con_t, io["con"][:, 0:NCON_KEPT], in_sem[0])
        vec_in = dma(vec_t, io["vec"], in_sem[1])
        nc.scalar.preload_act_table_set("natural_log_exp_and_others")
        for e in (pe, act, dve, pool):
            e.wait(con_in, vec_in)

        def mm(out, lhsT, rhs, start=True, stop=True):
            return nc.tensor.matmul(out, lhsT, rhs, start=start, stop=stop)

        def v_tt(out, a, b, op):
            return dve.done(nc.vector.tensor_tensor(out, a, b, op))

        def v_ts(out, a, s1, s2=None, op0=ALU.mult, op1=None):
            if op1 is None:
                return dve.done(nc.vector.tensor_scalar(out, a, s1, None, op0))
            return dve.done(nc.vector.tensor_scalar(out, a, s1, s2, op0, op1))

        def v_stt(out, a, s, b, op0, op1):
            return dve.done(nc.vector.scalar_tensor_tensor(out=out, in0=a, scalar=s, in1=b, op0=op0, op1=op1))

        def a_act(out, in_, func, bias=0.0, scale=1.0, accum=None):
            if accum is not None:
                return act.done(nc.scalar.activation(out, in_, func, bias=bias, scale=scale, accum_out=accum))
            return act.done(nc.scalar.activation(out, in_, func, bias=bias, scale=scale))

        later = Later()

        def fence():
            later.drain()
            act.wait(pe.last(), dve.last(), pool.last())
            dve.wait(pe.last(), act.last(), pool.last())
            pool.wait(pe.last(), act.last(), dve.last())

        def stage_load(dst, src, sem):
            return dma(dst, src, in_sem[sem], nc.gpsimd)

        def cut_all(parts, *marks):
            act.wait(*marks)
            for hi, lo, src in parts:
                m = a_act(hi, src, ACT.Copy)
            dve.wait(m, *marks)
            for hi, lo, src in parts:
                m = v_tt(lo, src, hi.bitcast(F32), ALU.subtract)
            return m

        def cut(hi, lo, src, *marks):
            return cut_all([(hi, lo, src)], *marks)

        def cut_steps(hi, lo, src, m):
            act.wait(m)
            m = a_act(hi, src, ACT.Copy)
            yield
            dve.wait(m)
            return v_tt(lo, src, hi.bitcast(F32), ALU.subtract)

        def slab_view(flat, item):
            _, _, k0, k1, n0, n1 = item
            return flat[:, 0:(k1 - k0) * (n1 - n0)].rearrange("p (k n) -> p k n", k=k1 - k0)

        def slab_load(item, slot, marks):
            name, index, k0, k1, n0, n1 = item
            W = io[name] if index is None else io[name][index]
            sp.wait(*marks)
            return dma(slab_view(slot[0], item), W.rearrange("(k p) n -> p k n", p=P)[:, k0:k1, n0:n1], slot[1])

        def slab_split(item, slot, landed, pair, pair_marks):
            size = (item[3] - item[2]) * (item[5] - item[4])
            hi, lo, src = pair[0][:, 0:size], pair[1][:, 0:size], slot[0][:, 0:size]
            act.wait(landed, *pair_marks)
            m = a_act(hi, src, ACT.Copy)

            def halves():
                yield m
                dve.wait(m, landed, *pair_marks)
                yield v_tt(lo, src, hi.bitcast(F32), ALU.subtract)
            return halves()

        plan = [item for product in products() for item in slabs(product)]
        stream = WeightStream(
            plan, LateRing([(raw_t[:, i * SLAB:(i + 1) * SLAB], raw_in[i]) for i in range(NRAW)]),
            LateRing([(whi_t[:, i * SLAB:(i + 1) * SLAB], wlo_t[:, i * SLAB:(i + 1) * SLAB]) for i in range(NPAIR)]),
            slab_load, slab_split)
        next_product = products()

        def three(out, w, x_, start, stop):
            mm(out, w[0], x_[0], start=start, stop=False)
            mm(out, w[0], x_[1], start=False, stop=False)
            return mm(out, w[1], x_[0], start=False, stop=stop)

        def giving_back(bank, steps):
            for freed in steps:
                if freed is not None:
                    psum.give(bank, freed)
                yield

        def linear_steps(name, src, ready, T, evac, rows=None):
            product = next(next_product)
            assert product[0] == name, (product, name)
            _, _, k_lo, k_hi, n_lo, n_hi = product
            for item in slabs(product):
                _, _, k0, k1, n0, n1 = item
                if k0 == k_lo:
                    count = rows or (n1 - n0) // P
                    later.until(lambda: len(psum.free) >= count)
                    banks = [psum.take(pe) for _ in range(count)]
                pair, landed = stream.next(item)
                w = [slab_view(half, item) for half in pair]
                pe.wait(landed)
                for j, bank in enumerate(banks):
                    for k in range(k0, k1):
                        i = k - k_lo
                        later.until(lambda: ready[i] is not None)
                        pe.wait(ready[i])
                        start, stop = k == k_lo, k == k_hi - 1
                        if rows:
                            tok = slice(j * P, (j + 1) * P)
                            x_hi, x_lo = src[0][:, i, tok], src[1][:, i, tok]
                            out = bank[:, 0:n1 - n0]
                            mm(out, x_hi, w[0][:, k - k0, :], start=start, stop=False)
                            mm(out, x_hi, w[1][:, k - k0, :], start=False, stop=False)
                            ins = mm(out, x_lo, w[0][:, k - k0, :], start=False, stop=stop)
                        else:
                            col = slice(j * P, (j + 1) * P)
                            ins = three(bank[:, 0:T], [half[:, k - k0, col] for half in w],
                                        [half[:, i, 0:T] for half in src], start, stop)
                    mark = pe.done(ins)
                    if k1 == k_hi:
                        if j == len(banks) - 1:
                            stream.used_up(pair, mark)
                        if rows:
                            freed = evac(j, n0 - n_lo, bank[:, 0:n1 - n0], mark)
                        else:
                            freed = evac((n0 - n_lo) // P + j, bank[:, 0:T], mark)
                        if isinstance(freed, tuple):
                            psum.give(bank, freed)
                        else:
                            later.add(giving_back(bank, freed))
                    later.step()
                if k1 != k_hi:
                    stream.used_up(pair, mark)
                yield

        def linear(name, src, ready, T, evac, rows=None, side=None):
            for _ in linear_steps(name, src, ready, T, evac, rows):
                if side is not None:
                    next(side, None)

        mod_v = mod_t.rearrange("p (l n s) -> p l n s", l=LAYERS2, s=2)
        bg_free = LateRing([(bg_t[:, i * BG_K * BG_N:(i + 1) * BG_K * BG_N].rearrange("p (k n) -> p k n", k=BG_K),
                             bg_in[i]) for i in range(NBG)])
        bg_groups = [(l, g) for l in range(LAYERS2) if l != WIDE_LAYER for g in range(6 * D // BG_N)]
        bg_steps = [(l, g, k) for l, g in bg_groups for k in range(0, KD, BG_K)]
        bg_flight = []
        bg_done = [0]
        bg_bank = []
        bg_tail = []

        def bg_pump():
            while bg_free.free and bg_done[0] + len(bg_flight) < len(bg_steps):
                l, g, k = bg_steps[bg_done[0] + len(bg_flight)]
                (slot, sem), marks = bg_free.take()
                sp.wait(*marks)
                W = io["w_mod"][l].rearrange("(k p) n -> p k n", p=P)
                bg_flight.append((slot, sem, dma(slot, W[:, k:k + BG_K, g * BG_N:(g + 1) * BG_N], sem)))

        def tail_steps(l, g, bank, m):
            rows = scr.take(act)
            act.wait(m)
            m = a_act(rows[0:2, :], bank[0:2, :], ACT.Copy)
            psum.give(bank, m)
            yield
            yield
            pe.wait(m)
            bank = psum.take(pe)
            for j in range(BG_N // P):
                ins = mm(bank[:, 2 * j:2 * j + 2], rows[0:2, j * P:(j + 1) * P], ident[0:2, 0:2])
            m = pe.done(ins)
            scr.give(rows, m)
            yield
            dve.wait(m)
            n, count = g * BG_N // P, BG_N // P
            bias = vec("b_mod", l * 6 * KD + n, count).unsqueeze(2).to_broadcast([P, count, 2])
            sums = bank[:, 0:2 * count].rearrange("p (n s) -> p n s", s=2)
            psum.give(bank, v_tt(mod_v[:, l, n:n + count, :], sums, bias, ALU.add))

        def fill(steps=1):
            for _ in range(steps):
                if bg_tail:
                    tail, turns = bg_tail[0]
                    bg_tail[0] = (tail, turns + 1)
                    next(tail, None)
                    if turns == 3:
                        bg_tail.pop()
                    elif turns == 2:
                        continue
                if bg_done[0] == len(bg_steps):
                    continue
                bg_pump()
                slot, sem, landed = bg_flight.pop(0)
                l, g, k = bg_steps[bg_done[0]]
                bg_done[0] += 1
                if k == 0:
                    bg_bank.append(psum.take(pe))
                pe.wait(landed, silu_ready)
                for i in range(BG_K):
                    ins = mm(bg_bank[0][0:2, :], silu_v[:, k + i, :], slot[:, i, :], start=(k + i == 0),
                             stop=(k + i == KD - 1))
                m = pe.done(ins)
                if k + BG_K == KD:
                    bg_tail.append((tail_steps(l, g, bg_bank.pop(), m), 0))
                bg_free.give((slot, sem), m)
                bg_pump()

        def settle():
            while bg_bank:
                fill(1)
            while bg_tail:
                tail, _ = bg_tail.pop()
                for _ in tail:
                    pass

        def wide_modulation(groups, slots, acc):
            loads = [(g, k) for g in groups for k in range(KD)]
            landed, free, acc_mark = {}, [(), ()], [None, None]

            def load(i):
                if i < len(loads):
                    g, k = loads[i]
                    sp.wait(*free[i % 2])
                    landed[i] = dma(slots[i % 2], io["w_mod"][WIDE_LAYER, k * P:(k + 1) * P, g * WIDE:(g + 1) * WIDE],
                                    wide_in[i % 2])
            load(0)
            load(1)
            for i, (g, k) in enumerate(loads):
                w = slots[i % 2]
                for s_ in range(2):
                    dve.wait(landed[i], silu_ready)
                    if acc_mark[s_]:
                        dve.wait(acc_mark[s_])
                    if k == 0:
                        acc_mark[s_] = v_ts(acc[s_], w, silu_v[:, k, s_:s_ + 1])
                    else:
                        acc_mark[s_] = v_stt(acc[s_], w, silu_v[:, k, s_:s_ + 1], acc[s_], ALU.mult, ALU.add)
                free[i % 2] = (acc_mark[1],)
                load(i + 2)
                yield
                if k == KD - 1:
                    later.until(lambda: psum.free)
                    bank = psum.take(pe)
                    pe.wait(*acc_mark)
                    for n in range(KD):
                        for s_ in range(2):
                            ins = mm(bank[:, 2 * n + s_:2 * n + s_ + 1], acc[s_][:, n * P:(n + 1) * P], ones[:, 0:1])
                    m = pe.done(ins)
                    acc_mark = [m, m]
                    yield
                    dve.wait(m)
                    bias = vec("b_mod", (WIDE_LAYER * 6 + g) * KD, KD).unsqueeze(2).to_broadcast([P, KD, 2])
                    sums = bank[:, 0:2 * KD].rearrange("p (n s) -> p n s", s=2)
                    psum.give(bank, v_tt(mod_v[:, WIDE_LAYER, g * KD:(g + 1) * KD, :], sums, bias, ALU.add))

        def finish_modulation(layer, parts):
            due = [l < layer or (l == layer and g * BG_N < parts * D) for l, g, _ in bg_steps]
            if bg_done[0] <= sum(due) + KD // BG_K:
                fill(sum(due) - bg_done[0])
                while bg_tail:
                    tail, _ = bg_tail.pop()
                    for _ in tail:
                        pass

        class SumSquares:

            def __init__(self, T):
                self.T, self.acc, self.mark = T, None, None

            def add(self, src, *marks):
                for _ in self.steps(src, *marks):
                    pass

            def steps(self, src, *marks):
                while not scr.free:
                    yield
                sq = scr.take(act, dve)
                act.wait(*marks)
                m = a_act(sq[:, 0:self.T], src, ACT.Square)
                yield
                if self.acc is None:
                    self.acc, self.mark = sq, m
                else:
                    dve.wait(m, self.mark)
                    self.mark = v_tt(self.acc[:, 0:self.T], self.acc[:, 0:self.T], sq[:, 0:self.T], ALU.add)
                    scr.give(sq, self.mark)

            def inv_rms(self, mean_scale, group=ones, fills=0):
                later.drain()
                fill(fills)
                return self.inv_rms_now(mean_scale, group)

            def inv_rms_now(self, mean_scale, group=ones):
                T = self.T
                bank = psum.take(pe)
                pe.wait(self.mark)
                m = pe.done(mm(bank[:, 0:T], group, self.acc[:, 0:T]))
                scr.give(self.acc, m)
                r = scr.take(act)
                act.wait(m)
                m = a_act(r[:, 0:T], bank[:, 0:T], ACT.Ln, bias=eps, scale=mean_scale)
                psum.give(bank, m)
                act.chain()
                return r, a_act(r[:, 0:T], r[:, 0:T], ACT.Exp, scale=-0.5)

        def squares_of(src, ready, T):
            sums = SumSquares(T)
            for k in range(KD):
                later.add(sums.steps(src(k), ready[k]))
                later.step()
            return sums

        def rms(sums, src, gain, out, T, fills=2):
            r, m = sums.inv_rms(1.0 / D, fills=fills)
            marks, left = [None] * KD, [KD]

            def chunk(k):
                while not scr.free:
                    yield
                t = scr.take(dve)
                dve.wait(m)
                scaled = v_stt(t[:, 0:T], src(k), gain(k), r[:, 0:T], ALU.mult, ALU.mult)
                left[0] -= 1
                if not left[0]:
                    scr.give(r, scaled)
                marks[k] = yield from cut_steps(out[0][:, k, 0:T], out[1][:, k, 0:T], t[:, 0:T], scaled)
                scr.give(t, marks[k])
            for k in range(KD):
                later.add(chunk(k))
                later.step()
            fill(fills // 2)
            return marks

        def sigmoid_steps(out, src, m, scale=1.0):
            dve.wait(m)
            m = v_ts(out, src, -44.0 / scale, op0=ALU.max)
            yield
            act.wait(m)
            m = a_act(out, out, ACT.Exp, scale=-scale)
            yield
            act.wait(m)
            m = a_act(out, out, ACT.Ln, bias=con("one"))
            yield
            act.wait(m)
            return a_act(out, out, ACT.Exp, scale=-1.0)

        def silu_steps(out, src, m, T):
            while not scr.free:
                yield
            t = scr.take(act, dve)
            m = yield from sigmoid_steps(t[:, 0:T], src, m)
            yield
            dve.wait(m)
            m = v_tt(out, src, t[:, 0:T], ALU.mult)
            scr.give(t, m)
            return m

        def at_once(steps):
            while True:
                try:
                    next(steps)
                except StopIteration as end:
                    return end.value

        def sigmoid(out, src, m, scale=1.0):
            return at_once(sigmoid_steps(out, src, m, scale))

        def silu_into(out, src, m, T):
            return at_once(silu_steps(out, src, m, T))

        class Attention:

            def __init__(self, units, scale):
                self.units, self.scale, self.open, self.turned = units, scale, [], []

            def scores(self, u):
                bank = psum.take(pe)
                nk = u["nk"]
                pe.wait(*u["ready"])
                for i, (q, k) in enumerate(u["pairs"]):
                    ins = mm(bank[:, 0:nk], q, k, start=(i == 0), stop=(i == len(u["pairs"]) - 1))
                m = pe.done(ins)
                probs = scr.take(dve, act)
                stats = small.take(dve, act)
                src = bank[:, 0:nk]
                dve.wait(m)
                if u["causal"]:
                    if nk > P:
                        v_ts(probs[:, 0:nk - P], bank[:, 0:nk - P], 1.0)
                    m = v_tt(probs[:, nk - P:nk], bank[:, nk - P:nk], con("causal"), ALU.add)
                    psum.give(bank, m)
                    dve.chain()
                    src = probs[:, 0:nk]
                dve.done(nc.vector.tensor_reduce(stats[:, 0:1], src, AX_X, ALU.max))
                dve.chain()
                m = v_ts(stats[:, 1:2], stats[:, 0:1], -self.scale)
                act.wait(m)
                m = a_act(probs[:, 0:nk], src, ACT.Exp, bias=stats[:, 1:2], scale=self.scale, accum=stats[:, 2:3])
                if not u["causal"]:
                    psum.give(bank, m)
                dve.wait(m)
                dve.done(nc.vector.reciprocal(stats[:, 3:4], stats[:, 2:3]))
                dve.chain()
                m = v_ts(probs[:, 0:nk], probs[:, 0:nk], stats[:, 3:4])
                small.give(stats, m)
                self.open.append((u, probs, m))

            def turn(self):
                u, probs, m = self.open.pop(0)
                nk = u["nk"]
                bank = psum.take(pe)
                pe.wait(m)
                for t in range(nk // P):
                    ins = nc.tensor.transpose(bank[:, t * P:(t + 1) * P], probs[:, t * P:(t + 1) * P], ident)
                m = pe.done(ins)
                scr.give(probs, m)
                turned = scr.take(act)
                act.wait(m)
                m = a_act(turned[:, 0:nk], bank[:, 0:nk], ACT.Copy)
                psum.give(bank, m)
                self.turned.append((u, turned, m))

            def finish(self):
                u, turned, m = self.turned.pop(0)
                nk = u["nk"]
                out = psum.take(pe)
                pe.wait(m)
                for o_rows, values, dst, part in u["outs"]:
                    for t in range(nk // P):
                        ins = mm(out[o_rows, part * P:(part + 1) * P], values(t), turned[:, t * P:(t + 1) * P],
                                 start=(t == 0), stop=(t == nk // P - 1))
                m = pe.done(ins)
                scr.give(turned, m)
                m2 = cut_all([(dst[0], dst[1], out[o_rows, part * P:(part + 1) * P])
                              for o_rows, _, dst, part in u["outs"]], m)
                psum.give(out, m2)

            def run(self, lag=3, behind=2, every=1):
                for i in range(len(self.units) + lag + behind):
                    if i < len(self.units):
                        self.scores(self.units[i])
                    if lag <= i < len(self.units) + lag:
                        self.turn()
                    if i >= lag + behind:
                        self.finish()
                    if i % every == 0:
                        fill(1)
                return dve.last()

        def add_to_x(sums, gate=None, bias=None):
            def evac(n, bank, m):
                T = bank.shape[-1]
                src, freed = bank, None
                if bias is not None:
                    t = scr.take(act)
                    act.wait(m)
                    m = freed = a_act(t[:, 0:T], bank, ACT.Identity, bias=bias(n))
                    src = t
                dve.wait(m)
                if gate is None:
                    m = v_tt(x[:, n, 0:T], src[:, 0:T], x[:, n, 0:T], ALU.add)
                else:
                    for s0 in range(0, T, S):
                        m = v_stt(x[:, n, s0:s0 + S], src[:, s0:s0 + S], gate(n, s0 // S), x[:, n, s0:s0 + S],
                                  ALU.mult, ALU.add)
                if bias is not None:
                    scr.give(t, m)
                if sums is not None:
                    def squares():
                        yield
                        yield from sums.steps(x[:, n, 0:sums.T], m)
                    later.add(squares())
                return freed or m
            return evac

        def copy_to(dst, marks=None, scale=1.0):
            def evac(n, bank, m):
                act.wait(m)
                m = a_act(dst(n), bank, ACT.Copy, scale=scale)
                if marks is not None:
                    marks.append(m)
                return m
            return evac

        def rows_to(dst):
            def evac(j, n, bank, m):
                act.wait(m)
                return a_act(dst[:, j, n:n + bank.shape[-1]], bank, ACT.Copy)
            return evac

        def conv_steps(out, bank, m, taps, T):
            act.wait(m)
            m = a_act(out, bank, ACT.Copy, scale=taps[0])
            for j in range(1, len(taps)):
                yield
                dve.wait(m)
                m = v_stt(out[:, j:T], bank[:, 0:T - j], taps[j], out[:, j:T], ALU.mult, ALU.add)
            return m

        def hx(k):
            return x[:, k, 0:S]

        silu_v = silu_c.rearrange("p (k s) -> p k s", s=2)
        silu_ready = silu_into(silu_c, vec("c", 0, 2 * KD), vec_in, 2 * KD)

        mem_t, memn = x[:, :, S:T2], [half[:, :, S:T2] for half in xn]
        stream.pump()
        mem_in = dma(mem_t, io["memT"], in_sem[5])
        xn_ready = rms(squares_of(hx, [x_in[k // 2] for k in range(KD)], S), hx, lambda k: vec("norm_mix", k), xn, S,
                       fills=0)

        for layer in range(2):
            st = ExitStack()
            mix = halves(st, f"mix{layer}", KD, S)
            mix_ready = [None] * KD
            if layer == 0:
                qk = tiles(st, "qk", KD, S)
                v = tiles(st, "v", 2, A_WIDTH)
                p = tiles(st, "p", 4, S)
                pool_w = tiles(st, "pool_w", 4, P)
                pool_inv = tile(st, "pool_inv", 4 * S)
                fence()
                pool_w_in = stage_load(pool_w, io["pool_w"], 6)
                at, n = CON["pool_inv"]
                pool_inv_in = stage_load(pool_inv, io["con"][:, at:at + n], 7)
                linear("ev_w_in", xn, xn_ready, S, copy_to(lambda n: qk[:, n, :]))
                linear("ev_w_in", xn, xn_ready, S, rows_to(v), rows=2)
                qkv_ready = act.last()
                linear("ev_w_in", xn, xn_ready, S, copy_to(lambda n: p[:, n, :]))
                p_ready = act.last()
                memn_ready = rms(squares_of(lambda k: mem_t[:, k, :], [mem_in] * KD, S), lambda k: mem_t[:, k, :],
                                 lambda k: vec("mem_norm", k), memn, S, fills=0)
                units = []
                for h in range(MOBA_HEADS):
                    part = slice(HD * (h % 2), HD * (h % 2) + HD)
                    for qt in range(2):
                        tok = slice(qt * P, (qt + 1) * P)
                        units.append(dict(nk=(qt + 1) * P, causal=True, ready=[qkv_ready],
                                          pairs=[(qk[part, h // 2, tok], qk[part, 4 + h // 2, 0:(qt + 1) * P])],
                                          outs=[(part, (lambda t, h=h: v[:, t, h * HD:(h + 1) * HD]),
                                                 [half[part, h // 2, tok] for half in mix], 0)]))
                attended = Attention(units, HD ** -0.5).run()
                for n in range(4):
                    mix_ready[n] = attended
                dve.wait(p_ready, pool_inv_in)
                pooled = []
                for g, w in enumerate(POOL_WINDOWS):
                    a, b = scr.take(dve), scr.take(dve)
                    src = p[:, g, :]
                    step = 1
                    while step < w:
                        v_ts(b[:, 0:step], src[:, 0:step], 1.0)
                        v_tt(b[:, step:S], src[:, step:S], src[:, 0:S - step], ALU.add)
                        dve.chain()
                        src, a, b = b[:, 0:S], b, a
                        step *= 2
                    v_tt(b[:, 0:S], src, pool_inv[:, g * S:(g + 1) * S], ALU.mult)
                    dve.chain()
                    m = v_tt(b[:, 0:S], b[:, 0:S], p[:, g, :], ALU.subtract)
                    scr.give(a, m)
                    pooled.append((b, m))
                fill(3)
                for g, (b, m) in enumerate(pooled):
                    bank = psum.take(pe)
                    pe.wait(m, pool_w_in)
                    m = pe.done(mm(bank[:, 0:S], pool_w[:, g, :], b[:, 0:S]))
                    dve.wait(m)
                    m = v_ts(b[:, 0:S], bank[:, 0:S], vec("pool_scale", g))
                    psum.give(bank, m)
                    mix_ready[4 + g] = cut(mix[0][:, 4 + g, :], mix[1][:, 4 + g, :], b[:, 0:S], m)
                    scr.give(b, mix_ready[4 + g])
            else:
                sgu = ExitStack()
                ab = tile(st, "ab", 16)
                beta, decay = tile(st, "beta", 8), tile(st, "decay", 8)
                u = tiles(sgu, "u", 4, S)
                vr = tiles(sgu, "vr", 2, SGU_WIDTH)
                sgu_w = tiles(sgu, "sgu_w", 4, P)
                sgu_row = tile(sgu, "sgu_row", NROW)
                fence()
                sgu_in = stage_load(sgu_w, io["sgu_wT"], 8)
                row_in = stage_load(sgu_row, io["row"], 9)

                def row(name, i=0, n=None):
                    at, size = ROW[name]
                    return sgu_row[:, at + i:at + (size if n is None else i + n)]

                def gelu(out, bank, m, T, ready, n):
                    while len(scr.free) < 2:
                        yield
                    raw, t = scr.take(act), scr.take(act, dve)
                    act.wait(m)
                    m = a_act(raw[:, 0:T], bank, ACT.Copy)
                    yield m
                    act.wait(m)
                    m = a_act(t[:, 0:T], raw[:, 0:T], ACT.Square)
                    yield
                    dve.wait(m)
                    m = v_ts(t[:, 0:T], t[:, 0:T], 0.044715, 1.0, ALU.mult, ALU.add)
                    yield
                    dve.wait(m)
                    m = v_tt(t[:, 0:T], t[:, 0:T], raw[:, 0:T], ALU.mult)
                    m = yield from sigmoid_steps(t[:, 0:T], t[:, 0:T], m, scale=2.0 * float(np.sqrt(2.0 / np.pi)))
                    yield
                    dve.wait(m)
                    ready[n] = v_tt(out, t[:, 0:T], raw[:, 0:T], ALU.mult)
                    scr.give(raw, ready[n])
                    scr.give(t, ready[n])

                u_ready, vr_ready = [None] * 4, [None] * 2

                def evac_u(n, bank, m):
                    return gelu(u[:, n, :], bank, m, S, u_ready, n)

                def evac_vr(j, n, bank, m):
                    return gelu(vr[:, j, n:n + 512], bank, m, 512, vr_ready, j)
                linear("od_w_in", xn, xn_ready, S, evac_u)
                linear("od_w_in", xn, xn_ready, S, evac_vr, rows=2)

                def evac_ab(j, n, bank, m):
                    act.wait(m)
                    return a_act(ab[:, j * 8:(j + 1) * 8], bank, ACT.Copy)
                linear("od_w_in", xn, xn_ready, S, evac_ab, rows=2)

                later.drain()

                def small_steps():
                    neg_a, tmp, tmp2 = (small.take(act, dve) for _ in range(3))
                    a_act(neg_a[:, 0:4], vec("a_log", 0, DN_HEADS), ACT.Exp)
                    for j in range(2):
                        braw, araw = ab[:, j * 8:j * 8 + 4], ab[:, j * 8 + 4:j * 8 + 8]
                        bj, gj = beta[:, j * 4:j * 4 + 4], decay[:, j * 4:j * 4 + 4]
                        dve.wait(sigmoid(bj, braw, act.last()))
                        v_tt(gj, araw, vec("dt_bias", 0, DN_HEADS), ALU.add)
                        act.wait(dve.last())
                        act.chain()
                        a_act(tmp[:, 0:4], gj, ACT.Abs)
                        act.chain()
                        a_act(tmp[:, 0:4], tmp[:, 0:4], ACT.Exp, scale=-1.0)
                        act.chain()
                        m = a_act(tmp2[:, 0:4], tmp[:, 0:4], ACT.Ln, bias=con("one"))
                        dve.wait(m)
                        dve.chain()
                        v_stt(gj, gj, 0.0, tmp2[:, 0:4], ALU.max, ALU.add)
                        dve.chain()
                        m = v_stt(gj, gj, -1.0, neg_a[:, 0:4], ALU.mult, ALU.mult)
                        act.wait(m)
                        yield
                    for s_ in (neg_a, tmp, tmp2):
                        small.give(s_, m)
                    for j in range(2):
                        s_ = small.take(dve, act)
                        c0 = scr.take(act, dve)
                        dve.wait(vr_ready[j], row_in)
                        dve.done(nc.vector.tensor_reduce(s_[:, 0:1], vr[:, j, :], AX_X, ALU.add))
                        dve.chain()
                        v_ts(s_[:, 1:2], s_[:, 0:1], -1.0 / SGU_WIDTH)
                        dve.chain()
                        m = v_ts(vr[:, j, :], vr[:, j, :], s_[:, 1:2], op0=ALU.add)
                        act.wait(m)
                        a_act(c0, vr[:, j, :], ACT.Square, accum=s_[:, 2:3])
                        act.chain()
                        a_act(s_[:, 3:4], s_[:, 2:3], ACT.Ln, bias=eps, scale=1.0 / SGU_WIDTH)
                        act.chain()
                        m = a_act(s_[:, 4:5], s_[:, 3:4], ACT.Exp, scale=-0.5)
                        scr.give(c0, m)
                        yield
                        dve.wait(m)
                        v_stt(vr[:, j, :], vr[:, j, :], s_[:, 4:5], row("sgu_ln_g"), ALU.mult, ALU.mult)
                        dve.chain()
                        m = v_tt(vr[:, j, :], vr[:, j, :], row("sgu_ln_b"), ALU.add)
                        small.give(s_, m)
                        vr_ready[j] = m
                    dve.wait(sgu_in)
                    m = v_tt(sgu_w, sgu_w, con("upto").unsqueeze(1).to_broadcast([P, 4, P]), ALU.mult)
                    yield
                    pe.wait(m)
                    for g in range(4):
                        bank = psum.take(pe)
                        for j in range(2):
                            ins = mm(bank[:, j * P:(j + 1) * P], vr[:, j, g * P:(g + 1) * P], sgu_w[:, g, :])
                        m = pe.done(ins)
                        t = scr.take(dve)
                        dve.wait(m)
                        for j in range(2):
                            m = v_tt(t[:, j * P:(j + 1) * P], bank[:, j * P:(j + 1) * P], row("sgu_b", g * P, P),
                                     ALU.add)
                        psum.give(bank, m)
                        dve.chain()
                        m = v_tt(t[:, 0:S], t[:, 0:S], u[:, g, :], ALU.mult)
                        mix_ready[g] = cut(mix[0][:, g, :], mix[1][:, g, :], t[:, 0:S], m)
                        scr.give(t, mix_ready[g])
                        yield
                for _ in small_steps():
                    fill(1)
                beta_ready = act.last()
                sgu.close()

                dqkv = tiles(st, "dqkv", 12, S)
                gate = tiles(st, "gate", 4, S)
                fence()
                d_ready = [None] * 12

                def conv_silu_norm(n, bank, m):
                    out = dqkv[:, n, :]
                    m = yield from conv_steps(out, bank, m, [vec("dn_conv", (DN_CONV - 1 - j) * 12 + n)
                                                             for j in range(DN_CONV)], S)
                    yield m
                    m = yield from silu_steps(out, out, m, S)
                    if n < 8:
                        yield
                        sums = SumSquares(S)
                        yield from sums.steps(out, m)
                        while not (scr.free and psum.free):
                            yield
                        r, m = sums.inv_rms_now(1.0)
                        yield
                        yield
                        dve.wait(m)
                        m = v_stt(out, out, (P ** -0.5) if n < 4 else 1.0, r[:, 0:S], ALU.mult, ALU.mult)
                        scr.give(r, m)
                    d_ready[n] = m

                def gate_silu(n, bank, m):
                    m = yield from silu_steps(gate[:, n, :], bank, m, S)
                    yield m
                linear("od_w_in", xn, xn_ready, S, conv_silu_norm)
                linear("od_w_in", xn, xn_ready, S, gate_silu)
                later.drain()
                gate_ready = dve.last()

                H4 = DN_HEADS * P
                delta = ExitStack()
                (eG, bB, AT, QK, Tm, TT, Xm, LT, vb, kg, kd, qd, state, spread) = (
                    tile(delta, name, H4) for name in ("eG", "bB", "AT", "QK", "Tm", "TT", "Xm", "LT", "vb", "kg", "kd",
                                                       "qd", "state", "spread"))
                o_raw = tiles(delta, "o_raw", 4, S)
                level = tile(delta, "level", P * len(INV_LEVELS))
                gcol = small.take(dve, act)
                fence()
                at, n = CON["level"]
                level_in = stage_load(level, io["con"][:, at:at + n], 10)

                def h_(t, h):
                    return t[:, h * P:(h + 1) * P]

                def by_head(t):
                    return t.rearrange("p (h t) -> p h t", h=DN_HEADS)

                def all_heads(t):
                    return t.unsqueeze(1).to_broadcast([P, DN_HEADS, P])

                def spread_columns(src):
                    for h in range(DN_HEADS):
                        m = v_ts(h_(spread, h), ones, src[:, h:h + 1])
                    return m

                for n in range(2):
                    tok = slice(n * P, (n + 1) * P)
                    if n:
                        fence()
                    dve.wait(beta_ready)
                    m = spread_columns(decay[:, n * 4:n * 4 + 4])
                    pe.wait(m)
                    bank, bank2 = psum.take(pe), psum.take(pe)
                    for h in range(DN_HEADS):
                        mm(h_(bank, h), h_(spread, h), con("upto"))
                    m = pe.done(mm(bank2[:, 0:4], con("upto"), decay[:, n * 4:n * 4 + 4]))
                    fill(1)
                    act.wait(m)
                    m = a_act(gcol[:, 0:4], bank2[:, 0:4], ACT.Copy)
                    psum.give(bank2, m)
                    m2 = a_act(eG, bank, ACT.Exp)
                    dve.wait(m, m2)
                    for h in range(DN_HEADS):
                        v_ts(h_(LT, h), h_(bank, h), gcol[:, h:h + 1], 0.0, ALU.subtract, ALU.min)
                    last_col = by_head(bank)[:, :, P - 1:P].rearrange("p h o -> p (h o)")
                    kdc, egc = small.take(dve, act), small.take(dve, act)
                    m = v_tt(kdc[:, 0:4], last_col, gcol[:, 0:4], ALU.subtract)
                    psum.give(bank, m)
                    act.wait(m)
                    a_act(LT, LT, ACT.Exp)
                    act.chain()
                    a_act(kdc[:, 0:4], kdc[:, 0:4], ACT.Exp)
                    m3 = a_act(egc[:, 0:4], gcol[:, 0:4], ACT.Exp)
                    dve.wait(m)
                    m = spread_columns(beta[:, n * 4:n * 4 + 4])
                    pe.wait(m)
                    bank = psum.take(pe)
                    for h in range(DN_HEADS):
                        ins = mm(h_(bank, h), h_(spread, h), ident)
                    m = pe.done(ins)
                    act.wait(m)
                    m = a_act(bB, bank, ACT.Copy)
                    psum.give(bank, m)
                    dve.wait(m3, m)
                    v_tt(by_head(LT), by_head(LT), all_heads(con("upto")), ALU.mult)
                    bank, bank2 = psum.take(pe), psum.take(pe)
                    pe.wait(*d_ready)
                    for h in range(DN_HEADS):
                        mm(h_(bank, h), dqkv[:, 4 + h, tok], dqkv[:, 4 + h, tok])
                    for h in range(DN_HEADS):
                        ins = mm(h_(bank2, h), dqkv[:, 4 + h, tok], dqkv[:, h, tok])
                    m = pe.done(ins)
                    dve.wait(m)
                    dve.chain()
                    v_tt(AT, bank, LT, ALU.mult)
                    m = v_tt(QK, bank2, LT, ALU.mult)
                    psum.give(bank, m)
                    psum.give(bank2, m)
                    dve.chain()
                    v_tt(AT, AT, bB, ALU.mult)
                    v_tt(by_head(qd), dqkv[:, 0:4, tok], by_head(eG), ALU.mult)
                    bank, bank2 = psum.take(pe), psum.take(pe)
                    for h in range(DN_HEADS):
                        nc.tensor.transpose(h_(bank, h), dqkv[:, 8 + h, tok], ident)
                        ins = nc.tensor.transpose(h_(bank2, h), dqkv[:, 4 + h, tok], ident)
                    turned = pe.done(ins)

                    def scaled_rows(vbank, kbank):
                        dve.wait(turned)
                        for h in range(DN_HEADS):
                            bcol = beta[:, n * 4 + h:n * 4 + h + 1]
                            v_ts(h_(vb, h), h_(vbank, h), bcol)
                            v_ts(h_(kg, h), h_(kbank, h), bcol, egc[:, h:h + 1], ALU.mult, ALU.mult)
                            m = v_ts(h_(kd, h), h_(kbank, h), kdc[:, h:h + 1])
                            yield
                        psum.give(vbank, m)
                        psum.give(kbank, m)
                        small.give(kdc, m)
                        small.give(egc, m)
                    rows_steps = scaled_rows(bank, bank2)
                    dve.wait(level_in)

                    def level_part(li):
                        lev = all_heads(level[:, li * P:(li + 1) * P])
                        out = (LT, bB)[li % 2]
                        dve.chain()
                        return out, v_tt(by_head(out), by_head(AT), lev, ALU.mult)
                    ahead = level_part(0)
                    for li, s_ in enumerate(INV_LEVELS):
                        part_T, m = ahead
                        if li + 1 < len(INV_LEVELS):
                            ahead = level_part(li + 1)
                        if s_ == 1:
                            dve.wait(m)
                            m = v_tt(by_head(TT), all_heads(ident), by_head(part_T), ALU.subtract)
                            bank = psum.take(pe)
                            pe.wait(m)
                            for h in range(DN_HEADS):
                                ins = nc.tensor.transpose(h_(bank, h), h_(TT, h), ident)
                            m = pe.done(ins)
                            act.wait(m)
                            T_ready = a_act(Tm, bank, ACT.Copy)
                            psum.give(bank, T_ready)
                            continue
                        bank = psum.take(pe)
                        pe.wait(m, T_ready)
                        for h in range(DN_HEADS):
                            ins = mm(h_(bank, h), h_(part_T, h), h_(Tm, h))
                        m = pe.done(ins)
                        act.wait(m)
                        m = a_act(Xm, bank, ACT.Copy)
                        psum.give(bank, m)
                        pe.wait(m)
                        bank, bank2 = psum.take(pe), psum.take(pe)
                        for h in range(DN_HEADS):
                            mm(h_(bank, h), h_(TT, h), h_(Xm, h))
                        for h in range(DN_HEADS):
                            ins = mm(h_(bank2, h), h_(Xm, h), h_(TT, h))
                        m = pe.done(ins)
                        fill(1)
                        dve.wait(m)
                        v_stt(TT, bank2, -1.0, TT, ALU.mult, ALU.add)
                        T_ready = v_stt(Tm, bank, -1.0, Tm, ALU.mult, ALU.add)
                        psum.give(bank, T_ready)
                        psum.give(bank2, T_ready)
                        next(rows_steps, None)
                    pe.wait(T_ready, dve.last())
                    bank, bank2 = psum.take(pe), psum.take(pe)
                    for h in range(DN_HEADS):
                        mm(h_(bank, h), h_(TT, h), h_(vb, h))
                    for h in range(DN_HEADS):
                        ins = mm(h_(bank2, h), h_(kg, h), h_(TT, h))
                    m = pe.done(ins)
                    new_v = scr.take(act, dve)
                    act.wait(m)
                    if n == 0:
                        m = a_act(new_v, bank, ACT.Copy)
                        psum.give(bank, m)
                        psum.give(bank2, m)
                        pe.wait(m)
                    else:
                        Um, wT = scr.take(act), scr.take(act)
                        a_act(Um, bank, ACT.Copy)
                        m = a_act(wT, bank2, ACT.Copy)
                        psum.give(bank, m)
                        psum.give(bank2, m)
                        bank = psum.take(pe)
                        pe.wait(m, state_ready)
                        for h in range(DN_HEADS):
                            ins = mm(h_(bank, h), h_(wT, h), h_(state, h))
                        m = pe.done(ins)
                        scr.give(wT, m)
                        dve.wait(m, act.last())
                        m = v_stt(new_v, bank, -1.0, Um, ALU.mult, ALU.add)
                        scr.give(Um, m)
                        psum.give(bank, m)
                        pe.wait(m)
                    bank = psum.take(pe)
                    for h in range(DN_HEADS):
                        if n:
                            mm(h_(bank, h), h_(state, h), h_(qd, h), start=True, stop=False)
                        ins = mm(h_(bank, h), h_(new_v, h), h_(QK, h), start=(n == 0), stop=True)
                    m = pe.done(ins)
                    act.wait(m)
                    o_ready = a_act(o_raw[:, :, tok], by_head(bank), ACT.Copy)
                    psum.give(bank, o_ready)
                    if n == 0:
                        bank = psum.take(pe)
                        for h in range(DN_HEADS):
                            ins = mm(h_(bank, h), h_(kd, h), h_(new_v, h))
                        m = pe.done(ins)
                        act.wait(m)
                        state_ready = a_act(state, bank, ACT.Copy)
                        psum.give(bank, state_ready)
                    scr.give(new_v, m)
                small.give(gcol, dve.last(), act.last())
                normed = []
                for h in range(DN_HEADS):
                    sums = SumSquares(S)
                    sums.add(o_raw[:, h, :], o_ready)
                    normed.append(sums)
                normed = [sums.inv_rms(1.0 / P) for sums in normed]
                fill(2)
                for h, (r, m) in enumerate(normed):
                    dve.wait(m, gate_ready)
                    v_stt(r[:, 0:S], o_raw[:, h, :], vec("dn_norm_g"), r[:, 0:S], ALU.mult, ALU.mult)
                    dve.chain()
                    m = v_tt(r[:, 0:S], r[:, 0:S], gate[:, h, :], ALU.mult)
                    mix_ready[4 + h] = cut(mix[0][:, 4 + h, :], mix[1][:, 4 + h, :], r[:, 0:S], m)
                    scr.give(r, mix_ready[4 + h])
                delta.close()
            sums = SumSquares(S)
            linear(("ev_w_out", "od_w_out")[layer], mix, mix_ready, S, add_to_x(sums))
            st.close()

            st = ExitStack()
            oT = halves(st, f"oT{layer}", KD, S)
            kT, qT = tiles(st, f"kT{layer}", KD, S), tiles(st, f"qT{layer}", KD, S)
            vm = tiles(st, f"vm{layer}", 2, D)
            fence()
            linear("xattn_wkv", memn, memn_ready, S, copy_to(lambda n: kT[:, n, :]))
            xn_ready = rms(sums, hx, lambda k: vec("norm_xattn", layer * KD + k), xn, S)
            linear("xattn_wkv", memn, memn_ready, S, rows_to(vm), rows=2)
            linear("xattn_wq", xn, xn_ready, S, copy_to(lambda n: qT[:, n, :]))
            qkv_ready = act.last()
            units = []
            for h in range(X_HEADS):
                for qt in range(2):
                    tok = slice(qt * P, (qt + 1) * P)
                    units.append(dict(nk=S, causal=False, ready=[qkv_ready],
                                      pairs=[(qT[:, 2 * h + i, tok], kT[:, 2 * h + i, :]) for i in range(2)],
                                      outs=[(slice(0, P), (lambda t, c=2 * h + i: vm[:, t, c * P:(c + 1) * P]),
                                             [half[:, 2 * h + i, tok] for half in oT], i) for i in range(2)]))
            attended = Attention(units, S ** -0.5).run()
            sums = SumSquares(S)
            linear("xattn_wo", oT, [attended] * KD, S, add_to_x(sums))
            st.close()

            xn_ready = rms(sums, hx, lambda k: vec("norm_ffn", layer * KD + k), xn, S)
            st = ExitStack()
            hid = halves(st, f"hid{layer}", FC, S)
            gated = tiles(st, f"gated{layer}", 4, S)
            fence()
            hid_ready = [None] * FC

            def conv_taps(c):
                return [vec("ffn_conv", (layer * FFN_CONV + FFN_CONV - 1 - j) * 2 * FC + c) for j in range(FFN_CONV)]

            gated_ready, gated_read = [None] * 4, [pe.last()] * 4

            def gate_steps(n, c, bank, m):
                g = gated[:, n, :]
                act.wait(gated_read[n])
                m = yield from conv_steps(g, bank, m, conv_taps(c), S)
                yield m
                gated_ready[n] = yield from silu_steps(g, g, m, S)

            def up_steps(n, c, bank, m):
                while not scr.free:
                    yield
                t = scr.take(act, dve)
                m = yield from conv_steps(t[:, 0:S], bank, m, conv_taps(FC + c), S)
                yield m
                dve.wait(m, gated_ready[n])
                m = gated_read[n] = v_tt(t[:, 0:S], gated[:, n, :], t[:, 0:S], ALU.mult)
                yield
                hid_ready[c] = yield from cut_steps(hid[0][:, c, :], hid[1][:, c, :], t[:, 0:S], m)
                scr.give(t, hid_ready[c])

            for n0 in range(0, FC, 4):
                def evac_gate(n, bank, m, n0=n0):
                    return gate_steps(n, n0 + n, bank, m)

                def evac_up(n, bank, m, n0=n0):
                    return up_steps(n, n0 + n, bank, m)
                linear("ffn_w_up", xn, xn_ready, S, evac_gate)
                linear("ffn_w_up", xn, xn_ready, S, evac_up)
            sums = SumSquares(S)
            linear("ffn_w_down", hid, hid_ready, S, add_to_x(sums))
            st.close()
            if layer == 0:
                xn_ready = rms(sums, hx, lambda k: vec("norm_mix", KD + k), xn, S)

        sp.wait(dve.last())
        ctx_in = dma(x[:, :, S:T2], io["ctxT"], in_sem[3])
        r, m = sums.inv_rms(1.0 / D)
        fill(2)
        dve.wait(m)
        sums = SumSquares(T2)
        for k in range(KD):
            m = v_stt(hx(k), hx(k), vec("final_norm", k), r[:, 0:S], ALU.mult, ALU.mult)
            if k == KD - 1:
                scr.give(r, m)
            sums.add(x[:, k, :], m, ctx_in)

        def modulated(sums, layer, gains, shift, scale, T):
            r, m = sums.inv_rms(1.0 / D, fills=3)
            finish_modulation(layer, scale + 2)
            mA = modA.rearrange("p (k s) -> p k s", s=2)
            dve.chain()
            for s_ in range(T // S):
                v_stt(mA[:, :, s_], mod_v[:, layer, scale * KD:(scale + 1) * KD, s_], 1.0,
                      vec(gains, layer * KD, KD), ALU.add, ALU.mult)
            dve.wait(m)
            dve.chain()
            marks, left = [None] * KD, [KD]
            streams = [slice(s_ * S, (s_ + 1) * S) for s_ in range(T // S)]

            def chunk(k, m):
                while not scr.free:
                    yield
                t = scr.take(dve)
                add = [mod_v[:, layer, shift * KD + k, s_:s_ + 1] for s_ in range(T // S)]
                dve.wait(m)
                for s_, c in enumerate(streams):
                    m = v_stt(t[:, c], x[:, k, c], mA[:, k, s_:s_ + 1], r[:, c], ALU.mult, ALU.mult)
                left[0] -= 1
                if not left[0]:
                    scr.give(r, m)
                yield
                act.wait(m)
                for s_, c in enumerate(streams):
                    m = a_act(xn[0][:, k, c], t[:, c], ACT.Identity, bias=add[s_])
                yield
                dve.wait(m)
                for s_, c in enumerate(streams):
                    m = v_stt(xn[1][:, k, c], t[:, c], add[s_], xn[0][:, k, c].bitcast(F32), ALU.add, ALU.subtract)
                marks[k] = m
                scr.give(t, m)
            for k in range(KD):
                later.add(chunk(k, m))
                later.step()
            fill(2)
            return marks

        def gate_of(layer, which):
            return lambda n, s_: mod_v[:, layer, which * KD + n, s_:s_ + 1]

        for layer in range(LAYERS2):
            last_layer = layer == LAYERS2 - 1
            TO = S if last_layer else T2
            xn_ready = modulated(sums, layer, "g_norm_mix", 0, 1, T2)
            sums = SumSquares(TO)
            st = ExitStack()
            if layer % 3 == 0:
                g = layer // 3
                name = f"gla{g}_"
                oT = tiles(st, name + "o", KD, T2)
                inner = ExitStack()
                qT, kT = tiles(inner, name + "q", 4, T2), tiles(inner, name + "k", 4, T2)
                vr = tiles(inner, name + "v", 4, D)
                sets = [[tiles(inner, f"{name}set{i}{d}", 3, T2) for d in range(2)] for i in range(2)]
                states = [tile(inner, f"{name}state{d}", GLA_DV) for d in range(2)]
                low = tile(inner, name + "low", T2)
                g2 = tile(inner, name + "g2", 512)
                restart = tile(inner, name + "restart", T2)
                masks = tile(inner, name + "masks", 2 * GLA_C)
                masked = [tile(inner, f"{name}masked{i}", GLA_C) for i in range(4)]
                e_last = tile(inner, name + "e_last", 4 * 8)
                totals = tile(inner, name + "totals", 4 * 8)
                fence()
                g2_in = stage_load(g2[0:32 + GLA_RANK, :], io["gla_w_g2"][g], 11)
                at, n = CON["restart"]
                restart_in = stage_load(restart, io["con"][:, at:at + n], 12)
                at, n = CON["gla_mask"]
                masks_in = stage_load(masks, io["con"][:, at:at + n], 13)
                linear("gla_w_in", xn, xn_ready, TO, copy_to(lambda n: qT[:, n, 0:TO], scale=GLA_DK ** -0.5))
                linear("gla_w_in", xn, xn_ready, T2, copy_to(lambda n: kT[:, n, :]))
                linear("gla_w_g1", xn, xn_ready, T2, copy_to(lambda n: low))
                low_ready = act.last()

                def prepare(h):
                    pe.wait(low_ready, g2_in)
                    dve.wait(restart_in)
                    for d in range(2):
                        qb, kb, kd = (sets[h % 2][d][:, i, :] for i in range(3))
                        slot = (h % 2) * 2 + d
                        bank = psum.take(pe)
                        rank = slice(32 * d, 32 * d + GLA_RANK)
                        m = pe.done(mm(bank, g2[rank, h * P:(h + 1) * P], low[rank, :]))
                        z, a, b = scr.take(act, dve), scr.take(act, dve), scr.take(act, dve)
                        bias = vec("gla_b_g", (g * 2 + d) * 4 + h)
                        act.wait(m)
                        a_act(z, bank, ACT.Identity, bias=bias)
                        m = a_act(a, bank, ACT.Abs, bias=bias)
                        psum.give(bank, m)
                        act.chain()
                        a_act(a, a, ACT.Exp, scale=-1.0)
                        act.chain()
                        m = a_act(a, a, ACT.Ln, bias=con("one"))
                        yield
                        dve.wait(m)
                        v_stt(z, z, 0.0, a, ALU.min, ALU.subtract)
                        dve.chain()
                        v_ts(z, z, 1.0 / GLA_TAU)
                        dve.chain()
                        bc, zc = (t.rearrange("p (c t) -> p c t", t=GLA_C) for t in (b, z))
                        dve.done(nc.vector.tensor_tensor_scan(b, restart, z, 0.0, ALU.mult, ALU.add))
                        dve.chain()
                        total = totals[:, slot * 8:slot * 8 + 8]
                        total_b = total.unsqueeze(2).to_broadcast([P, 8, GLA_C])
                        m = v_ts(total, bc[:, :, GLA_C - 1:GLA_C].rearrange("p c o -> p (c o)"), 1.0)
                        yield
                        dve.chain()
                        if d == 1:
                            v_tt(b, z, b, ALU.subtract)
                            dve.chain()
                            m = v_tt(bc, bc, total_b, ALU.add)
                            dve.chain()
                        v_tt(zc, total_b, bc, ALU.subtract)
                        m = dve.last()
                        act.wait(m)
                        a_act(e_last[:, slot * 8:slot * 8 + 8], total, ACT.Exp)
                        m1 = a_act(a, b, ACT.Exp)
                        act.chain()
                        m2 = a_act(b, b, ACT.Exp, scale=-1.0)
                        m3 = a_act(z, z, ACT.Exp)
                        yield
                        dve.wait(m1)
                        v_tt(qb[:, 0:TO], qT[:, h, 0:TO], a[:, 0:TO], ALU.mult)
                        dve.wait(m2)
                        v_tt(kb, kT[:, h, :], b, ALU.mult)
                        dve.wait(m3)
                        dve.chain()
                        m = v_tt(a, kT[:, h, :], z, ALU.mult)
                        scr.give(z, m)
                        scr.give(b, m)
                        yield
                        bank = psum.take(pe)
                        pe.wait(m)
                        for t in range(4):
                            ins = nc.tensor.transpose(bank[:, t * P:(t + 1) * P], a[:, t * P:(t + 1) * P], ident)
                        m = pe.done(ins)
                        scr.give(a, m)
                        act.wait(m)
                        m = a_act(kd, bank, ACT.Copy)
                        psum.give(bank, m)
                        yield

                prep = prepare(0)
                v_steps = linear_steps("gla_w_in", xn, xn_ready, T2, rows_to(vr), rows=4)
                for _ in range(KD // SLAB_K):
                    next(v_steps)
                    next(prep, None)
                    next(prep, None)
                for _ in prep:
                    fill(1)

                def r_mix_steps(n, bank, m):
                    while not scr.free:
                        yield
                    t = scr.take(act, dve)
                    m = yield from sigmoid_steps(t[:, 0:TO], bank, m)
                    yield
                    dve.wait(m)
                    m = v_tt(t[:, 0:TO], bank, t[:, 0:TO], ALU.mult)
                    yield m
                    while normed[n // 2] is None:
                        yield
                    dve.wait(m, normed[n // 2])
                    r_ready[n] = v_tt(oT[:, n, 0:TO], oT[:, n, 0:TO], t[:, 0:TO], ALU.mult)
                    scr.give(t, r_ready[n])

                r_ready, normed = [None] * KD, [None] * GLA_HEADS
                r_steps = linear_steps("gla_w_in", xn, xn_ready, TO, r_mix_steps)
                orders = ([4, 5, 6, 7, 0, 1, 2, 3], [7, 6, 5, 4, 3, 2, 1, 0])
                dve.wait(masks_in)
                masked_ring = Ring(masked)

                def o_rows(h):
                    return oT[:, 2 * h:2 * h + 2, :].rearrange("p e t -> p (e t)").rearrange("p (t v) -> p t v", v=GLA_DV)

                settle()

                def scan(h):
                    pe.wait(dve.last(), act.last())
                    state_ready, written = [None, None], {}

                    def early(step):
                        out = []
                        bank = psum.take(pe)
                        m = None
                        for d in range(2):
                            c = orders[d][step]
                            part = slice(GLA_C * (c % 2), GLA_C * (c % 2) + GLA_C)
                            qb, kb, kd = (sets[h % 2][d][:, i, :] for i in range(3))
                            tk = slice(c * GLA_C, (c + 1) * GLA_C)
                            if not (last_layer and c >= 4):
                                m = pe.done(mm(bank[part, d * GLA_C:(d + 1) * GLA_C], kb[:, tk], qb[:, tk]))
                                am = masked_ring.take(dve)
                                dve.wait(m)
                                m = v_tt(am[part, :], bank[part, d * GLA_C:(d + 1) * GLA_C],
                                         masks[part, d * GLA_C:(d + 1) * GLA_C], ALU.mult)
                                out.append((am, m))
                            else:
                                out.append(None)
                        psum.give(bank, *([m] if m else []))
                        ub = [psum.take(pe), psum.take(pe)]
                        u_done = None
                        if step < 7:
                            for d in range(2):
                                c = orders[d][step]
                                part = slice(GLA_C * (c % 2), GLA_C * (c % 2) + GLA_C)
                                kd = sets[h % 2][d][:, 2, :]
                                ins = mm(ub[d][:, 0:256], kd[part, (c // 2) * P:(c // 2 + 1) * P],
                                         vr[part, c // 2, h * GLA_DV:(h + 1) * GLA_DV])
                            u_done = pe.done(ins)
                        return out, ub, u_done

                    def late(step, out, ub, u_done):
                        o_done = [None, None]
                        for d in range(2):
                            c = orders[d][step]
                            if out[d] is None:
                                continue
                            part = slice(GLA_C * (c % 2), GLA_C * (c % 2) + GLA_C)
                            tk = slice(c * GLA_C, (c + 1) * GLA_C)
                            am, m = out[d]
                            pe.wait(m)
                            if step:
                                pe.wait(state_ready[d])
                            o = ub[d][part, GLA_DV:2 * GLA_DV]
                            if step:
                                mm(o, sets[h % 2][d][:, 0, tk], states[d], start=True, stop=False)
                            ins = mm(o, am[part, :], vr[part, c // 2, h * GLA_DV:(h + 1) * GLA_DV], start=(step == 0),
                                     stop=True)
                            m = o_done[d] = pe.done(ins)
                            masked_ring.give(am, m)
                        if step < 7:
                            for d in range(2):
                                dve.wait(u_done, *([o_done[d]] if o_done[d] else []))
                                src, c = ub[d][:, 0:256], orders[d][step]
                                slot = (h % 2) * 2 + d
                                if step == 0:
                                    state_ready[d] = v_ts(states[d], src, 1.0)
                                else:
                                    dve.wait(state_ready[d])
                                    state_ready[d] = v_stt(states[d], states[d],
                                                           e_last[:, slot * 8 + c:slot * 8 + c + 1], src,
                                                           ALU.mult, ALU.add)
                        act.wait(dve.last())
                        for d in range(2):
                            c = orders[d][step]
                            if out[d] is None:
                                continue
                            part = slice(GLA_C * (c % 2), GLA_C * (c % 2) + GLA_C)
                            src, dst = ub[d][part, GLA_DV:2 * GLA_DV], o_rows(h)[part, c // 2, :]
                            if c in written:
                                dve.wait(o_done[d], written[c])
                                written[c] = v_tt(dst, src, dst, ALU.add)
                            else:
                                act.wait(o_done[d])
                                written[c] = a_act(dst, src, ACT.Copy)
                        for bank in ub:
                            psum.give(bank, pe.last(), dve.last(), act.last())

                    held = early(0)
                    for step in range(8):
                        after = early(step + 1) if step < 7 else None
                        late(step, *held)
                        held = after
                        yield

                def norm_head(h):
                    rows, tiles_out = o_rows(h), TO // P
                    stats = small.take(act)
                    act.wait(dve.last())
                    act.chain()
                    for t in range(tiles_out):
                        junk = scr.take(act)
                        m = a_act(junk[:, 0:GLA_DV], rows[:, t, :], ACT.Square, accum=stats[:, t:t + 1])
                        scr.give(junk, m)
                    yield
                    act.wait(m)
                    m = a_act(stats[:, 4:4 + tiles_out], stats[:, 0:tiles_out], ACT.Ln, bias=eps, scale=1.0 / GLA_DV)
                    act.wait(m)
                    m = a_act(stats[:, 4:4 + tiles_out], stats[:, 4:4 + tiles_out], ACT.Exp, scale=-0.5)
                    yield
                    dve.wait(m)
                    for t in range(tiles_out):
                        m = v_ts(rows[:, t, :], rows[:, t, :], stats[:, 4 + t:5 + t])
                    small.give(stats, m)
                    yield
                    turned = [psum.take(pe) for _ in range(2)]
                    pe.wait(m)
                    for e, bank in enumerate(turned):
                        for t in range(tiles_out):
                            ins = nc.tensor.transpose(bank[:, t * P:(t + 1) * P], rows[:, t, e * P:(e + 1) * P], ident)
                    m = pe.done(ins)
                    act.wait(m)
                    for e, bank in enumerate(turned):
                        m = a_act(oT[:, 2 * h + e, 0:TO], bank[:, 0:TO], ACT.Copy, scale=vec("gla_g_head", g * 2 + e))
                        psum.give(bank, m)
                    normed[h] = m
                    yield

                R_AT = [(1, 5), (1, 7), (2, 1), (2, 5), (3, 1), (3, 3), (3, 5)]
                for h in range(GLA_HEADS):
                    prep = prepare(h + 1) if h < GLA_HEADS - 1 else iter(())
                    norm = norm_head(h - 1) if h else iter(())
                    for step, _ in enumerate(scan(h)):
                        next(norm, None)
                        next(prep, None)
                        if step in (1,4):
                            next(prep, None)
                        if h == 0 and step % 2:
                            next(v_steps)
                        elif (h, step) in R_AT:
                            next(r_steps)
                        later.step()
                    next(v_steps, None)
                    for _ in prep:
                        fill(1)
                for _ in norm_head(GLA_HEADS - 1):
                    fill(1)
                inner.close()
                mixed = halves(st, name + "mixed", KD, T2)
                for _ in r_steps:
                    pass
                fence()
                m_ready = [None] * KD

                def cut_mixed(k):
                    m_ready[k] = yield from cut_steps(mixed[0][:, k, 0:TO], mixed[1][:, k, 0:TO], oT[:, k, 0:TO],
                                                      r_ready[k])
                for k in range(KD):
                    later.add(cut_mixed(k))
                fill(3)
                linear("gla_w_out", mixed, m_ready, TO, add_to_x(sums, gate_of(layer, 2)))
            elif layer % 3 == 1:
                u = tile(st, "u_pad", KD * 2 * PADDED).rearrange("p (k s t) -> p k s t", k=KD, s=2)
                y = tiles(st, "y", KD, T2)
                yh = halves(st, "yh", KD, T2)
                fence()
                for k in range(KD):
                    dve.done(nc.vector.memset(u[:, k, :, 0:CONV_PAD], 0.0))
                    dve.done(nc.vector.memset(u[:, k, :, CONV_PAD + S:PADDED], 0.0))
                u_ready = [None] * KD
                y_ready = [None] * KD

                def depthwise_vector(chunks):
                    for j in range(CONV_W):
                        for n in chunks:
                            out = y[:, n, :].rearrange("p (s t) -> p s t", s=2)
                            if j == 0:
                                dve.wait(u_ready[n])
                                y_ready[n] = v_ts(out, u[:, n, :, 0:S], vec("w_dw", n), vec("b_dw", n), ALU.mult,
                                                  ALU.add)
                            else:
                                dve.wait(y_ready[n])
                                y_ready[n] = v_stt(out, u[:, n, :, j:j + S], vec("w_dw", j * KD + n), out,
                                                   ALU.mult, ALU.add)
                        if j % 3 == 2:
                            yield

                def depthwise_tensor(chunks):
                    GROUP = 4
                    for n in chunks:
                        bank = psum.take(pe)
                        pe.wait(u_ready[n])
                        for j0 in range(0, CONV_W, GROUP):
                            taps = range(j0, min(j0 + GROUP, CONV_W))
                            diag = scr.take(act)
                            for j in taps:
                                m = a_act(diag[:, (j - j0) * P:(j - j0 + 1) * P], ident, ACT.Copy,
                                          scale=vec("w_dw", j * KD + n))
                            pe.wait(m)
                            for j in taps:
                                ins = mm(bank.rearrange("p (s t) -> p s t", s=2),
                                         diag[:, (j - j0) * P:(j - j0 + 1) * P], u[:, n, :, j:j + S],
                                         start=(j == 0), stop=(j == CONV_W - 1))
                            m = pe.done(ins)
                            scr.give(diag, m)
                            yield
                        act.wait(m)
                        y_ready[n] = a_act(y[:, n, :], bank, ACT.Identity, bias=vec("b_dw", n))
                        psum.give(bank, y_ready[n])

                def glu_steps(n, bank, m):
                    while not scr.free:
                        yield
                    t = scr.take(act, dve)
                    act.wait(m)
                    m = a_act(t, bank, ACT.Identity, bias=vec("b_pw1", KD + n))
                    yield m
                    m = yield from sigmoid_steps(t, t, m)
                    yield
                    dve.wait(m)
                    ua = u[:, n, :, CONV_PAD:CONV_PAD + S]
                    u_ready[n] = v_tt(ua, ua, t.rearrange("p (s t) -> p s t", s=2), ALU.mult)
                    scr.give(t, u_ready[n])

                taps = iter(())
                for n0 in range(0, KD, 4):
                    def evac_a(n, bank, m, n0=n0):
                        act.wait(m)
                        return a_act(u[:, n0 + n, :, CONV_PAD:CONV_PAD + S], bank.rearrange("p (s t) -> p s t", s=2),
                                     ACT.Identity, bias=vec("b_pw1", n0 + n))

                    def evac_gt(n, bank, m, n0=n0):
                        return glu_steps(n0 + n, bank, m)
                    linear("conv_w_pw1", xn, xn_ready, T2, evac_a, side=taps)
                    linear("conv_w_pw1", xn, xn_ready, T2, evac_gt, side=taps)
                    later.drain()
                    if n0 == 0:
                        taps = depthwise_vector((0, 1))
                on_tensor = depthwise_tensor((5, 6, 7))
                for rest in (taps, depthwise_vector((2, 3)), depthwise_vector((4,))):
                    for _ in rest:
                        next(on_tensor, None)
                for _ in on_tensor:
                    pass
                bank = psum.take(pe)
                order = (0, 1, 5, 2, 3, 6, 7, 4)
                for i, k in enumerate(order):
                    pe.wait(y_ready[k])
                    ins = mm(bank, ones, y[:, k, :], start=(i == 0), stop=(i == KD - 1))
                m = pe.done(ins)
                mean = scr.take(act)
                act.wait(m)
                m = a_act(mean, bank, ACT.Copy, scale=1.0 / D)
                psum.give(bank, m)
                fill(1)
                dve.wait(m)
                squares = SumSquares(T2)
                for k in range(KD):
                    m = v_tt(y[:, k, :], y[:, k, :], mean, ALU.subtract)
                    if k == KD - 1:
                        scr.give(mean, m)
                    later.add(squares.steps(y[:, k, :], m))
                    later.step()
                    if k % 2:
                        fill(1)
                r, normed = squares.inv_rms(1.0 / D)
                fill(2)

                def scale_silu(k):
                    yk = y[:, k, :]
                    dve.wait(normed)
                    m = v_tt(yk, yk, r, ALU.mult)
                    yield
                    act.wait(m)
                    m = a_act(yk, yk, ACT.Identity, bias=vec("ln_b", k), scale=vec("ln_g", k))
                    yield
                    m = yield from silu_steps(yk, yk, m, T2)
                    yield
                    y_ready[k] = yield from cut_steps(yh[0][:, k, :], yh[1][:, k, :], yk, m)
                for k in range(KD):
                    y_ready[k] = None
                for k in range(KD):
                    later.add(scale_silu(k))
                    later.step()
                    if k % 2:
                        fill(1)
                later.drain()
                scr.give(r, dve.last())
                linear("conv_w_pw2", yh, y_ready, T2, add_to_x(sums, gate_of(layer, 2), lambda n: vec("b_pw2", n)))
            else:
                KC = KV_HEADS * HD // P
                qT, kT = tiles(st, "gq", KD, T2), tiles(st, "gk", KC, T2)
                vr = tiles(st, "gv", 4, KV_HEADS * HD)
                oT = halves(st, "go", KD, T2)
                rot = tile(st, "rot", 2 * S)
                fence()
                at, _ = CON["cos"]
                rot_in = stage_load(rot, io["con"][:, at:at + 2 * S], 14)
                cos, sin = rot[:, 0:S], rot[:, S:2 * S]
                raw_ready = []
                rotated = []

                def norm_and_rotate():
                    n = 0
                    while n < KD + KC:
                        if n >= len(raw_ready):
                            yield
                            continue
                        t_ = qT[:, n, :] if n < KD else kT[:, n - KD, :]
                        squares = SumSquares(T2)
                        squares.add(t_, raw_ready[n])
                        yield
                        r, m = squares.inv_rms(1.0 / HD, con("head_ones"))
                        dve.wait(m, rot_in)
                        m = v_stt(t_, t_, vec("g_q") if n < KD else vec("g_k"), r, ALU.mult, ALU.mult)
                        yield
                        bank = psum.take(pe)
                        pe.wait(m)
                        m2 = pe.done(mm(bank[:, 0:S], con("rope_swap"), t_[:, 0:S]))
                        dve.wait(m2)
                        m = v_tt(r[:, 0:S], bank[:, 0:S], sin, ALU.mult)
                        psum.give(bank, m)
                        v_tt(t_[:, 0:S], t_[:, 0:S], cos, ALU.mult)
                        dve.chain()
                        m = v_tt(t_[:, 0:S], t_[:, 0:S], r[:, 0:S], ALU.add)
                        scr.give(r, m)
                        rotated.append(m)
                        n += 1
                rotate = norm_and_rotate()
                linear("attn_w_qkv", xn, xn_ready, T2, copy_to(lambda n: qT[:, n, :], raw_ready), side=rotate)
                linear("attn_w_qkv", xn, xn_ready, T2, copy_to(lambda n: kT[:, n, :], raw_ready), side=rotate)
                linear("attn_w_qkv", xn, xn_ready, T2, rows_to(vr), rows=4, side=rotate)
                v_ready = act.last()
                for _ in rotate:
                    fill(1)
                units = []
                for h in range(Q_HEADS):
                    part = slice(HD * (h % 2), HD * (h % 2) + HD)
                    kv = HEAD_ORDER[h] // (Q_HEADS // KV_HEADS)
                    for qt in range(4):
                        tok = slice(qt * P, (qt + 1) * P)
                        lat = qt < 2
                        first_tile = 0 if lat else 2
                        units.append(dict(nk=T2 if lat else S, causal=False, ready=[rotated[-1], v_ready],
                                          pairs=[(qT[part, h // 2, tok], kT[part, kv // 2, first_tile * P:T2])],
                                          outs=[(part, (lambda t, kv=kv, f=first_tile:
                                                        vr[:, f + t, kv * HD:(kv + 1) * HD]),
                                                 [half[part, h // 2, tok] for half in oT], 0)]))
                attended = Attention(units, HD ** -0.5).run(every=2)
                linear("attn_w_out", oT, [attended] * KD, T2, add_to_x(sums, gate_of(layer, 2)))
            st.close()

            xn_ready = modulated(sums, layer, "g_norm_mlp", 3, 4, TO)
            sums = None if last_layer else SumSquares(T2)
            HC = FC2 // 2
            feed = ExitStack()
            wide = None
            if layer in WIDE_AT:
                wide = wide_modulation(WIDE_AT[layer], [tile(feed, f"wide_w{layer}{i}", WIDE) for i in range(2)],
                                       [tile(feed, f"wide_acc{layer}{i}", WIDE) for i in range(2)])
            for half in range(2):
                st = ExitStack()
                hid = halves(st, f"mlp{layer}{half}", HC, T2)
                fence()
                hid_ready = [None] * HC

                def relu_steps(n, bank, m):
                    while not scr.free:
                        yield
                    t = scr.take(act)
                    act.wait(m)
                    m = a_act(t[:, 0:TO], bank, ACT.Relu)
                    yield m
                    dve.wait(m)
                    m = v_tt(t[:, 0:TO], t[:, 0:TO], t[:, 0:TO], ALU.mult)
                    yield
                    hid_ready[n] = yield from cut_steps(hid[0][:, n, 0:TO], hid[1][:, n, 0:TO], t[:, 0:TO], m)
                    scr.give(t, hid_ready[n])
                linear("w_mlp_in", xn, xn_ready, TO, relu_steps, side=wide)
                linear("w_mlp_out", hid, hid_ready, TO,
                       add_to_x(sums if half else None, gate_of(layer, 5)), side=wide)
                st.close()
            for _ in wide or ():
                pass
            feed.close()

        sp.wait(dve.last())
        out_mark = dma(io["out"], x[:, :, 0:S], out_sem)
        sp.wait(out_mark)
        assert stream.loaded == len(plan) and bg_done[0] == len(bg_steps) and not bg_tail


WEIGHTS = [("ev_w_in", "ev_w_in", 0), ("ev_w_out", "ev_w_out", 0), ("od_w_in", "od_w_in", 0),
           ("od_w_out", "od_w_out", 0), ("xattn_wq", "xattn_wq", None), ("xattn_wkv", "xattn_wkv", None),
           ("xattn_wo", "xattn_wo", None), ("ffn_w_up", "ffn_w_up", None), ("ffn_w_down", "ffn_w_down", None),
           ("w_mlp_in", "w_mlp_in_2", None), ("w_mlp_out", "w_mlp_out_2", None),
           ("gla_w_in", "gla_w_in_2", None), ("gla_w_out", "gla_w_out_2", None), ("conv_w_pw1", "conv_w_pw1_2", 0),
           ("conv_w_pw2", "conv_w_pw2_2", 0), ("w_mod", "w_mod_2", None)]


def kernel(**inputs):
    import concourse.bacc as _bacc
    from concourse.bass_utils import run_bass_kernel_spmd as _run

    a = {k: np.asarray(v) for k, v in inputs.items()}

    def cols(v):
        return np.ascontiguousarray(v.reshape(-1, P).T)

    def tokens(t):
        return np.ascontiguousarray(t[0].T.reshape(KD, P, -1).transpose(1, 0, 2))

    vec = np.zeros((P, NVEC), np.float32)

    def put(name, value):
        at, n = VEC[name]
        vec[:, at:at + n] = value
    for name in ("mem_norm", "norm_mix", "norm_xattn", "norm_ffn", "pool_scale", "final_norm", "dn_conv", "dn_norm_g",
                 "ffn_conv"):
        put(name, cols(a[name]))
    for name, src in (("g_norm_mix", "g_norm_mix_2"), ("g_norm_mlp", "g_norm_mlp_2"), ("b_mod", "b_mod_2"),
                      ("gla_b_g", "gla_b_g_2"), ("gla_g_head", "gla_g_head_2"), ("b_pw1", "conv_b_pw1_2"),
                      ("w_dw", "conv_w_dw_2"), ("b_dw", "conv_b_dw_2"), ("ln_g", "conv_ln_g_2"),
                      ("ln_b", "conv_ln_b_2"), ("b_pw2", "conv_b_pw2_2")):
        put(name, cols(a[src]))
    put("g_q", np.concatenate([a["attn_g_q_2"][0]] * 2)[:, None])
    put("g_k", np.concatenate([a["attn_g_k_2"][0]] * 2)[:, None])
    put("c", np.stack([cols(a["c_2"]), cols(a["c_ctx_2"])], axis=2).reshape(P, 2 * KD))
    put("a_log", a["dn_a_log"].ravel())
    put("dt_bias", a["dn_dt_bias"].ravel())
    row = np.broadcast_to(np.concatenate([a["sgu_ln_g"].ravel(), a["sgu_ln_b"].ravel(), a["sgu_b"].ravel()]), (P, NROW))

    g1 = np.zeros((2, D, P), np.float32)
    g2 = np.zeros((2, 32 + GLA_RANK, 512), np.float32)
    for d in range(2):
        g1[:, :, 32 * d:32 * d + GLA_RANK] = a["gla_w_g1_2"][:, d]
        g2[:, 32 * d:32 * d + GLA_RANK] = a["gla_w_g2_2"][:, d]
    by_head = np.concatenate([np.arange(HD * h, HD * (h + 1)) for h in HEAD_ORDER])
    qkv = a["attn_w_qkv_2"][0]
    qkv = np.concatenate([qkv[:, by_head], qkv[:, D:]], axis=1)
    arrays = {
        "attn_w_qkv": qkv, "attn_w_out": a["attn_w_out_2"][0][by_head],
        "con": shape_constants(), "vec": vec, "row": np.ascontiguousarray(row),
        "xT": tokens(a["x"]), "memT": tokens(a["mem"]), "ctxT": tokens(a["ctx_2"]),
        "pool_w": np.ascontiguousarray(a["pool_w"][0].transpose(1, 0, 2)),
        "sgu_wT": np.ascontiguousarray(a["sgu_w"][0].transpose(2, 0, 1)),
        "gla_w_g1": g1,
        "gla_w_g2": g2,
    }
    for name, src, index in WEIGHTS:
        arrays[name] = np.ascontiguousarray(a[src] if index is None else a[src][index])
    nc = _bacc.Bacc("TRN2", target_bir_lowering=False, num_devices=1)
    io = {name: nc.dram_tensor(f"in_{name}", v.shape, F32, kind="ExternalInput").ap() for name, v in arrays.items()}
    io["out"] = nc.dram_tensor("out_xT", (P, KD, S), F32, kind="ExternalOutput").ap()
    build(nc, io)
    r = _run(nc, [{f"in_{name}": v for name, v in arrays.items()}], core_ids=[0])
    out = r.results[0]["out_xT"]
    return np.ascontiguousarray(out.transpose(1, 0, 2).reshape(D, S).T)[None]
```
